# Optimizing a Trainium2 kernel written in Bass

```python
import math
import jax, jax.numpy as jnp
from jax import lax
import numpy as np
import jax
import jax.numpy as jnp

D_MODEL = 1024
BATCH = 1
SEQ = 256
DEPTH = 1

MIX_WIDTH = D_MODEL
POOL_WIDTH = MIX_WIDTH // 2
POOL_WINDOWS = (2, 4, 8, 16)
N_POOL_GROUPS = len(POOL_WINDOWS)
POOL_GROUP_DIM = POOL_WIDTH // N_POOL_GROUPS
ATTN_WIDTH = MIX_WIDTH - POOL_WIDTH
HEAD_DIM = 64
N_ATTN_HEADS = ATTN_WIDTH // HEAD_DIM
DILATED_BRANCHES = ((128, 1), (512, 4), (2048, 16))
ATTN_BLOCK = 128
IN_WIDTH = POOL_WIDTH + 3 * ATTN_WIDTH
N_REL_BUCKETS = 32
REL_MAX_EXACT = N_REL_BUCKETS // 2
REL_MAX_DISTANCE = 2048
N_EXPERTS = 32
TOP_K = 4
D_EXPERT = D_MODEL
SWIGLU_LIMIT = 7.0
SWIGLU_ALPHA = 1.702
MOE_BLOCK = 128
PLE_DIM = 256
NORM_EPS = 1e-6
NEG_INF = -1e30


def rmsnorm(x, g):
    xf = x.astype(jnp.float32)
    y = xf * lax.rsqrt(jnp.mean(xf * xf, axis=-1, keepdims=True) + NORM_EPS)
    return (y * g.astype(jnp.float32)).astype(x.dtype)

def pool_mixer(u, w_pool, pool_scale):
    B, S, _ = u.shape
    ug = u.reshape(B, S, N_POOL_GROUPS, POOL_GROUP_DIM)
    t = jnp.arange(S)
    outs = []
    for gi, w in enumerate(POOL_WINDOWS):
        ch = ug[:, :, gi].astype(jnp.float32)
        cs = jnp.cumsum(ch, axis=1)
        prev = jnp.pad(cs, ((0, 0), (w, 0), (0, 0)))[:, :S]
        cnt = jnp.minimum(t + 1, w).astype(jnp.float32)[None, :, None]
        outs.append(((cs - prev) / cnt - ch).astype(u.dtype))
    pooled = jnp.stack(outs, axis=2)
    mixed = jnp.einsum('bsgc,gcd->bsgd', pooled, w_pool)
    return mixed.reshape(B, S, POOL_WIDTH) * pool_scale

def t5_bucket(dist):
    n = jnp.maximum(dist, 1).astype(jnp.float32)
    large = REL_MAX_EXACT + (jnp.log(n / REL_MAX_EXACT) / math.log(REL_MAX_DISTANCE / REL_MAX_EXACT)
                             * (N_REL_BUCKETS - REL_MAX_EXACT)).astype(jnp.int32)
    large = jnp.minimum(large, N_REL_BUCKETS - 1)
    return jnp.where(dist < REL_MAX_EXACT, dist, large)

def dilated_branch(q, k, v, rel_bias, window, dil):
    B, S, H, Dh = q.shape
    w_sub = window // dil
    blk = ATTN_BLOCK
    span = dil * blk
    Sp = -(-S // span) * span
    L = Sp // dil
    nb = L // blk

    def to_sub(t):
        t = jnp.pad(t, ((0, 0), (0, Sp - S), (0, 0), (0, 0)))
        t = t.reshape(B, nb, blk, dil, H, Dh)
        return t.transpose(0, 3, 4, 1, 2, 5)

    qs, ks, vs = to_sub(q), to_sub(k), to_sub(v)
    shift = lambda t: jnp.concatenate([jnp.zeros_like(t[:, :, :, :1]), t[:, :, :, :-1]], axis=3)
    keys = jnp.concatenate([shift(ks), ks], axis=4)
    vals = jnp.concatenate([shift(vs), vs], axis=4)

    s = jnp.einsum('brhnqc,brhnkc->brhnqk', qs, keys).astype(jnp.float32) * (1.0 / math.sqrt(Dh))
    qi = jnp.arange(blk)[:, None]
    ki = jnp.arange(2 * blk)[None, :]
    rel = blk + qi - ki
    bias = rel_bias[t5_bucket(jnp.maximum(rel, 0) * dil)]
    s = s + bias.transpose(2, 0, 1)[:, None].astype(jnp.float32)
    band = (rel >= 0) & (rel <= w_sub)
    first_ok = (jnp.arange(nb)[:, None, None] > 0) | (ki[None] >= blk)
    mask = band[None] & first_ok
    s = jnp.where(mask, s, NEG_INF)
    m = jnp.max(s, axis=-1)
    e = jnp.exp(s - m[..., None])
    l = jnp.sum(e, axis=-1)
    o = jnp.einsum('brhnqk,brhnkc->brhnqc', e, vals.astype(jnp.float32)) / l[..., None]
    lse = m + jnp.log(l)
    o = o.transpose(0, 3, 4, 1, 2, 5).reshape(B, Sp, H, Dh)[:, :S]
    lse = lse.transpose(0, 3, 4, 1, 2).reshape(B, Sp, H)[:, :S]
    return o, lse

def dilated_attention(q, k, v, rel_bias):
    outs, lses = [], []
    for window, dil in DILATED_BRANCHES:
        o, lse = dilated_branch(q, k, v, rel_bias, window, dil)
        outs.append(o)
        lses.append(lse)
    w = jax.nn.softmax(jnp.stack(lses, axis=0), axis=0)
    out = jnp.sum(w[..., None] * jnp.stack(outs, axis=0), axis=0)
    return out.astype(q.dtype)

def moe(h, w_router, b_router, w_gate_up, b_gate_up, w_down, b_down):
    B, S, D = h.shape
    T = B * S
    hf = h.reshape(T, D)
    logits = (hf @ w_router + b_router).astype(jnp.float32)
    topv, topi = lax.top_k(logits, TOP_K)
    gates = jax.nn.softmax(topv, axis=-1)

    expert_ids = topi.reshape(-1)
    token_ids = jnp.repeat(jnp.arange(T), TOP_K)
    gate_flat = gates.reshape(-1)
    order = jnp.argsort(expert_ids)
    sorted_e = expert_ids[order]
    group_sizes = jnp.bincount(expert_ids, length=N_EXPERTS)
    group_starts = jnp.cumsum(group_sizes) - group_sizes
    padded_sizes = (group_sizes + MOE_BLOCK - 1) // MOE_BLOCK * MOE_BLOCK
    padded_ends = jnp.cumsum(padded_sizes)
    padded_starts = padded_ends - padded_sizes
    rank = jnp.arange(T * TOP_K) - group_starts[sorted_e]
    dest = padded_starts[sorted_e] + rank

    n_rows = T * TOP_K + N_EXPERTS * MOE_BLOCK
    n_blocks = n_rows // MOE_BLOCK
    row_token = jnp.zeros((n_rows,), jnp.int32).at[dest].set(token_ids[order])
    row_gate = jnp.zeros((n_rows,), h.dtype).at[dest].set(gate_flat[order].astype(h.dtype))
    block_expert = jnp.minimum(
        jnp.searchsorted(padded_ends, jnp.arange(n_blocks) * MOE_BLOCK, side='right'),
        N_EXPERTS - 1)
    xs = hf[row_token].reshape(n_blocks, MOE_BLOCK, D)

    def expert_block(args):
        xb, e = args
        gu = xb @ w_gate_up[e] + b_gate_up[e]
        g, u = gu[:, :D_EXPERT], gu[:, D_EXPERT:]
        g = jnp.minimum(g, SWIGLU_LIMIT)
        u = jnp.clip(u, -SWIGLU_LIMIT, SWIGLU_LIMIT)
        glu = g * jax.nn.sigmoid(SWIGLU_ALPHA * g)
        return ((u + 1.0) * glu) @ w_down[e] + b_down[e]

    ys = lax.map(expert_block, (xs, block_expert)).reshape(n_rows, D)
    out = jnp.zeros((T, D), h.dtype).at[row_token].add(ys * row_gate[:, None])
    return out.reshape(B, S, D)

def first_inputs(seed: int = 0) -> dict:
    key = jax.random.key(seed)
    ks = jax.random.split(key, 24)
    f32 = jnp.float32
    nrm = lambda k, shape, s: jax.random.normal(k, shape, f32) * s
    gain = lambda k, shape: 1.0 + 0.05 * jax.random.normal(k, shape, f32)
    return {
        "x": nrm(ks[0], (BATCH, SEQ, D_MODEL), 1.0),
        "p": nrm(ks[1], (DEPTH, BATCH, SEQ, PLE_DIM), 1.0),
        "g_mix": gain(ks[2], (DEPTH, D_MODEL)),
        "w_in": nrm(ks[3], (DEPTH, D_MODEL, IN_WIDTH), D_MODEL ** -0.5),
        "w_pool": nrm(ks[4], (DEPTH, N_POOL_GROUPS, POOL_GROUP_DIM, POOL_GROUP_DIM), POOL_GROUP_DIM ** -0.5),
        "pool_scale": gain(ks[5], (DEPTH, POOL_WIDTH)),
        "rel_bias": nrm(ks[6], (N_REL_BUCKETS, N_ATTN_HEADS), 0.5),
        "w_out": nrm(ks[7], (DEPTH, MIX_WIDTH, D_MODEL), MIX_WIDTH ** -0.5),
        "g_ffn": gain(ks[8], (DEPTH, D_MODEL)),
        "w_router": nrm(ks[9], (DEPTH, D_MODEL, N_EXPERTS), D_MODEL ** -0.5),
        "b_router": nrm(ks[10], (DEPTH, N_EXPERTS), 0.01),
        "w_gate_up": nrm(ks[11], (DEPTH, N_EXPERTS, D_MODEL, 2 * D_EXPERT), D_MODEL ** -0.5),
        "b_gate_up": nrm(ks[12], (DEPTH, N_EXPERTS, 2 * D_EXPERT), 0.01),
        "w_down": nrm(ks[13], (DEPTH, N_EXPERTS, D_EXPERT, D_MODEL), D_EXPERT ** -0.5),
        "b_down": nrm(ks[14], (DEPTH, N_EXPERTS, D_MODEL), 0.01),
        "g_ple": gain(ks[15], (DEPTH, D_MODEL)),
        "w_ple_gate": nrm(ks[16], (DEPTH, D_MODEL, D_MODEL), D_MODEL ** -0.5),
        "w_ple_proj": nrm(ks[17], (DEPTH, PLE_DIM, D_MODEL), PLE_DIM ** -0.5),
        "g_final": gain(ks[18], (D_MODEL,)),
    }

def first_block(x, p, g_mix, w_in, w_pool, pool_scale, rel_bias, w_out, g_ffn,
              w_router, b_router, w_gate_up, b_gate_up, w_down, b_down,
              g_ple, w_ple_gate, w_ple_proj, g_final):
    B, S, _ = x.shape
    for i in range(DEPTH):
        h = rmsnorm(x, g_mix[i])
        z = jnp.einsum('bsd,de->bse', h, w_in[i])
        u = z[..., :POOL_WIDTH]
        qkv = z[..., POOL_WIDTH:].reshape(B, S, 3, N_ATTN_HEADS, HEAD_DIM)
        q, k, v = qkv[:, :, 0], qkv[:, :, 1], qkv[:, :, 2]
        a_out = pool_mixer(u, w_pool[i], pool_scale[i])
        b_out = dilated_attention(q, k, v, rel_bias).reshape(B, S, ATTN_WIDTH)
        mix = jnp.concatenate([a_out, b_out], axis=-1)
        x = x + jnp.einsum('bse,ed->bsd', mix, w_out[i])
        x = x + moe(rmsnorm(x, g_ffn[i]), w_router[i], b_router[i], w_gate_up[i],
                    b_gate_up[i], w_down[i], b_down[i])
        gate = jax.nn.sigmoid(jnp.einsum('bsd,de->bse', rmsnorm(x, g_ple[i]), w_ple_gate[i]))
        x = x + jnp.einsum('bsp,pd->bsd', p[i], w_ple_proj[i]) * gate
    return rmsnorm(x, g_final)


DEPTH_2 = 2

EPS = 1e-6
ROPE_THETA = 10000.0
NEG_INF_2 = -1e30
D_FF = 2816
N_BRANCH = 3
MIX_WIDTH_2 = 512

MLA_HEADS = 8
MLA_Q_RANK = 256
MLA_KV_RANK = 128
MLA_NOPE = 64
MLA_ROPE = 32
MLA_V = 64
MLA_QK = MLA_NOPE + MLA_ROPE
ATTN_BLOCK_Q = 128

GDN_HEADS = 4
GDN_DK = 128
GDN_DV = 128
GDN_CONV = 4
GDN_CHUNK = 64

MOBA_HEADS = 8
MOBA_DH = 64
MOBA_BLOCK = 256
MOBA_TOPK = 3
MOBA_QCHUNK = 64

IN_SPLITS = (
    MLA_Q_RANK,
    MLA_KV_RANK,
    MLA_ROPE,
    GDN_HEADS * GDN_DK,
    GDN_HEADS * GDN_DK,
    GDN_HEADS * GDN_DV,
    GDN_HEADS,
    GDN_HEADS,
    GDN_HEADS * GDN_DV,
    3 * MOBA_HEADS * MOBA_DH,
    N_BRANCH * D_MODEL,
)
D_IN = sum(IN_SPLITS)


def split_cols(t, sizes):
    offs = np.cumsum(sizes)[:-1].tolist()
    return jnp.split(t, offs, axis=-1)

def rms_norm(x, g):
    xf = x.astype(jnp.float32)
    y = xf * lax.rsqrt(jnp.mean(xf * xf, axis=-1, keepdims=True) + EPS)
    return (y * g.astype(jnp.float32)).astype(x.dtype)

def l2norm(x):
    return x * lax.rsqrt(jnp.sum(x * x, axis=-1, keepdims=True) + EPS)

def rope(x, pos):
    d = x.shape[-1]
    half = d // 2
    inv_freq = ROPE_THETA ** (-jnp.arange(half, dtype=jnp.float32) * 2.0 / d)
    ang = pos.astype(jnp.float32)[:, None] * inv_freq[None, :]
    cos = jnp.cos(ang)[None, :, None, :]
    sin = jnp.sin(ang)[None, :, None, :]
    xf = x.astype(jnp.float32)
    x1, x2 = xf[..., :half], xf[..., half:]
    return jnp.concatenate([x1 * cos - x2 * sin, x2 * cos + x1 * sin], axis=-1).astype(x.dtype)

def swiglu(h, w_in, w_out):
    gate, up = jnp.split(h @ w_in, 2, axis=-1)
    return (jax.nn.silu(gate) * up) @ w_out

def causal_dwconv(x, w):
    c = x.shape[-1]
    k = w.shape[0]
    return lax.conv_general_dilated(
        x, w[:, None, :].astype(x.dtype), window_strides=(1,), padding=[(k - 1, 0)],
        dimension_numbers=('NWC', 'WIO', 'NWC'), feature_group_count=c)

def causal_attention_blocked(q, k, v, scale):
    b, h, s, dk = q.shape
    nb = s // ATTN_BLOCK_Q
    qb = jnp.moveaxis(q.reshape(b, h, nb, ATTN_BLOCK_Q, dk), 2, 0)
    k_pos = jnp.arange(s)

    def one_block(args):
        i, q_i = args
        logits = jnp.einsum('bhqd,bhkd->bhqk', q_i, k, preferred_element_type=jnp.float32) * scale
        q_pos = i * ATTN_BLOCK_Q + jnp.arange(ATTN_BLOCK_Q)
        logits = jnp.where(k_pos[None, :] <= q_pos[:, None], logits, NEG_INF_2)
        p = jax.nn.softmax(logits, axis=-1).astype(v.dtype)
        return jnp.einsum('bhqk,bhkd->bhqd', p, v)

    o = lax.map(one_block, (jnp.arange(nb), qb))
    return jnp.moveaxis(o, 0, 2).reshape(b, h, s, v.shape[-1])

def mla_branch(c_q, c_kv, k_rope, pos, cq_norm, ckv_norm, w_uq, w_ukv, q_norm, k_norm):
    b, s, _ = c_q.shape
    h = MLA_HEADS
    q = (rms_norm(c_q, cq_norm) @ w_uq).reshape(b, s, h, MLA_QK)
    kv = (rms_norm(c_kv, ckv_norm) @ w_ukv).reshape(b, s, h, MLA_NOPE + MLA_V)
    k_nope, v = kv[..., :MLA_NOPE], kv[..., MLA_NOPE:]
    k = jnp.concatenate([k_nope, jnp.broadcast_to(k_rope[:, :, None, :], (b, s, h, MLA_ROPE))], axis=-1)
    q = rms_norm(q, q_norm)
    k = rms_norm(k, k_norm)
    q = jnp.concatenate([q[..., :MLA_NOPE], rope(q[..., MLA_NOPE:], pos)], axis=-1)
    k = jnp.concatenate([k[..., :MLA_NOPE], rope(k[..., MLA_NOPE:], pos)], axis=-1)
    to_bhsd = lambda t: jnp.transpose(t, (0, 2, 1, 3))
    o = causal_attention_blocked(to_bhsd(q), to_bhsd(k), to_bhsd(v), MLA_QK ** -0.5)
    return jnp.transpose(o, (0, 2, 1, 3)).reshape(b, s, h * MLA_V)

def gated_delta_rule_chunked(q, k, v, beta, g):
    b, s, h, dk = q.shape
    dv = v.shape[-1]
    c = GDN_CHUNK
    n = s // c

    def chunks(t):
        return jnp.moveaxis(t.reshape((b, n, c, h) + t.shape[3:]), 3, 1)

    q, k, v, beta, g = (chunks(t) for t in (q, k, v, beta, g))
    gcum = jnp.cumsum(g, axis=-1)
    tril = jnp.tril(jnp.ones((c, c), dtype=bool))
    strict = jnp.tril(jnp.ones((c, c), dtype=bool), -1)
    decay = jnp.exp(jnp.where(tril, gcum[..., :, None] - gcum[..., None, :], NEG_INF_2))
    k_beta = k * beta[..., None]
    a = jnp.where(strict, jnp.einsum('bhnid,bhnjd->bhnij', k_beta, k) * decay, 0.0)
    eye = jnp.eye(c, dtype=q.dtype)
    rhs = jnp.concatenate([v * beta[..., None], k_beta * jnp.exp(gcum)[..., None]], axis=-1)
    sol = lax.linalg.triangular_solve(eye + a, rhs, left_side=True, lower=True, unit_diagonal=True)
    u, w = sol[..., :dv], sol[..., dv:]
    qk = jnp.einsum('bhnid,bhnjd->bhnij', q, k) * decay
    q_dec = q * jnp.exp(gcum)[..., None]
    g_last = gcum[..., -1]
    k_dec = k * jnp.exp(g_last[..., None] - gcum)[..., None]

    def step(state, xs):
        q_i, w_i, u_i, qk_i, k_i, gl_i = xs
        v_new = u_i - jnp.einsum('bhcd,bhde->bhce', w_i, state)
        o_i = jnp.einsum('bhcd,bhde->bhce', q_i, state) + jnp.einsum('bhcj,bhje->bhce', qk_i, v_new)
        state = state * jnp.exp(gl_i)[..., None, None] + jnp.einsum('bhcd,bhce->bhde', k_i, v_new)
        return state, o_i

    xs = tuple(jnp.moveaxis(t, 2, 0) for t in (q_dec, w, u, qk, k_dec, g_last))
    state0 = jnp.zeros((b, h, dk, dv), q.dtype)
    _, o = lax.scan(step, state0, xs)
    return jnp.transpose(o, (1, 0, 3, 2, 4)).reshape(b, s, h, dv)

def gdn_branch(q, k, v, b_logit, a_logit, z, conv_w, a_log, dt_bias, out_norm):
    b, s, _ = q.shape
    f32 = jnp.float32
    qkv = jax.nn.silu(causal_dwconv(jnp.concatenate([q, k, v], axis=-1), conv_w)).astype(f32)
    q, k, v = jnp.split(qkv, [GDN_HEADS * GDN_DK, 2 * GDN_HEADS * GDN_DK], axis=-1)
    q = l2norm(q.reshape(b, s, GDN_HEADS, GDN_DK)) * (GDN_DK ** -0.5)
    k = l2norm(k.reshape(b, s, GDN_HEADS, GDN_DK))
    v = v.reshape(b, s, GDN_HEADS, GDN_DV)
    beta = jax.nn.sigmoid(b_logit.astype(f32))
    g = -jnp.exp(a_log.astype(f32)) * jax.nn.softplus(a_logit.astype(f32) + dt_bias.astype(f32))
    o = gated_delta_rule_chunked(q, k, v, beta, g)
    o = rms_norm(o, out_norm).astype(z.dtype) * jax.nn.silu(z.reshape(b, s, GDN_HEADS, GDN_DV))
    return o.reshape(b, s, GDN_HEADS * GDN_DV)

def moba_branch(qkv, pos, q_norm, k_norm):
    b, s, _ = qkv.shape
    h, dh, bs = MOBA_HEADS, MOBA_DH, MOBA_BLOCK
    q, k, v = (t.reshape(b, s, h, dh) for t in jnp.split(qkv, 3, axis=-1))
    q = rope(rms_norm(q, q_norm), pos)
    k = rope(rms_norm(k, k_norm), pos)
    nb = -(-s // bs)
    s_pad = nb * bs

    def prep(t):
        return jnp.pad(jnp.transpose(t, (0, 2, 1, 3)), ((0, 0), (0, 0), (0, s_pad - s), (0, 0)))

    q, k, v = prep(q), prep(k), prep(v)
    kb = k.reshape(b, h, nb, bs, dh)
    vb = v.reshape(b, h, nb, bs, dh)
    k_mean = jnp.mean(kb.astype(jnp.float32), axis=3)
    gate = jnp.einsum('bhsd,bhnd->bhsn', q.astype(jnp.float32), k_mean)
    q_blk = jnp.arange(s_pad) // bs
    gate = jnp.where(jnp.arange(nb)[None, :] < q_blk[:, None], gate, NEG_INF_2)
    n_sel = min(MOBA_TOPK, nb)
    _, sel = lax.top_k(gate, n_sel)
    sel_valid = sel < q_blk[:, None]
    scale = dh ** -0.5
    b_idx = jnp.arange(b)[:, None, None, None]
    h_idx = jnp.arange(h)[None, :, None, None]
    key_off = jnp.arange(bs)

    def one_chunk(ci):
        start = ci * MOBA_QCHUNK
        q_c = lax.dynamic_slice_in_dim(q, start, MOBA_QCHUNK, axis=2)
        sel_c = lax.dynamic_slice_in_dim(sel, start, MOBA_QCHUNK, axis=2)
        valid_c = lax.dynamic_slice_in_dim(sel_valid, start, MOBA_QCHUNK, axis=2)
        k_sel = kb[b_idx, h_idx, sel_c]
        v_sel = vb[b_idx, h_idx, sel_c]
        s_sel = jnp.einsum('bhqd,bhqnkd->bhqnk', q_c, k_sel, preferred_element_type=jnp.float32) * scale
        s_sel = jnp.where(valid_c[..., None], s_sel, NEG_INF_2)
        j = start // bs
        k_own = lax.dynamic_index_in_dim(kb, j, axis=2, keepdims=False)
        v_own = lax.dynamic_index_in_dim(vb, j, axis=2, keepdims=False)
        s_own = jnp.einsum('bhqd,bhkd->bhqk', q_c, k_own, preferred_element_type=jnp.float32) * scale
        q_pos = start + jnp.arange(MOBA_QCHUNK)
        k_pos = j * bs + key_off
        s_own = jnp.where(k_pos[None, :] <= q_pos[:, None], s_own, NEG_INF_2)
        logits = jnp.concatenate([s_sel.reshape(b, h, MOBA_QCHUNK, n_sel * bs), s_own], axis=-1)
        p = jax.nn.softmax(logits, axis=-1).astype(v.dtype)
        p_sel = p[..., :n_sel * bs].reshape(b, h, MOBA_QCHUNK, n_sel, bs)
        p_own = p[..., n_sel * bs:]
        return (jnp.einsum('bhqnk,bhqnkd->bhqd', p_sel, v_sel)
                + jnp.einsum('bhqk,bhkd->bhqd', p_own, v_own))

    o = lax.map(one_chunk, jnp.arange(s_pad // MOBA_QCHUNK))
    o = jnp.transpose(o, (1, 0, 3, 2, 4)).reshape(b, s_pad, h * dh)
    return o[:, :s]

def second_inputs(seed: int = 0) -> dict:
    key = jax.random.key(seed)
    ks = jax.random.split(key, 24)
    L = DEPTH_2
    f32 = jnp.float32

    def nrm(k, shape, fan_in):
        return jax.random.normal(k, shape, f32) * (fan_in ** -0.5)

    def gain(k, shape):
        return 1.0 + 0.02 * jax.random.normal(k, shape, f32)

    dt = jnp.exp(jax.random.uniform(ks[14], (L, GDN_HEADS), f32, np.log(1e-3), np.log(1e-1)))
    return {
        'x': jax.random.normal(ks[0], (BATCH, SEQ, D_MODEL), f32),
        'ffa_norm': gain(ks[1], (L, D_MODEL)),
        'ffa_w_in': nrm(ks[2], (L, D_MODEL, 2 * D_FF), D_MODEL),
        'ffa_w_out': nrm(ks[3], (L, D_FF, D_MODEL), D_FF),
        'mix_norm': gain(ks[4], (L, D_MODEL)),
        'w_in': nrm(ks[5], (L, D_MODEL, D_IN), D_MODEL),
        'mla_cq_norm': gain(ks[6], (L, MLA_Q_RANK)),
        'mla_ckv_norm': gain(ks[7], (L, MLA_KV_RANK)),
        'mla_w_uq': nrm(ks[8], (L, MLA_Q_RANK, MLA_HEADS * MLA_QK), MLA_Q_RANK),
        'mla_w_ukv': nrm(ks[9], (L, MLA_KV_RANK, MLA_HEADS * (MLA_NOPE + MLA_V)), MLA_KV_RANK),
        'mla_q_norm': gain(ks[10], (L, MLA_QK)),
        'mla_k_norm': gain(ks[11], (L, MLA_QK)),
        'gdn_conv': nrm(ks[12], (L, GDN_CONV, GDN_HEADS * (2 * GDN_DK + GDN_DV)), GDN_CONV),
        'gdn_a_log': jnp.log(jax.random.uniform(ks[13], (L, GDN_HEADS), f32, 1.0, 16.0)),
        'gdn_dt_bias': dt + jnp.log(-jnp.expm1(-dt)),
        'gdn_out_norm': gain(ks[15], (L, GDN_DV)),
        'moba_q_norm': gain(ks[16], (L, MOBA_DH)),
        'moba_k_norm': gain(ks[17], (L, MOBA_DH)),
        'w_branch': nrm(ks[18], (L, N_BRANCH, MIX_WIDTH_2, D_MODEL), MIX_WIDTH_2),
        'w_out': nrm(ks[19], (L, D_MODEL, D_MODEL), D_MODEL),
        'ffb_norm': gain(ks[20], (L, D_MODEL)),
        'ffb_w_in': nrm(ks[21], (L, D_MODEL, 2 * D_FF), D_MODEL),
        'ffb_w_out': nrm(ks[22], (L, D_FF, D_MODEL), D_FF),
    }

def second_block(x, ffa_norm, ffa_w_in, ffa_w_out, mix_norm, w_in, mla_cq_norm, mla_ckv_norm,
              mla_w_uq, mla_w_ukv, mla_q_norm, mla_k_norm, gdn_conv, gdn_a_log, gdn_dt_bias,
              gdn_out_norm, moba_q_norm, moba_k_norm, w_branch, w_out, ffb_norm, ffb_w_in,
              ffb_w_out):
    b, s, _ = x.shape
    pos = jnp.arange(s, dtype=jnp.int32)
    for l in range(DEPTH_2):
        x = x + 0.5 * swiglu(rms_norm(x, ffa_norm[l]), ffa_w_in[l], ffa_w_out[l])
        h = rms_norm(x, mix_norm[l])
        (c_q, c_kv, k_rope, g_q, g_k, g_v, g_b, g_a, g_z, m_qkv, gate_logits) = split_cols(h @ w_in[l], IN_SPLITS)
        o_mla = mla_branch(c_q, c_kv, k_rope, pos, mla_cq_norm[l], mla_ckv_norm[l], mla_w_uq[l],
                           mla_w_ukv[l], mla_q_norm[l], mla_k_norm[l])
        o_gdn = gdn_branch(g_q, g_k, g_v, g_b, g_a, g_z, gdn_conv[l], gdn_a_log[l], gdn_dt_bias[l],
                           gdn_out_norm[l])
        o_moba = moba_branch(m_qkv, pos, moba_q_norm[l], moba_k_norm[l])
        branches = jnp.stack([o_mla, o_gdn, o_moba], axis=2)
        up = jnp.einsum('bsnw,nwd->bsnd', branches, w_branch[l])
        gates = jax.nn.sigmoid(gate_logits.reshape(b, s, N_BRANCH, D_MODEL))
        x = x + jnp.sum(gates * up, axis=2) @ w_out[l]
        x = x + 0.5 * swiglu(rms_norm(x, ffb_norm[l]), ffb_w_in[l], ffb_w_out[l])
    return x


def setup_inputs(seed=0):
    out = dict(first_inputs(seed))
    for name, value in second_inputs(seed + 1).items():
        if name != "x":
            out[name + "_2"] = value
    return out


def reference(
    x, p, g_mix, w_in, w_pool, pool_scale, rel_bias, w_out, g_ffn, w_router, b_router,
    w_gate_up, b_gate_up, w_down, b_down, g_ple, w_ple_gate, w_ple_proj, g_final, ffa_norm_2,
    ffa_w_in_2, ffa_w_out_2, mix_norm_2, w_in_2, mla_cq_norm_2, mla_ckv_norm_2, mla_w_uq_2,
    mla_w_ukv_2, mla_q_norm_2, mla_k_norm_2, gdn_conv_2, gdn_a_log_2, gdn_dt_bias_2,
    gdn_out_norm_2, moba_q_norm_2, moba_k_norm_2, w_branch_2, w_out_2, ffb_norm_2, ffb_w_in_2,
    ffb_w_out_2,
):
    x = first_block(
        x, p, g_mix, w_in, w_pool, pool_scale, rel_bias, w_out, g_ffn, w_router, b_router,
        w_gate_up, b_gate_up, w_down, b_down, g_ple, w_ple_gate, w_ple_proj, g_final,
    )
    return second_block(
        x, ffa_norm_2, ffa_w_in_2, ffa_w_out_2, mix_norm_2, w_in_2, mla_cq_norm_2,
        mla_ckv_norm_2, mla_w_uq_2, mla_w_ukv_2, mla_q_norm_2, mla_k_norm_2, gdn_conv_2,
        gdn_a_log_2, gdn_dt_bias_2, gdn_out_norm_2, moba_q_norm_2, moba_k_norm_2, w_branch_2,
        w_out_2, ffb_norm_2, ffb_w_in_2, ffb_w_out_2,
    )


_drawn_inputs = setup_inputs


def setup_inputs(seed=0):
    import zlib

    import numpy as np

    out = dict(_drawn_inputs(seed))
    spreads = {}
    factors = {'b_gate_up': 8.0,
     'b_down': 8.0,
     'g_ple': 5.631,
     'ffa_norm_2': 4.241,
     'mix_norm_2': 3.331,
     'mla_cq_norm_2': 8.0,
     'mla_ckv_norm_2': 8.0,
     'mla_q_norm_2': 8.0,
     'mla_k_norm_2': 8.0,
     'gdn_out_norm_2': 7.176,
     'moba_q_norm_2': 8.0,
     'moba_k_norm_2': 8.0,
     'ffb_norm_2': 5.158}
    for name, (base, spread) in spreads.items():
        noise = np.random.default_rng([zlib.crc32(name.encode()), seed]).standard_normal(out[name].shape)
        drawn = base * np.exp(spread * noise) if base else spread * noise
        out[name] = jnp.asarray(drawn.astype(out[name].dtype))
    for name, factor in factors.items():
        out[name] = (out[name] * factor).astype(out[name].dtype)
    return out
```

```python
import concourse.bass as bass
from concourse import mybir
from concourse.alu_op_type import AluOpType as ALU
from contextlib import ExitStack
import numpy as np

F32 = mybir.dt.float32
I32 = mybir.dt.int32
ACT = mybir.ActivationFunctionType
AX = mybir.AxisListType

P = 128
S, D = 256, 1024
NT, KC = S // P, D // P
EPS = 1e-6
NEG = -1e30
H, V = 8, 64
E, TOPK, FE = 32, 4, 1024
DFF = 2816
FC = DFF // P
UNIT = 4096
SLOTS = 6
FIRST_UNITS, PLE_UNITS, EXPERT_UNITS = 6, 3, 6
FFN_IN_UNITS, FFN_OUT_UNITS = FC // 2, 6
U_FFA_IN, U_FFA_OUT = 0, 11
U_MLA, U_MLA_UP, U_MOBA, U_GDN, U_Z, U_GATES = 17, 18, 19, 22, 25, 26
U_BRANCH, U_WOUT, U_FFB_IN, U_FFB_OUT = 32, 35, 37, 48
LAYER_UNITS = 54
LAYER_WORDS = [UNIT] * LAYER_UNITS
LAYER_WORDS[U_FFA_OUT + 5] = LAYER_WORDS[U_FFB_OUT + 5] = UNIT // 2
LAYER_WORDS[U_MLA], LAYER_WORDS[U_MLA_UP] = KC * 424, 2560
PLE_WORDS = [UNIT, UNIT, UNIT // 2]
LAYERS = 2
MLA_D, MOBA_D, FIRST_D = 96, 64, 64
MLA_COLS = 424
GH = 4


def columns(widths):
    at, out = 0, {}
    for name, w in widths:
        out[name] = (at, at + w)
        at += w
    out["all"] = (0, at)
    return out


CONST = columns([("ident", P), ("flip", P), ("ones", P), ("tri", P), ("tri_strict", P), ("after_mask", P), ("causal", 2 * P),
                 ("iota", P), ("levels", 7 * P), ("cos16", 32), ("sin16", 32), ("cos32", 64), ("sin32", 64)])
FVEC = columns([("g_mix", KC), ("g_ffn", KC), ("g_ple", KC), ("pool_scale", 4), ("b_router", E), ("w_router", KC * E)])
LVEC = columns([("g_ffa", KC), ("g_mix", KC), ("g_ffb", KC), ("conv", 48), ("c_norm", 3), ("q_norm", 96),
                ("k_norm", 96), ("out_norm", P), ("moba_q", 64), ("moba_k", 64), ("a_log", GH), ("dt", GH)])
POOL_WORDS = 4 * NT * S
ACT_T, SILU_TMP = 0, 5632
BRANCH_T, COMB, MLA_ROWS, WORK = 0, 3072, 5120, 5968
STATS, SCRATCH = 17232, 18200


class BankUses:

    def __init__(self):
        self.count, self.at = [0] * 8, {}

    def add(self, key, bank):
        self.at[key] = (bank, self.count[bank])
        self.count[bank] += 1


class Core:

    def __init__(self, nc, ctx):
        self.nc, self.ctx, self.names = nc, ctx, {}
        sb = lambda name, shape, dt=F32: ctx.enter_context(nc.sbuf_tensor(name, shape, dt))
        self.ring = [sb(f"ring{i}", [P, UNIT]) for i in range(SLOTS)]
        self.x = sb("x_res", [P, NT, D])
        self.h = sb("h_rows", [P, NT, D])
        self.hT = sb("hT", [P, KC, S])
        self.const = sb("const", [P, CONST["all"][1]])
        self.fvec = sb("fvec", [P, FVEC["all"][1]])
        self.lvec = sb("lvec", [P, LVEC["all"][1]])
        self.scratch = sb("scratch", [P, SCRATCH])
        self.bank = [ctx.enter_context(nc.psum_tensor(f"bank{b}", [P, 512], F32)) for b in range(8)]
        sem = lambda name: ctx.enter_context(nc.semaphore(name))
        self.arrived = [sem(f"weights_arrived{i}") for i in range(SLOTS)]
        self.stored = sem("output_stored")
        self.later_arrived = [sem(f"later_weights_arrived{i}") for i in range(SLOTS)]
        self.bank_full = [sem(f"bank_full{b}") for b in range(8)]
        self.bank_free = [sem(f"bank_free{b}") for b in range(8)]
        self.dve_step = sem("dve_step")
        self.act_step = sem("act_step")
        self.pool = [sem(f"stage{i}") for i in range(80)]
        self.clear = range(self.later_arrived[0].num, self.pool[-1].num + 1)

    def c(self, name, w=None):
        a, b = CONST[name]
        return self.const[:, a:b]

    def f(self, name):
        a, b = FVEC[name]
        return self.fvec[:, a:b]

    def lv(self, name):
        a, b = LVEC[name]
        return self.lvec[:, a:b]

    def s(self, at, *shape):
        n = int(np.prod(shape))
        v = self.scratch[:, at:at + n]
        if len(shape) == 1:
            return v
        names = "abcd"[:len(shape)]
        return v.rearrange(f"p ({' '.join(names)}) -> p {' '.join(names)}", **dict(zip(names, shape)))

    def begin(self, uses):
        self.names, self.uses = {}, uses

    def sem(self, name):
        if name not in self.names:
            self.names[name] = self.pool[len(self.names)]
        return self.names[name]

    def end_phase(self):
        self.nc.all_engine_barrier(sems_to_clear=self.clear)

    def claim(self, pe, key):
        b, k = self.uses.at[key]
        if k:
            pe.wait_ge(self.bank_free[b], k)
        return self.bank[b], self.bank_full[b]

    def filled(self, eng, key):
        b, k = self.uses.at[key]
        eng.wait_ge(self.bank_full[b], k + 1)
        return self.bank[b], self.bank_free[b]

    def evacuated(self, eng, *keys):
        for key in keys:
            b, k = self.uses.at[key]
            eng.wait_ge(self.bank_free[b], k + 1)


def part(bank, *shape):
    n = int(np.prod(shape))
    names = "abc"[:len(shape)]
    return bank[:, 0:n].rearrange(f"p ({' '.join(names)}) -> p {' '.join(names)}", **dict(zip(names, shape)))


def chain_of(eng, sem):
    count = [0]

    def link(ins):
        count[0] += 1
        ins.then_inc(sem, 1)
        eng.wait_ge(sem, count[0])
    return link



def rstd_dve(k, dve, link, v, mean, n):
    link(k.nc.vector.tensor_scalar(v, v, mean, EPS, ALU.mult, ALU.add))
    k.nc.vector.reciprocal(v, v).then_inc(k.sem("inverse_variance"), 1)
    dve.wait_ge(k.sem("rstd_ready"), n + 1)


def rstd_act(k, act, v, n):
    act.wait_ge(k.sem("inverse_variance"), n + 1)
    k.nc.scalar.activation(v, v, ACT.Sqrt).then_inc(k.sem("rstd_ready"), 1)


def bc(ap, shape):
    return ap.to_broadcast(shape)



def norm_uses(uses, n, banks=(0, 1, 2, 3)):
    for t in range(NT):
        for half in range(2):
            uses.add(("norm", n, t, half), banks[2 * t + half])


def norm_act(k, act, n, x_ready=None, power=0):
    nc, st = k.nc, k.s(STATS, 512)
    if x_ready is not None:
        act.wait_ge(*x_ready)
    for t in range(NT):
        nc.scalar.activation(k.h[:, t, :], k.x[:, t, :], ACT.Square, accum_out=st[:, t:t + 1]).then_inc(k.sem("ss_ready"), 1)
    rstd_act(k, act, st[:, 0:2], power)


def norm_dve(k, dve, link, n, gain, power=0):
    nc, st = k.nc, k.s(STATS, 512)
    dve.wait_ge(k.sem("ss_ready"), 2 * (n + 1))
    rstd_dve(k, dve, link, st[:, 0:2], 1.0 / D, power)
    for t in range(NT):
        nc.vector.tensor_scalar(k.h[:, t, :], k.x[:, t, :], st[:, t:t + 1], None, ALU.mult).then_inc(k.sem("h_ready"), 1)
    for t in range(NT):
        for half in range(2):
            b, free = k.filled(dve, ("norm", n, t, half))
            nc.vector.tensor_tensor(k.hT[:, 4 * half:4 * half + 4, t * P:(t + 1) * P], part(b, 4, P),
                                    bc(gain[:, 4 * half:4 * half + 4].unsqueeze(2), [P, 4, P]), ALU.mult).then_inc(free, 1)


def norm_pe(k, pe, n):
    nc = k.nc
    for t in range(NT):
        pe.wait_ge(k.sem("h_ready"), 2 * n + t + 1)
        for half in range(2):
            b, full = k.claim(pe, ("norm", n, t, half))
            for j in range(4):
                c = 4 * half + j
                last = nc.tensor.transpose(b[:, j * P:(j + 1) * P], k.h[:, t, c * P:(c + 1) * P], k.c("ident"))
            last.then_inc(full, 1)


def hT_written(k, eng, n):
    k.evacuated(eng, *[("norm", n, t, half) for t in range(NT) for half in range(2)])



def attn_uses(uses, n):
    for q in range(2):
        for t in range(NT):
            for half in range(2):
                uses.add(("qkT", n, q, t, half), 4 * q + 2 * t + half)
    for t in range(NT):
        for pair in range(4):
            uses.add(("score", n, t, pair), 4 * t + pair)
    for half in range(2):
        uses.add(("pT", n, 0, half), half)
    for pair in range(4):
        uses.add(("pT", n, 1, pair), 2 + pair)
    for t in range(NT):
        uses.add(("o", n, t), 6 + t)
    for t in range(NT):
        uses.add(("oT", n, t), t)


class Attn:

    def __init__(self, k, n, d, qk, v, qkT, prob, pT, o, outT):
        self.n, self.d = n, d
        self.qk = k.s(qk, 2 * NT * H, d)
        self.v = k.s(v, NT, H, V)
        self.qkT = k.s(qkT, 2, H, S)
        self.prob = [k.s(prob, H, P), k.s(prob + H * P, H, 2 * P)]
        self.pT = [k.s(pT, H, 1, P), k.s(pT + H * P, H, 2, P)]
        self.o = k.s(o, NT, H, V)
        self.outT = k.s(outT, 4, S)
        self.st = k.s(STATS + 64 + 0, 64)


def attn_pe(k, pe, a):
    nc, n, d = k.nc, a.n, a.d
    pe.wait_ge(k.sem("qk_ready"), a.n + 1)
    for q in range(2):
        for t in range(NT):
            for half in range(2):
                b, full = k.claim(pe, ("qkT", n, q, t, half))
                for j in range(4):
                    row = (q * NT + t) * H + 4 * half + j
                    last = nc.tensor.transpose(b[0:d, j * P:(j + 1) * P], a.qk[:, row, :], k.c("ident"))
                last.then_inc(full, 1)
    k.evacuated(pe, *[("qkT", n, q, t, half) for q in range(2) for t in range(NT) for half in range(2)])
    for t in range(NT):
        w = (t + 1) * P
        for pair in range(4):
            b, full = k.claim(pe, ("score", n, t, pair))
            for j in range(2):
                h = 2 * pair + j
                last = nc.tensor.matmul(b[:, j * 2 * P:j * 2 * P + w], a.qkT[0:d, 0, h, t * P:(t + 1) * P],
                                        a.qkT[0:d, 1, h, 0:w], start=True, stop=True)
            last.then_inc(full, 1)
    for t in range(NT):
        per = 4 if t == 0 else 2
        for g in range(H // per):
            b, full = k.claim(pe, ("pT", n, t, g))
            for j in range(per):
                h = per * g + j
                pe.wait_ge(k.sem("prob_ready"), 2 * H * n + H * t + h + 1)
                for c in range(t + 1):
                    at = (j * (t + 1) + c) * P
                    last = nc.tensor.transpose(b[:, at:at + P], a.prob[t][:, h, c * P:(c + 1) * P], k.c("ident"))
            last.then_inc(full, 1)
    for t in range(NT):
        b, full = k.claim(pe, ("o", n, t))
        k.evacuated(pe, *[("pT", n, t, g) for g in range(2 if t == 0 else 4)])
        for h in range(H):
            for c in range(t + 1):
                last = nc.tensor.matmul(b[:, h * V:(h + 1) * V], a.pT[t][:, h, c, :], a.v[:, c, h, :],
                                        start=(c == 0), stop=(c == t))
        last.then_inc(full, 1)
    for t in range(NT):
        b, full = k.claim(pe, ("oT", n, t))
        k.evacuated(pe, ("o", n, t))
        for c in range(4):
            last = nc.tensor.transpose(b[:, c * P:(c + 1) * P], a.o[:, t, 2 * c:2 * c + 2, :], k.c("ident"))
        last.then_inc(full, 1)


def attn_act(k, act, a):
    nc, n, d = k.nc, a.n, a.d
    for q in range(2):
        for t in range(NT):
            for half in range(2):
                b, free = k.filled(act, ("qkT", n, q, t, half))
                nc.scalar.copy(a.qkT[0:d, q, 4 * half:4 * half + 4, t * P:(t + 1) * P], part(b, 4, P)[0:d])\
                    .then_inc(free, 1)
    for t in range(NT):
        for h in range(H):
            act.wait_ge(k.sem("max_ready"), 8 * n + 4 * t + h // 2 + 1)
            nc.scalar.activation(a.prob[t][:, h, :], a.prob[t][:, h, :], ACT.Exp, bias=a.st[:, 8 * t + h:8 * t + h + 1],
                                 accum_out=a.st[:, 16 + 8 * t + h:17 + 8 * t + h]).then_inc(k.sem("prob_ready"), 1)
    for t in range(NT):
        per = 4 if t == 0 else 2
        for g in range(H // per):
            b, free = k.filled(act, ("pT", n, t, g))
            nc.scalar.copy(a.pT[t][:, per * g:per * g + per, :, :].rearrange("p a b c -> p (a b c)"),
                           b[:, 0:per * (t + 1) * P]).then_inc(free, 1)


def attn_dve(k, dve, link, a, scale, mask):
    nc, n = k.nc, a.n
    for t in range(NT):
        w = (t + 1) * P
        for pair in range(4):
            b, free = k.filled(dve, ("score", n, t, pair))
            s = a.prob[t][:, 2 * pair:2 * pair + 2, :]
            nc.vector.scalar_tensor_tensor(out=s, in0=part(b, 2, 2 * P)[:, :, 0:w], scalar=scale, in1=mask(t, pair),
                                           op0=ALU.mult, op1=ALU.add).then_inc(free, 1)
            k.evacuated(dve, ("score", n, t, pair))
            m = 8 * t + 2 * pair
            nc.vector.tensor_reduce(a.st[:, m:m + 2], s, AX.X, ALU.max, negate=True).then_inc(k.sem("max_ready"), 1)
    for t in range(NT):
        dve.wait_ge(k.sem("prob_ready"), 2 * H * n + H * (t + 1))
        link(nc.vector.reciprocal(a.st[:, 32 + 8 * t:40 + 8 * t], a.st[:, 16 + 8 * t:24 + 8 * t]))
        b, free = k.filled(dve, ("o", n, t))
        nc.vector.tensor_tensor(a.o[:, t, :, :], part(b, H, V), bc(a.st[:, 32 + 8 * t:40 + 8 * t].unsqueeze(2), [P, H, V]),
                                ALU.mult).then_inc(free, 1)
    for t in range(NT):
        b, free = k.filled(dve, ("oT", n, t))
        nc.vector.tensor_copy(a.outT[:, :, t * P:(t + 1) * P], part(b, 4, P)).then_inc(free, 1)


def rows_pe(k, pe, key, w, lhsT, cols, chunks=KC):
    for t in range(NT):
        b, full = k.claim(pe, key + (t,))
        for c in range(chunks):
            last = k.nc.tensor.matmul(b[:, 0:cols], lhsT[:, c, t * P:(t + 1) * P], w[:, c, 0:cols],
                                      start=(c == 0), stop=(c == chunks - 1))
        last.then_inc(full, 1)
    return last



def ffn_uses(uses, n):
    for u in range(FFN_IN_UNITS):
        uses.add(("gate", n, u), 2 * (u % 2))
        uses.add(("up", n, u), 2 * (u % 2) + 1)
    for t in range(NT):
        for v in range(2):
            uses.add(("ffn_out", n, t, v), 4 + 2 * t + v)


def ffn_pe(k, pe, n, first_in, first_out, unit):
    nc = k.nc
    hT_written(k, pe, 2 * n)
    for u in range(FFN_IN_UNITS):
        w = unit(pe, first_in + u).rearrange("p (c g n) -> p c g n", c=KC, g=2)
        for g, key in enumerate(("gate", "up")):
            b, full = k.claim(pe, (key, n, u))
            for j in range(2):
                for c in range(KC):
                    last = nc.tensor.matmul(b[:, j * S:(j + 1) * S], w[:, c, g, j * P:(j + 1) * P], k.hT[:, c, :],
                                            start=(c == 0), stop=(c == KC - 1))
            last.then_inc(full, 1)
    out = {(t, v): k.claim(pe, ("ffn_out", n, t, v)) for t in range(NT) for v in range(2)}
    for u in range(FFN_OUT_UNITS):
        w = unit(pe, first_out + u).rearrange("p (c n) -> p c n", c=4)
        for c in range(4 * u, min(4 * u + 4, FC)):
            if c % 2 == 0:
                k.evacuated(pe, ("up", n, c // 2))
            for t in range(NT):
                for v in range(2):
                    last = nc.tensor.matmul(out[t, v][0][:, :], k.s(ACT_T, FC, S)[:, c, t * P:(t + 1) * P],
                                            w[:, c - 4 * u, v * 512:(v + 1) * 512], start=(c == 0), stop=(c == FC - 1))
                    if c == FC - 1:
                        last.then_inc(out[t, v][1], 1)
        if u < FFN_OUT_UNITS - 1:
            last.then_inc(k.sem("out_unit_used"), 1)


def ffn_act(k, act, n):
    for u in range(FFN_IN_UNITS):
        b, free = k.filled(act, ("gate", n, u))
        if u >= 2:
            k.evacuated(act, ("up", n, u - 2))
        k.nc.scalar.activation(k.s(SILU_TMP, 2, 512)[:, u % 2, :], b[:, :], ACT.Silu).then_inc(free, 1)


def ffn_dve(k, dve, n, x_sem):
    nc = k.nc
    for u in range(FFN_IN_UNITS):
        b, free = k.filled(dve, ("up", n, u))
        k.evacuated(dve, ("gate", n, u))
        nc.vector.tensor_tensor(k.s(ACT_T, FC // 2, 512)[:, u, :], k.s(SILU_TMP, 2, 512)[:, u % 2, :], b[:, :],
                                ALU.mult).then_inc(free, 1)
    for t in range(NT):
        for v in range(2):
            b, free = k.filled(dve, ("ffn_out", n, t, v))
            x = k.x[:, t, v * 512:(v + 1) * 512]
            nc.vector.scalar_tensor_tensor(out=x, in0=b[:, :], scalar=0.5, in1=x, op0=ALU.mult, op1=ALU.add)\
                .then_inc(free, 1)



def head_norm_dve(k, dve, link, qk, sq, d, gains, power):
    nc, n = k.nc, 2 * NT * H
    st = k.s(STATS + 128, n)
    link(nc.vector.tensor_tensor(sq, qk, qk, ALU.mult))
    link(nc.vector.tensor_reduce(st, sq, AX.X, ALU.add))
    rstd_dve(k, dve, link, st, 1.0 / d, power)
    link(nc.vector.tensor_tensor(qk, qk, bc(st.unsqueeze(2), [P, n, d]), ALU.mult))
    for i, g in enumerate(gains):
        half = qk[:, i * n // 2:(i + 1) * n // 2, :]
        link(nc.vector.tensor_tensor(half, half, bc(g.unsqueeze(1), [P, n // 2, d]), ALU.mult))


def rope_dve(k, dve, link, qk, tmp, at, half, cos, sin, last_sem):
    nc = k.nc
    n = NT * H * half
    for i in range(2):
        rows = qk[:, i * NT * H:(i + 1) * NT * H, :].rearrange("p (t h) d -> p t h d", t=NT)
        x1, x2 = rows[:, :, :, at:at + half], rows[:, :, :, at + half:at + 2 * half]
        a, b, c, d = (k.s(tmp + j * n, NT, H, half) for j in range(4))
        cb, sb = (bc(v.rearrange("p (t f) -> p t f", t=NT).unsqueeze(2), [P, NT, H, half]) for v in (cos, sin))
        nc.vector.tensor_tensor(a, x1, cb, ALU.mult)
        nc.vector.tensor_tensor(b, x2, sb, ALU.mult)
        nc.vector.tensor_tensor(c, x2, cb, ALU.mult)
        link(nc.vector.tensor_tensor(d, x1, sb, ALU.mult))
        nc.vector.tensor_tensor(x1, a, b, ALU.subtract)
        ins = nc.vector.tensor_tensor(x2, c, d, ALU.add)
        if i == 0:
            link(ins)
        else:
            ins.then_inc(last_sem, 1)



GDN_RAW, GDN_CONV, GDN_SQ, GDN_V, GDN_KDEC, GDN_DIAG = 5968, 9076, 12148, 14196, 15220, 15732
GDN_DECAY, GDN_M, GDN_QK = 5968, 6992, 8016
GDN_X, GDN_XT, GDN_P, GDN_OT = 12148, 13172, 3072, 4096
LEVELS = 7


def gdn_uses(uses):
    for i in range(3):
        for pair in range(2):
            uses.add(("raw", i, pair), 2 * i + pair)
    for t in range(NT):
        uses.add(("z", t), 6 + t)
    for b in range(4):
        uses.add(("l2", b), b)
    uses.add(("gc",), 4)
    for t in range(NT):
        uses.add(("gcB", t), 5 + t)
    for t in range(NT):
        uses.add(("vT", t), t)
    for t in range(NT):
        uses.add(("betaB", t), 2 + t)
    for t in range(NT):
        uses.add(("KK", t), (7, 4)[t])
    for t in range(NT):
        uses.add(("QK", t), 5 + t)
    uses.add(("kdec",), 0)
    for lev in range(LEVELS):
        for t in range(NT):
            uses.add(("P", lev, t), 4 * t + 3)
        for t in range(NT):
            if lev < LEVELS - 1:
                uses.add(("XP", lev, t), 4 * t + 1)
            uses.add(("PX", lev, t), 4 * t + 2)
    for key, b in ((("vn", 0), 0), (("go", 0), 1), (("S1",), 2), (("KS",), 3), (("QS",), 4), (("vn", 1), 5),
                   (("go", 1), 6), (("goT", 0), 0), (("goT", 1), 1)):
        uses.add(key, b)


class Gdn:
    def __init__(self, k):
        self.raw = k.s(GDN_RAW, 12, S + 3)
        self.cv = k.s(GDN_CONV, 12, S)
        self.sq = k.s(GDN_SQ, 8, S)
        self.v = k.s(GDN_V, NT, GH, P)
        self.kdec = k.s(GDN_KDEC, GH, P)
        self.gdiag = k.s(GDN_DIAG, NT, GH, P)
        self.bdiag = k.h[:, 1, :].rearrange("p (t h n) -> p t h n", t=NT, h=GH)
        self.z = k.h[:, 0, :].rearrange("p (t n) -> p t n", t=NT)
        self.o = self.bdiag
        self.decay, self.m, self.qk = (k.s(a, NT, GH, P) for a in (GDN_DECAY, GDN_M, GDN_QK))
        self.X, self.XT, self.P, self.OT = (k.s(a, NT, GH, P) for a in (GDN_X, GDN_XT, GDN_P, GDN_OT))
        self.R, self.vn, self.S1, self.tmp = self.OT, self.X, k.s(GDN_P, GH, P), k.s(GDN_P + GH * P, GH, P)
        small = lambda at, *shape: k.s(STATS + 256 + at, *shape)
        self.beta, self.xa, self.nax, self.ex, self.ln = (small(8 * i, NT, GH) for i in range(5))
        self.eal, self.g, self.gsum, self.glast = small(40, GH), small(44, NT, GH), small(52, NT, GH), small(60, GH)
        self.gsum_all, self.eg, self.dk, self.ostat = small(52, 12), small(64, NT, GH), small(72, GH), small(76, 8)
        self.b_in = k.s(MLA_ROWS, NT, MLA_COLS)[:, :, 416:420]
        self.a_in = k.s(MLA_ROWS, NT, MLA_COLS)[:, :, 420:424]


def heads_mm(nc, b, lhsT, rhs):
    for h in range(GH):
        last = nc.tensor.matmul(b[:, h * P:(h + 1) * P], lhsT[:, h, :], rhs[:, h, :], start=True, stop=True)
    return last


def gdn_pe(k, pe, unit):
    nc, G = k.nc, Gdn(k)
    for i in range(3):
        w = unit(pe, U_GDN + i).rearrange("p (c n) -> p c n", c=KC)
        for pair in range(2):
            b, full = k.claim(pe, ("raw", i, pair))
            for j in range(2):
                for c in range(KC):
                    col = (2 * pair + j) * P
                    last = nc.tensor.matmul(b[:, j * S:(j + 1) * S], w[:, c, col:col + P], k.hT[:, c, :],
                                            start=(c == 0), stop=(c == KC - 1))
            last.then_inc(full, 1)
    rows_pe(k, pe, ("z",), unit(pe, U_Z).rearrange("p (c n) -> p c n", c=KC), k.hT, 512)
    for b4 in range(4):
        b, full = k.claim(pe, ("l2", b4))
        pe.wait_ge(k.sem("sq_ready"), b4 // 2 + 1)
        nc.tensor.matmul(b[:, :], k.c("ones"), G.sq[:, 2 * b4:2 * b4 + 2, :], start=True, stop=True).then_inc(full, 1)
    b, full = k.claim(pe, ("gc",))
    pe.wait_ge(k.sem("g_ready"), 1)
    nc.tensor.matmul(b[:, 0:4], k.c("tri"), G.g[:, 0, :], start=True, stop=True)
    nc.tensor.matmul(b[:, 4:8], k.c("tri"), G.g[:, 1, :], start=True, stop=True)
    nc.tensor.matmul(b[:, 8:12], k.c("ones"), G.g[:, 0, :], start=True, stop=True).then_inc(full, 1)
    pe.wait_ge(k.sem("gdiag_ready"), 1)
    for t in range(NT):
        b, full = k.claim(pe, ("gcB", t))
        nc.tensor.matmul(b[:, :], k.c("ones"), G.gdiag[:, t, :, :], start=True, stop=True).then_inc(full, 1)
    pe.wait_ge(k.sem("conv_silu"), 3)
    for t in range(NT):
        b, full = k.claim(pe, ("vT", t))
        for h in range(GH):
            last = nc.tensor.transpose(b[:, h * P:(h + 1) * P], G.cv[:, 8 + h, t * P:(t + 1) * P], k.c("ident"))
        last.then_inc(full, 1)
    pe.wait_ge(k.sem("bdiag_ready"), 1)
    for t in range(NT):
        b, full = k.claim(pe, ("betaB", t))
        nc.tensor.matmul(b[:, :], k.c("ones"), G.bdiag[:, t, :, :], start=True, stop=True).then_inc(full, 1)
    pe.wait_ge(k.sem("l2_done"), 1)
    for key, at in (("KK", GH), ("QK", 0)):
        for t in range(NT):
            b, full = k.claim(pe, (key, t))
            cols = slice(t * P, (t + 1) * P)
            heads_mm(nc, b, G.cv[:, GH:2 * GH, cols], G.cv[:, at:at + GH, cols]).then_inc(full, 1)
    b, full = k.claim(pe, ("kdec",))
    for h in range(GH):
        last = nc.tensor.transpose(b[:, h * P:(h + 1) * P], G.cv[:, GH + h, 0:P], k.c("ident"))
    last.then_inc(full, 1)
    for lev in range(LEVELS):
        for t in range(NT):
            b, full = k.claim(pe, ("P", lev, t))
            pe.wait_ge(k.sem("ot_ready"), 2 * lev + t + 1)
            if lev:
                k.evacuated(pe, ("XP", lev - 1, t))
            heads_mm(nc, b, G.OT[:, t], G.X[:, t]).then_inc(full, 1)
        for t in range(NT):
            k.evacuated(pe, ("P", lev, t))
            if lev < LEVELS - 1:
                b, full = k.claim(pe, ("XP", lev, t))
                heads_mm(nc, b, G.XT[:, t], G.P[:, t]).then_inc(full, 1)
            b, full = k.claim(pe, ("PX", lev, t))
            heads_mm(nc, b, G.P[:, t], G.XT[:, t]).then_inc(full, 1)
    k.evacuated(pe, ("PX", LEVELS - 1, 0), ("PX", LEVELS - 1, 1))
    b, full = k.claim(pe, ("vn", 0))
    pe.wait_ge(k.sem("r_ready"), 1)
    heads_mm(nc, b, G.XT[:, 0], G.R[:, 0]).then_inc(full, 1)
    k.evacuated(pe, ("vn", 0))
    b, full = k.claim(pe, ("go", 0))
    heads_mm(nc, b, G.qk[:, 0], G.vn[:, 0]).then_inc(full, 1)
    b, full = k.claim(pe, ("S1",))
    k.evacuated(pe, ("kdec",))
    heads_mm(nc, b, G.kdec, G.vn[:, 0]).then_inc(full, 1)
    k.evacuated(pe, ("S1",))
    b, full = k.claim(pe, ("KS",))
    heads_mm(nc, b, G.cv[:, GH:2 * GH, P:2 * P], G.S1).then_inc(full, 1)
    b, full = k.claim(pe, ("QS",))
    heads_mm(nc, b, G.cv[:, 0:GH, P:2 * P], G.S1).then_inc(full, 1)
    b, full = k.claim(pe, ("vn", 1))
    pe.wait_ge(k.sem("r_ready"), 2)
    heads_mm(nc, b, G.XT[:, 1], G.R[:, 1]).then_inc(full, 1)
    k.evacuated(pe, ("vn", 1))
    b, full = k.claim(pe, ("go", 1))
    heads_mm(nc, b, G.qk[:, 1], G.vn[:, 1]).then_inc(full, 1)
    pe.wait_ge(k.sem("go_ready"), 1)
    for t in range(NT):
        b, full = k.claim(pe, ("goT", t))
        for h in range(GH):
            last = nc.tensor.transpose(b[:, h * P:(h + 1) * P], G.o[:, t, h, :], k.c("ident"))
        last.then_inc(full, 1)


def gdn_act(k, act):
    nc, G = k.nc, Gdn(k)
    act.wait_ge(k.sem("xa_ready"), 1)
    nc.scalar.activation(G.ex, G.nax, ACT.Exp).then_inc(k.act_step, 1)
    nc.scalar.activation(G.eal, k.lv("a_log"), ACT.Exp)
    act.wait_ge(k.act_step, 1)
    nc.scalar.activation(G.ln, G.ex, ACT.Ln, bias=1.0).then_inc(k.sem("softplus"), 1)
    nc.scalar.activation(G.beta, G.b_in, ACT.Sigmoid).then_inc(k.sem("beta_ready"), 1)
    for i in range(3):
        for pair in range(2):
            b, free = k.filled(act, ("raw", i, pair))
            nc.scalar.copy(G.raw[:, 4 * i + 2 * pair:4 * i + 2 * pair + 2, 3:3 + S], part(b, 2, S)).then_inc(free, 1)
    for t in range(NT):
        b, free = k.filled(act, ("z", t))
        nc.scalar.activation(G.z[:, t, :], b[:, :], ACT.Silu).then_inc(free, 1)
    for i in range(3):
        act.wait_ge(k.sem("conv_ready"), i + 1)
        cv = G.cv[:, 4 * i:4 * i + 4, :]
        nc.scalar.activation(cv, cv, ACT.Silu).then_inc(k.sem("conv_silu"), 1)
    for i in range(2):
        act.wait_ge(k.sem("l2_inverse"), 2 * i + 2)
        sq = G.sq[:, 4 * i:4 * i + 4, :]
        nc.scalar.activation(sq, sq, ACT.Sqrt).then_inc(k.sem("l2_rstd"), 1)
    for t in range(NT):
        b, free = k.filled(act, ("vT", t))
        nc.scalar.copy(G.v[:, t], part(b, GH, P)).then_inc(free, 1)
    act.wait_ge(k.sem("dk_in"), 1)
    nc.scalar.activation(G.dk, G.dk, ACT.Exp).then_inc(k.sem("eg_ready"), 1)
    nc.scalar.activation(G.eg, G.gsum, ACT.Exp).then_inc(k.sem("eg_ready"), 1)
    for t in range(NT):
        act.wait_ge(k.sem("decay_in"), t + 1)
        nc.scalar.activation(G.decay[:, t], G.decay[:, t], ACT.Exp).then_inc(k.sem("decay_ready"), 1)
    for lev in range(LEVELS):
        for t in range(NT):
            b, free = k.filled(act, ("P", lev, t))
            nc.scalar.copy(G.P[:, t], part(b, GH, P)).then_inc(free, 1)
    rstd_act(k, act, G.ostat, 5)
    for t in range(NT):
        b, free = k.filled(act, ("goT", t))
        nc.scalar.copy(k.s(BRANCH_T, 3, 4, S)[:, 1, :, t * P:(t + 1) * P], part(b, 4, P)).then_inc(free, 1)


def gdn_dve(k, dve, link):
    nc, G = k.nc, Gdn(k)
    V_ = nc.vector
    heads = lambda ap: bc(ap.unsqueeze(2), [P, GH, P])
    same = lambda name: bc(k.c(name).unsqueeze(1), [P, GH, P])
    link(V_.tensor_tensor(G.xa, G.a_in, bc(k.lv("dt").unsqueeze(1), [P, NT, GH]), ALU.add))
    V_.scalar_tensor_tensor(out=G.nax, in0=G.xa, scalar=-1.0, in1=G.xa, op0=ALU.mult, op1=ALU.min).then_inc(k.sem("xa_ready"), 1)
    V_.memset(G.raw[:, :, 0:3], 0.0)
    dve.wait_ge(k.sem("softplus"), 1)
    V_.tensor_scalar(G.eal, G.eal, -1.0, None, ALU.mult)
    link(V_.scalar_tensor_tensor(out=G.xa, in0=G.xa, scalar=0.0, in1=G.ln, op0=ALU.max, op1=ALU.add))
    V_.tensor_tensor(G.g, G.xa, bc(G.eal.unsqueeze(1), [P, NT, GH]), ALU.mult).then_inc(k.sem("g_ready"), 1)
    dve.wait_ge(k.sem("g_ready"), 1)
    for t in range(NT):
        ins = V_.tensor_tensor(G.gdiag[:, t], same("tri"), heads(G.g[:, t, :]), ALU.mult)
    ins.then_inc(k.sem("gdiag_ready"), 1)
    dve.wait_ge(k.sem("beta_ready"), 1)
    for t in range(NT):
        ins = V_.tensor_tensor(G.bdiag[:, t], same("ident"), heads(G.beta[:, t, :]), ALU.mult)
    ins.then_inc(k.sem("bdiag_ready"), 1)
    conv = k.lv("conv").rearrange("p (c j) -> p c j", j=4)
    for i in range(3):
        k.evacuated(dve, ("raw", i, 0), ("raw", i, 1))
        for j in range(4):
            for c in range(4 * i, 4 * i + 4):
                x, y, w = G.raw[:, c, j:j + S], G.cv[:, c, :], conv[:, c, j:j + 1]
                if j == 0:
                    ins = V_.tensor_scalar(y, x, w, None, ALU.mult)
                else:
                    ins = V_.scalar_tensor_tensor(out=y, in0=x, scalar=w, in1=y, op0=ALU.mult, op1=ALU.add)
            if j < 3:
                link(ins)
            else:
                ins.then_inc(k.sem("conv_ready"), 1)
    for i in range(2):
        dve.wait_ge(k.sem("conv_silu"), i + 1)
        cv = G.cv[:, 4 * i:4 * i + 4, :]
        V_.tensor_tensor(G.sq[:, 4 * i:4 * i + 4, :], cv, cv, ALU.mult).then_inc(k.sem("sq_ready"), 1)
    for b4 in range(4):
        b, free = k.filled(dve, ("l2", b4))
        V_.tensor_scalar(G.sq[:, 2 * b4:2 * b4 + 2, :], part(b, 2, S), EPS, None, ALU.add).then_inc(free, 1)
    for b4 in range(4):
        k.evacuated(dve, ("l2", b4))
        part_sq = G.sq[:, 2 * b4:2 * b4 + 2, :]
        V_.reciprocal(part_sq, part_sq).then_inc(k.sem("l2_inverse"), 1)
    dve.wait_ge(k.sem("l2_rstd"), 2)
    q, kk = G.cv[:, 0:GH, :], G.cv[:, GH:2 * GH, :]
    V_.scalar_tensor_tensor(out=q, in0=q, scalar=float(P) ** -0.5, in1=G.sq[:, 0:GH, :], op0=ALU.mult, op1=ALU.mult)
    V_.tensor_tensor(kk, kk, G.sq[:, GH:2 * GH, :], ALU.mult).then_inc(k.sem("l2_done"), 1)
    b, free = k.filled(dve, ("gc",))
    V_.tensor_copy(G.gsum_all, b[:, 0:12]).then_inc(free, 1)
    k.evacuated(dve, ("gc",))
    V_.tensor_tensor(G.dk, G.glast, G.gsum[:, 0, :], ALU.subtract).then_inc(k.sem("dk_in"), 1)
    for t in range(NT):
        b, free = k.filled(dve, ("gcB", t))
        V_.tensor_tensor(G.decay[:, t], part(b, GH, P), same("after_mask"), ALU.add).then_inc(free, 1)
        k.evacuated(dve, ("gcB", t))
        V_.tensor_tensor(G.decay[:, t], G.decay[:, t], heads(G.gsum[:, t, :]), ALU.subtract).then_inc(k.sem("decay_in"), 1)
    link(V_.tensor_copy(G.X[:, :].rearrange("p t h n -> p (t h) n"), bc(k.c("ident").unsqueeze(1), [P, 8, P])))
    link(V_.tensor_copy(G.XT[:, :].rearrange("p t h n -> p (t h) n"), bc(k.c("ident").unsqueeze(1), [P, 8, P])))
    for t in range(NT):
        dve.wait_ge(k.sem("decay_ready"), t + 1)
        b, free = k.filled(dve, ("KK", t))
        V_.tensor_tensor(G.m[:, t], part(b, GH, P), G.decay[:, t], ALU.mult).then_inc(free, 1)
        b, free = k.filled(dve, ("betaB", t))
        k.evacuated(dve, ("KK", t))
        V_.tensor_tensor(G.m[:, t], part(b, GH, P), G.m[:, t], ALU.mult).then_inc(free, 1)
        b, free = k.filled(dve, ("QK", t))
        V_.tensor_tensor(G.qk[:, t], part(b, GH, P), G.decay[:, t], ALU.mult).then_inc(free, 1)
    levels = k.c("levels").rearrange("p (l n) -> p l n", l=LEVELS)
    k.evacuated(dve, ("betaB", 0), ("betaB", 1))
    for lev in range(LEVELS):
        for t in range(NT):
            if lev:
                k.filled(dve, ("P", lev - 1, t))
            V_.tensor_tensor(G.OT[:, t], G.m[:, t], bc(levels[:, lev, :].unsqueeze(1), [P, GH, P]), ALU.mult)\
                .then_inc(k.sem("ot_ready"), 1)
        for t in range(NT):
            if lev < LEVELS - 1:
                b, free = k.filled(dve, ("XP", lev, t))
                V_.tensor_tensor(G.X[:, t], G.X[:, t], part(b, GH, P), ALU.subtract).then_inc(free, 1)
            b, free = k.filled(dve, ("PX", lev, t))
            V_.tensor_tensor(G.XT[:, t], G.XT[:, t], part(b, GH, P), ALU.subtract).then_inc(free, 1)
            if lev < LEVELS - 1:
                k.evacuated(dve, ("XP", lev, t))
            k.evacuated(dve, ("PX", lev, t))
    k.evacuated(dve, ("vT", 0), ("vT", 1))
    V_.tensor_tensor(G.R[:, 0], G.v[:, 0], heads(G.beta[:, 0, :]), ALU.mult).then_inc(k.sem("r_ready"), 1)
    dve.wait_ge(k.sem("eg_ready"), 2)
    b, free = k.filled(dve, ("kdec",))
    V_.tensor_tensor(G.kdec, part(b, GH, P), heads(G.dk), ALU.mult).then_inc(free, 1)
    b, free = k.filled(dve, ("vn", 0))
    V_.tensor_copy(G.vn[:, 0], part(b, GH, P)).then_inc(free, 1)
    b, free = k.filled(dve, ("go", 0))
    V_.tensor_copy(G.o[:, 0], part(b, GH, P)).then_inc(free, 1)
    b, free = k.filled(dve, ("S1",))
    V_.tensor_copy(G.S1, part(b, GH, P)).then_inc(free, 1)
    b, free = k.filled(dve, ("KS",))
    V_.tensor_tensor(G.tmp, part(b, GH, P), heads(G.eg[:, 1, :]), ALU.mult).then_inc(free, 1)
    k.evacuated(dve, ("KS",))
    link(V_.tensor_tensor(G.tmp, G.v[:, 1], G.tmp, ALU.subtract))
    V_.tensor_tensor(G.R[:, 1], G.tmp, heads(G.beta[:, 1, :]), ALU.mult).then_inc(k.sem("r_ready"), 1)
    b, free = k.filled(dve, ("QS",))
    dve.wait_ge(k.sem("r_ready"), 2)
    V_.tensor_tensor(G.tmp, part(b, GH, P), heads(G.eg[:, 1, :]), ALU.mult).then_inc(free, 1)
    b, free = k.filled(dve, ("vn", 1))
    V_.tensor_copy(G.vn[:, 1], part(b, GH, P)).then_inc(free, 1)
    k.evacuated(dve, ("QS",))
    b, free = k.filled(dve, ("go", 1))
    V_.tensor_tensor(G.o[:, 1], part(b, GH, P), G.tmp, ALU.add).then_inc(free, 1)
    k.evacuated(dve, ("go", 0), ("go", 1))
    o8, sq8 = (v.rearrange("p t h n -> p (t h) n") for v in (G.o, G.gdiag))
    link(V_.tensor_tensor(sq8, o8, o8, ALU.mult))
    link(V_.tensor_reduce(G.ostat, sq8, AX.X, ALU.add))
    rstd_dve(k, dve, link, G.ostat, 1.0 / P, 5)
    link(V_.tensor_tensor(o8, o8, bc(G.ostat.unsqueeze(2), [P, 8, P]), ALU.mult))
    link(V_.tensor_tensor(o8, o8, bc(k.lv("out_norm").unsqueeze(1), [P, 8, P]), ALU.mult))
    k.evacuated(dve, ("z", 0), ("z", 1))
    flat = k.h[:, 1, :]
    V_.tensor_tensor(flat, flat, k.h[:, 0, :], ALU.mult).then_inc(k.sem("go_ready"), 1)



F_MIX, F_POOLED, F_O, F_U, F_WPOOL = 0, 2048, 3072, 4096, 5120
F_POOLMAT, F_ONEHOT, F_LNC, F_REV, F_RELB = 13136, 15200, 15584, 15968, 16352
DIST = 384


def first_attn(k):
    return Attn(k, 0, FIRST_D, 5968, 12112, 13136, 5968, 9040, F_O, F_MIX + 4 * S)


def phase_first(k, dram):
    nc = k.nc
    uses = BankUses()
    norm_uses(uses, 0)
    uses.add(("dist",), 4)
    for i in range(4):
        for t in range(NT):
            uses.add(("rows", i, t), (4 + 2 * i + t) % 8)
    for g in range(4):
        uses.add(("pooled", g), g)
    for g in range(4):
        uses.add(("mixed", g), 4 + g)
    for i in range(4):
        uses.add(("flip", i), i)
    attn_uses(uses, 0)
    for v in range(2):
        for t in range(NT):
            uses.add(("wout", t, v), 2 + 2 * v + t)
    k.begin(uses)
    bias = k.h[:, :, :].rearrange("p t (a n) -> p (t a) n", n=2 * P)
    pooled, mixT = k.s(F_POOLED, 4, S), k.s(F_MIX, KC, S)
    poolmat, u_rows, w_pool = k.s(F_POOLMAT, 4, NT, S), k.s(F_U, NT, 4, P), k.s(F_WPOOL, 4, P)
    onehot, lnc, rev = (k.s(a, DIST) for a in (F_ONEHOT, F_LNC, F_REV))
    relb = k.s(F_RELB, H)
    a = first_attn(k)

    with nc.Block() as block:
        @block.sync
        def _(sp):
            sp.dma_start(k.x[:, :, :], dram["x"].rearrange("o (t p) d -> p (o t) d", p=P)).then_inc(k.sem("x_loaded"), 16)
            sp.dma_start(k.const[:, :], dram["const"]).then_inc(k.sem("const_loaded"), 16)
            sp.dma_start(k.fvec[:, :], dram["fvec"]).then_inc(k.sem("fvec_loaded"), 16)
            sp.dma_start(k.s(F_ONEHOT, 1, DIST)[0:32], dram["onehot"].unsqueeze(1))\
                .then_inc(k.sem("dist_in"), 16)
            sp.dma_start(lnc[0:H, :], dram["lnc"]).then_inc(k.sem("dist_in"), 16)
            sp.dma_start(relb[0:32, :], dram["rel_bias"]).then_inc(k.sem("dist_in"), 16)
            for u in range(2):
                sp.dma_start(k.ring[u][:, :], dram["first_units"][u]).then_inc(k.arrived[u], 16)
            sp.dma_start(k.scratch[:, F_POOLMAT:F_POOLMAT + POOL_WORDS], dram["poolmat"]).then_inc(k.sem("pool_in"), 16)
            sp.dma_start(w_pool, dram["w_pool"].rearrange("o g c d -> c (o g) d")).then_inc(k.sem("pool_in"), 16)
            for u in range(2, FIRST_UNITS):
                sp.dma_start(k.ring[u][:, :], dram["first_units"][u]).then_inc(k.arrived[u], 16)
            sp.wait_ge(k.sem("rev_ready"), 1)
            sp.dma_start(dram["rev"], rev[0:H, :]).then_inc(k.sem("rev_stored"), 16)
            sp.wait_ge(k.sem("rev_stored"), 16)
            hT_written(k, sp, 0)
            base = dram["rev"]
            for h in range(H):
                src = bass.AP(base.tensor, base.offset + h * DIST, [[1, P], [1, 2 * P]])
                sp.dma_start(bias[:, h, :], src).then_inc(k.sem("bias_loaded"), 16)

        @block.tensor
        def _(pe):
            pe.wait_ge(k.sem("const_loaded"), 16)
            norm_pe(k, pe, 0)
            b, full = k.claim(pe, ("dist",))
            pe.wait_ge(k.sem("dist_in"), 48)
            nc.tensor.matmul(b[0:H, 0:DIST], relb[0:32, :], onehot[0:32, :], start=True, stop=True).then_inc(full, 1)
            hT_written(k, pe, 0)
            for i in range(4):
                pe.wait_ge(k.arrived[i], 16)
                rows_pe(k, pe, ("rows", i), k.ring[i][:, :].rearrange("p (c n) -> p c n", c=KC), k.hT, 512)
            pe.wait_ge(k.sem("pool_in"), 32)
            k.evacuated(pe, ("rows", 3, 0), ("rows", 3, 1))
            for g in range(4):
                b, full = k.claim(pe, ("pooled", g))
                for t in range(NT):
                    last = nc.tensor.matmul(b[:, 0:S], u_rows[:, t, g, :], poolmat[:, g, t, :], start=(t == 0), stop=(t == 1))
                last.then_inc(full, 1)
            for g in range(4):
                b, full = k.claim(pe, ("mixed", g))
                k.evacuated(pe, ("pooled", g))
                nc.tensor.matmul(b[:, 0:S], w_pool[:, g, :], pooled[:, g, :], start=True, stop=True).then_inc(full, 1)
            pe.wait_ge(k.sem("bias_loaded"), 16 * H)
            for i in range(4):
                b, full = k.claim(pe, ("flip", i))
                nc.tensor.matmul(b[:, :], k.c("flip"), bias[:, 2 * i:2 * i + 2, :], start=True, stop=True).then_inc(full, 1)
            attn_pe(k, pe, a)
            k.evacuated(pe, ("oT", 0, 0), ("oT", 0, 1), *[("mixed", g) for g in range(4)])
            for v in range(2):
                pe.wait_ge(k.arrived[4 + v], 16)
                w = k.ring[4 + v][:, :].rearrange("p (c n) -> p c n", c=KC)
                for t in range(NT):
                    b, full = k.claim(pe, ("wout", t, v))
                    for c in range(KC):
                        last = nc.tensor.matmul(b[:, :], mixT[:, c, t * P:(t + 1) * P], w[:, c, :],
                                                start=(c == 0), stop=(c == KC - 1))
                    last.then_inc(full, 1)

        @block.scalar
        def _(act):
            norm_act(k, act, 0, (k.sem("x_loaded"), 16))
            for i in range(4):
                for t in range(NT):
                    b, free = k.filled(act, ("rows", i, t))
                    to = (a.qk[:, t * H:(t + 1) * H, :], a.qk[:, (NT + t) * H:(NT + t + 1) * H, :], a.v[:, t, :, :],
                          u_rows[:, t])[i]
                    nc.scalar.copy(to, part(b, *((4, P) if i == 3 else (H, 64)))).then_inc(free, 1)
            act.wait_ge(k.sem("rev_stored"), 16)
            attn_act(k, act, a)

        @block.vector
        def _(dve):
            link = chain_of(dve, k.dve_step)
            dve.wait_ge(k.sem("fvec_loaded"), 16)
            norm_dve(k, dve, link, 0, k.f("g_mix"))
            b, free = k.filled(dve, ("dist",))
            nc.vector.tensor_tensor(rev[0:H, :], b[0:H, 0:DIST], lnc[0:H, :], ALU.add).then_inc(free, 1)
            k.evacuated(dve, ("dist",))
            nc.vector.tensor_copy(k.s(STATS, 1), k.s(STATS, 1)).then_inc(k.sem("rev_ready"), 1)
            for g in range(4):
                b, free = k.filled(dve, ("pooled", g))
                nc.vector.tensor_copy(pooled[:, g, :], b[:, 0:S]).then_inc(free, 1)
            for g in range(4):
                b, free = k.filled(dve, ("mixed", g))
                nc.vector.tensor_scalar(mixT[:, g, :], b[:, 0:S], k.f("pool_scale")[:, g:g + 1], None, ALU.mult).then_inc(free, 1)
            k.evacuated(dve, *[("rows", i, t) for i in range(2) for t in range(NT)])
            nc.vector.memset(k.s(STATS + 4, 1), 0.0).then_inc(k.sem("qk_ready"), 1)
            for i in range(4):
                b, free = k.filled(dve, ("flip", i))
                nc.vector.tensor_copy(bias[:, 2 * i:2 * i + 2, :], part(b, 2, 2 * P)).then_inc(free, 1)
            k.evacuated(dve, *[("flip", i) for i in range(4)])
            attn_dve(k, dve, link, a, FIRST_D ** -0.5,
                     lambda t, pair: bias[:, 2 * pair:2 * pair + 2, (1 - t) * P:2 * P])
            for v in range(2):
                for t in range(NT):
                    b, free = k.filled(dve, ("wout", t, v))
                    x = k.x[:, t, v * 512:(v + 1) * 512]
                    nc.vector.tensor_tensor(x, b[:, :], x, ALU.add).then_inc(free, 1)
    k.end_phase()



M_XSEL, M_ACT, M_GU, M_SIG, M_Y, M_SEL, M_GSEL, M_GSELT = 0, 1024, 2048, 3072, 3584, 4608, 4864, 5120
M_RANK, M_GATE, M_BGU, M_BDOWN, M_ZERO, M_ROUTE = 5376, 5506, 5700, 6724, 7748, 7900
LIMIT, ALPHA = 7.0, 1.702
TURNS = 2 * E + 1
BIG = 1e30


def phase_moe(k, dram):
    nc = k.nc
    uses = BankUses()
    norm_uses(uses, 0)
    for t in range(NT):
        uses.add(("logits", t), t)
    for t in range(NT):
        uses.add(("rank", t), 2 + t)
    uses.add(("count",), 0)
    uses.add(("gateT",), 1)
    for t in range(NT):
        for v in range(2):
            uses.add(("acc", t, v), 4 + 2 * t + v)
    for half in range(2):
        uses.add(("gather", half), half)
    base = list(uses.count)
    turn = BankUses()
    for u in range(4):
        turn.add(("gu", u), u)
    for half in range(2):
        turn.add(("gather", half), half)
    turn.add(("selT",), 2)
    turn.add(("y", 0), 3)
    turn.add(("y", 1), 2)
    k.begin(uses)

    def turn_claim(pe, key, it):
        b, n = turn.at[key]
        pe.wait_ge(k.bank_free[b], it * turn.count[b] + (base[b] + n))
        return k.bank[b], k.bank_full[b]

    def turn_filled(eng, key, it):
        b, n = turn.at[key]
        eng.wait_ge(k.bank_full[b], it * turn.count[b] + (base[b] + n + 1))
        return k.bank[b], k.bank_free[b]

    def turn_evacuated(eng, key, it):
        b, n = turn.at[key]
        eng.wait_ge(k.bank_free[b], it * turn.count[b] + (base[b] + n + 1))

    xsel, acts, gu = k.s(M_XSEL, KC, P), k.s(M_ACT, KC, P), k.s(M_GU, 2, 4, P)
    sig, y, sel, gsel, gselT = k.s(M_SIG, 2, 2 * P), k.s(M_Y, 2, 512), k.s(M_SEL, NT, P), k.s(M_GSEL, NT, P), k.s(M_GSELT, NT, P)
    rank, gate, bgu = k.s(M_RANK, NT, TURNS), k.s(M_GATE, NT, TURNS), k.s(M_BGU, 2 * E, 16)
    b_down, zero = k.s(M_BDOWN, D), k.s(M_ZERO, P)
    small = lambda at, *shape: k.s(M_ROUTE + at, *shape)
    logits, left, eq, score, onehot, chosen, ex, raw = (small(64 * i, NT, E) for i in range(8))
    order, m, first, top, den = small(512, E), small(544, NT), small(546, NT), small(548, NT), small(550, NT)
    count, gateT = small(552, 1), small(560, NT, P)
    turns_i = small(553, 1).bitcast(I32)
    wide = lambda ap: bc(ap.unsqueeze(2), [P, NT, E])

    def turns_of(eng):
        eng.wait_ge(k.sem("turns_ready"), 1)
        return eng.value_load(turns_i[0:1, 0:1], min_val=E, max_val=2 * E)

    with nc.Block() as block:
        @block.sync
        def _(sp):
            sp.dma_start(bgu[:, 0:E, :], dram["b_gu"]).then_inc(k.sem("b_loaded"), 16)
            sp.dma_start(bgu[:, E:2 * E, :], dram["b_gu"]).then_inc(k.sem("b_loaded"), 16)
            sp.dma_start(b_down[0:E, :], dram["b_down"].rearrange("o e d -> (o e) d")).then_inc(k.sem("b_loaded"), 16)
            for u in range(EXPERT_UNITS):
                sp.dma_start(k.ring[u][:, :], dram["expert_units"][u]).then_inc(k.arrived[u], 16)
            turns = turns_of(sp)
            with sp.Fori(0, turns - 1) as it:
                for u in range(EXPERT_UNITS):
                    turn_filled(sp, ("gu", u) if u < 4 else ("y", u - 4), it)
                    sp.sem_inc(k.sem("unit_released"), 1)
                    nxt = ((it + 1) & (E - 1)) * EXPERT_UNITS + u
                    sp.dma_start(k.ring[u][:, :], dram["expert_units"][bass.ds(nxt, 1)].rearrange("o p n -> (o p) n"))\
                        .then_inc(k.arrived[u], 16)

        @block.tensor
        def _(pe):
            norm_pe(k, pe, 0)
            hT_written(k, pe, 0)
            w_router = k.f("w_router").rearrange("p (c e) -> p c e", c=KC)
            rows_pe(k, pe, ("logits",), w_router, k.hT, E)
            pe.wait_ge(k.sem("chosen_ready"), 1)
            for t in range(NT):
                b, full = k.claim(pe, ("rank", t))
                last = nc.tensor.matmul(b[:, 0:E], k.c("tri_strict"), chosen[:, t, :], start=True, stop=(t == 0))
                if t == 1:
                    last = nc.tensor.matmul(b[:, 0:E], k.c("ones"), chosen[:, 0, :], start=False, stop=True)
                last.then_inc(full, 1)
            b, full = k.claim(pe, ("count",))
            for t in range(NT):
                last = nc.tensor.matmul(b[:, 0:E], k.c("ones"), chosen[:, t, :], start=(t == 0), stop=(t == 1))
            last.then_inc(full, 1)
            b, full = k.claim(pe, ("gateT",))
            pe.wait_ge(k.sem("gate_ready"), 1)
            for t in range(NT):
                last = nc.tensor.transpose(b[0:E, t * P:(t + 1) * P], gate[:, t, 0:E], k.c("ident"))
            last.then_inc(full, 1)
            pe.wait_ge(k.sem("b_loaded"), 48)
            k.evacuated(pe, ("gateT",))
            for t in range(NT):
                for v in range(2):
                    b, full = k.claim(pe, ("acc", t, v))
                    nc.tensor.matmul(b[:, :], gateT[0:E, t, :], b_down[0:E, v * 512:(v + 1) * 512], start=True, stop=False)

            def gather(banks):
                for half, (b, full) in enumerate(banks):
                    for j in range(4):
                        c = 4 * half + j
                        for t in range(NT):
                            last = nc.tensor.matmul(b[:, j * P:(j + 1) * P], k.h[:, t, c * P:(c + 1) * P], sel[:, t, :],
                                                    start=(t == 0), stop=(t == 1))
                    last.then_inc(full, 1)

            pe.wait_ge(k.sem("sel_ready"), 1)
            gather([k.claim(pe, ("gather", half)) for half in range(2)])
            turns = turns_of(pe)
            with pe.Fori(0, turns) as it:
                for half in range(2):
                    pe.wait_ge(k.bank_free[half], it * turn.count[half] + base[half])
                for u in range(4):
                    pe.wait_ge(k.arrived[u], (it + 2) * 16)
                    w = k.ring[u][:, :].rearrange("p (c g n) -> p c g n", c=KC, g=2)
                    b, full = turn_claim(pe, ("gu", u), it)
                    for g in range(2):
                        for j in range(2):
                            for c in range(KC):
                                last = nc.tensor.matmul(b[:, (2 * g + j) * P:(2 * g + j + 1) * P],
                                                        w[:, c, g, j * P:(j + 1) * P], xsel[:, c, :],
                                                        start=(c == 0), stop=(c == KC - 1))
                    last.then_inc(full, 1)
                pe.wait_ge(k.sem("sel_ready"), it + 2)
                gather([turn_claim(pe, ("gather", half), it) for half in range(2)])
                pe.wait_ge(k.sem("gsel_ready"), it + 1)
                b, full = turn_claim(pe, ("selT",), it)
                for t in range(NT):
                    last = nc.tensor.transpose(b[:, t * P:(t + 1) * P], gsel[:, t, :], k.c("ident"))
                last.then_inc(full, 1)
                for v in range(2):
                    pe.wait_ge(k.arrived[4 + v], (it + 2) * 16)
                    w = k.ring[4 + v][:, :].rearrange("p (c n) -> p c n", c=KC)
                    b, full = turn_claim(pe, ("y", v), it)
                    for c in range(KC):
                        if v == 0 and c % 2 == 0:
                            pe.wait_ge(k.sem("act_ready"), it * 4 + (c // 2 + 1))
                        last = nc.tensor.matmul(b[:, :], acts[:, c, :], w[:, c, :], start=(c == 0), stop=(c == KC - 1))
                    last.then_inc(full, 1)
                turn_evacuated(pe, ("selT",), it)
                for v in range(2):
                    turn_evacuated(pe, ("y", v), it)
                    for t in range(NT):
                        nc.tensor.matmul(k.bank[4 + 2 * t + v][:, :], gselT[:, t, :], y[:, v, :], start=False, stop=False)
            pe.wait_ge(k.sem("zero_ready"), 1)
            for t in range(NT):
                for v in range(2):
                    nc.tensor.matmul(k.bank[4 + 2 * t + v][:, :], zero, y[:, v, :], start=False, stop=True)\
                        .then_inc(k.bank_full[4 + 2 * t + v], 1)

        @block.scalar
        def _(act):
            norm_act(k, act, 0)
            act.wait_ge(k.sem("centred"), 1)
            nc.scalar.activation(ex, ex, ACT.Exp).then_inc(k.sem("exp_ready"), 1)
            b, free = k.filled(act, ("gateT",))
            nc.scalar.copy(gateT[0:E], part(b, NT, P)[0:E]).then_inc(free, 1)
            turns = turns_of(act)
            with act.Fori(0, turns) as it:
                for u in range(4):
                    turn_evacuated(act, ("gu", u), it)
                    nc.scalar.activation(sig[:, u % 2, :], gu[:, u % 2, 0:2, :], ACT.Sigmoid, scale=ALPHA)\
                        .then_inc(k.sem("sig_ready"), 1)
                b, free = turn_filled(act, ("selT",), it)
                nc.scalar.copy(gselT, part(b, NT, P)).then_inc(free, 1)
                for v in range(2):
                    b, free = turn_filled(act, ("y", v), it)
                    nc.scalar.copy(y[:, v, :], b[:, :]).then_inc(free, 1)

        @block.vector
        def _(dve):
            V_ = nc.vector
            link = chain_of(dve, k.dve_step)
            gain = k.f("g_ffn")
            norm_dve(k, dve, link, 0, gain)
            V_.memset(zero, 0.0).then_inc(k.sem("zero_ready"), 1)
            V_.memset(rank[:, :, 2 * E:], -1000.0)
            V_.memset(gate[:, :, 2 * E:], 0.0)
            V_.memset(chosen, 0.0)
            V_.tensor_scalar(order, k.c("iota")[:, 0:E], -1.0, float(E), ALU.mult, ALU.add)
            for t in range(NT):
                b, free = k.filled(dve, ("logits", t))
                V_.tensor_tensor(logits[:, t, :], b[:, 0:E], k.f("b_router"), ALU.add).then_inc(free, 1)
            k.evacuated(dve, ("logits", 0), ("logits", 1))
            link(V_.tensor_copy(left, logits))
            for r in range(TOPK):
                m_r = top if r == 0 else m
                link(V_.tensor_reduce(m_r, left, AX.X, ALU.max))
                link(V_.tensor_tensor(eq, left, wide(m_r), ALU.is_equal))
                link(V_.tensor_tensor(score, eq, bc(order.unsqueeze(1), [P, NT, E]), ALU.mult))
                link(V_.tensor_reduce(first, score, AX.X, ALU.max))
                link(V_.tensor_tensor(onehot, score, wide(first), ALU.is_equal))
                link(V_.scalar_tensor_tensor(out=left, in0=onehot, scalar=-BIG, in1=left, op0=ALU.mult, op1=ALU.add))
                ins = V_.tensor_tensor(chosen, chosen, onehot, ALU.add)
                if r < TOPK - 1:
                    link(ins)
                else:
                    ins.then_inc(k.sem("chosen_ready"), 1)
            V_.tensor_tensor(ex, logits, wide(top), ALU.subtract).then_inc(k.sem("centred"), 1)
            dve.wait_ge(k.sem("exp_ready"), 1)
            link(V_.tensor_tensor(ex, ex, chosen, ALU.mult))
            link(V_.tensor_reduce(den, ex, AX.X, ALU.add))
            link(V_.reciprocal(den, den))
            V_.tensor_tensor(gate[:, :, 0:E], ex, wide(den), ALU.mult)
            V_.tensor_tensor(gate[:, :, E:2 * E], ex, wide(den), ALU.mult).then_inc(k.sem("gate_ready"), 1)
            for t in range(NT):
                b, free = k.filled(dve, ("rank", t))
                V_.scalar_tensor_tensor(out=raw[:, t, :], in0=b[:, 0:E], scalar=1000.0, in1=chosen[:, t, :],
                                        op0=ALU.add, op1=ALU.mult).then_inc(free, 1)
            k.evacuated(dve, ("rank", 0), ("rank", 1))
            V_.tensor_scalar(rank[:, :, 0:E], raw, -1000.0, None, ALU.add)
            link(V_.tensor_scalar(rank[:, :, E:2 * E], raw, -1000.0 - P, None, ALU.add))
            b, free = k.filled(dve, ("count",))
            V_.tensor_reduce(count, b[:, 0:E], AX.X, ALU.max).then_inc(free, 1)
            k.evacuated(dve, ("count",))
            link(V_.tensor_scalar(count, count, float(P), float(E), ALU.is_gt, ALU.mult))
            V_.tensor_scalar(turns_i, count, float(E), None, ALU.add).then_inc(k.sem("turns_ready"), 1)
            dve.wait_ge(k.sem("gate_ready"), 1)

            def select(out, col, gated, done):
                for t in range(NT):
                    g = gate[:, t, col] if gated else None
                    ins = V_.tensor_scalar(out[:, t, :], k.c("iota"), rank[:, t, col], g, ALU.is_equal,
                                           *((ALU.mult,) if gated else ()))
                ins.then_inc(k.sem(done), 1)

            def take(half, b, free):
                V_.tensor_tensor(xsel[:, 4 * half:4 * half + 4, :], part(b, 4, P),
                                 bc(gain[:, 4 * half:4 * half + 4].unsqueeze(2), [P, 4, P]), ALU.mult).then_inc(free, 1)

            select(sel, slice(0, 1), False, "sel_ready")
            for half in range(2):
                take(half, *k.filled(dve, ("gather", half)))
            dve.wait_ge(k.sem("b_loaded"), 48)
            turns = turns_of(dve)
            with dve.Fori(0, turns) as it:
                b, n = turn.at[("selT",)]
                dve.wait_ge(k.bank_full[b], it * turn.count[b] + (base[b] + n + 1 - turn.count[b]))
                select(gsel, bass.ds(it, 1), True, "gsel_ready")
                select(sel, bass.ds(it + 1, 1), False, "sel_ready")

                def evac(u):
                    b, free = turn_filled(dve, ("gu", u), it)
                    for g in range(2):
                        for j in range(2):
                            c = 8 * g + 2 * u + j
                            ins = V_.tensor_scalar(gu[:, u % 2, 2 * g + j, :], b[:, (2 * g + j) * P:(2 * g + j + 1) * P],
                                                   bgu[:, bass.ds(it, 1), c:c + 1].rearrange("p a b -> p (a b)"), LIMIT, ALU.add, ALU.min)
                    ins.then_inc(free, 1)

                evac(0)
                for u in range(4):
                    if u > 0:
                        dve.wait_ge(k.sem("act_ready"), it * 4 + u)
                    if u < 3:
                        evac(u + 1)
                    turn_evacuated(dve, ("gu", u), it)
                    g, up = gu[:, u % 2, 0:2, :], gu[:, u % 2, 2:4, :]
                    V_.tensor_scalar(up, up, -LIMIT, 1.0, ALU.max, ALU.add).then_inc(k.sem("up_step"), 1)
                    dve.wait_ge(k.sem("up_step"), it * 8 + (2 * u + 1))
                    V_.tensor_tensor(up, up, g, ALU.mult).then_inc(k.sem("up_step"), 1)
                    dve.wait_ge(k.sem("up_step"), it * 8 + (2 * u + 2))
                    dve.wait_ge(k.sem("sig_ready"), it * 4 + (u + 1))
                    V_.tensor_tensor(acts[:, 2 * u:2 * u + 2, :], up, sig[:, u % 2, :].rearrange("p (a b) -> p a b", a=2),
                                     ALU.mult).then_inc(k.sem("act_ready"), 1)
                dve.wait_ge(k.sem("act_ready"), it * 4 + 4)
                for half in range(2):
                    take(half, *turn_filled(dve, ("gather", half), it))
            for t in range(NT):
                for v in range(2):
                    b, free = k.filled(dve, ("acc", t, v))
                    x = k.x[:, t, v * 512:(v + 1) * 512]
                    V_.tensor_tensor(x, b[:, :], x, ALU.add).then_inc(free, 1)
    k.end_phase()



def phase_ple(k, dram):
    nc = k.nc
    uses = BankUses()
    norm_uses(uses, 0)
    for v in range(2):
        for t in range(NT):
            uses.add(("pgate", v, t), 2 * v + t)
    for v in range(2):
        for t in range(NT):
            uses.add(("proj", v, t), 4 + 2 * v + t)
    k.begin(uses)
    sg, tmp, pT, g_final = k.s(0, NT, D), k.s(2048, 4, 512), k.s(4096, 2, S), k.s(4608, D)

    with nc.Block() as block:
        @block.sync
        def _(sp):
            for u in range(PLE_UNITS):
                w = PLE_WORDS[u]
                sp.dma_start(k.ring[u][:, 0:w], dram["ple_units"][u, :, 0:w]).then_inc(k.later_arrived[u], 16)
            sp.dma_start(pT, dram["pT"].rearrange("(c p) n -> p c n", p=P)).then_inc(k.sem("p_loaded"), 16)
            sp.dma_start(g_final, dram["g_final"]).then_inc(k.sem("p_loaded"), 16)

        @block.tensor
        def _(pe):
            norm_pe(k, pe, 0)
            hT_written(k, pe, 0)
            for v in range(2):
                pe.wait_ge(k.later_arrived[v], 16)
                rows_pe(k, pe, ("pgate", v), k.ring[v][:, :].rearrange("p (c n) -> p c n", c=KC), k.hT, 512)
            pe.wait_ge(k.later_arrived[2], 16)
            pe.wait_ge(k.sem("p_loaded"), 32)
            w = k.ring[2][:, 0:PLE_WORDS[2]].rearrange("p (c n) -> p c n", c=2)
            for v in range(2):
                rows_pe(k, pe, ("proj", v), w[:, :, v * 512:(v + 1) * 512], pT, 512, chunks=2)

        @block.scalar
        def _(act):
            norm_act(k, act, 0)
            for v in range(2):
                for t in range(NT):
                    b, free = k.filled(act, ("pgate", v, t))
                    nc.scalar.activation(sg[:, t, v * 512:(v + 1) * 512], b[:, :], ACT.Sigmoid).then_inc(free, 1)
            for t in range(NT):
                act.wait_ge(k.sem("x_updated"), NT * 2)
                nc.scalar.activation(k.h[:, t, :], k.x[:, t, :], ACT.Square, accum_out=k.s(STATS + 8 + t, 1))\
                    .then_inc(k.sem("last_ss"), 1)
            rstd_act(k, act, k.s(STATS + 8, NT), 1)

        @block.vector
        def _(dve):
            link = chain_of(dve, k.dve_step)
            norm_dve(k, dve, link, 0, k.f("g_ple"))
            for v in range(2):
                for t in range(NT):
                    b, free = k.filled(dve, ("proj", v, t))
                    k.evacuated(dve, ("pgate", v, t))
                    s = tmp[:, 2 * v + t, :]
                    nc.vector.tensor_tensor(s, b[:, :], sg[:, t, v * 512:(v + 1) * 512], ALU.mult).then_inc(free, 1)
                    k.evacuated(dve, ("proj", v, t))
                    x = k.x[:, t, v * 512:(v + 1) * 512]
                    nc.vector.tensor_tensor(x, x, s, ALU.add).then_inc(k.sem("x_updated"), 1)
            dve.wait_ge(k.sem("last_ss"), 2)
            st = k.s(STATS + 8, NT)
            rstd_dve(k, dve, link, st, 1.0 / D, 1)
            for t in range(NT):
                nc.vector.scalar_tensor_tensor(out=k.x[:, t, :], in0=k.x[:, t, :], scalar=st[:, t:t + 1], in1=g_final,
                                               op0=ALU.mult, op1=ALU.mult)
    k.end_phase()



def layer_uses():
    uses = BankUses()
    norm_uses(uses, 0)
    ffn_uses(uses, 0)
    norm_uses(uses, 1)
    for t in range(NT):
        uses.add(("mla", t), 4 + t)
    for t in range(NT):
        uses.add(("cT", t), 6 + t)
    for t in range(NT):
        for i in range(2):
            uses.add(("q", t, i), 4 * t + i)
        for i in range(2):
            uses.add(("kv", t, i), 4 * t + 2 + i)
    attn_uses(uses, 0)
    for i in range(3):
        for t in range(NT):
            uses.add(("moba", i, t), 2 + 2 * i + t - (0 if i < 3 else 8))
    attn_uses(uses, 1)
    gdn_uses(uses)
    for i in range(6):
        for pair in range(2):
            uses.add(("gates", i, pair), (2 * i + pair) % 4)
    for n in range(3):
        for dp in range(4):
            uses.add(("branch", n, dp), 4 + dp)
    for v in range(2):
        for t in range(NT):
            uses.add(("wout", t, v), 2 * v + t)
    norm_uses(uses, 2, (4, 5, 6, 7))
    ffn_uses(uses, 1)
    return uses


def layer_attn(k, n):
    return (Attn(k, 0, MLA_D, WORK, 12112, 13136, WORK, 9040, COMB, BRANCH_T),
            Attn(k, 1, MOBA_D, WORK, 12112, 13136, WORK, 9040, COMB, BRANCH_T + 2 * 4 * S))[n]


def layer_unit_read(k, u):
    def full(*key):
        b, n = k.uses.at[key]
        return k.bank_full[b], n + 1
    for n, (i0, o0) in enumerate(((U_FFA_IN, U_FFA_OUT), (U_FFB_IN, U_FFB_OUT))):
        if i0 <= u < i0 + FFN_IN_UNITS:
            return full("up", n, u - i0)
        if o0 <= u < o0 + FFN_OUT_UNITS - 1:
            return k.sem("out_unit_used"), (FFN_OUT_UNITS - 1) * n + u - o0 + 1
        if u == o0 + FFN_OUT_UNITS - 1:
            return full("ffn_out", n, 1, 1)
    if u >= U_WOUT:
        return full("wout", 1, u - U_WOUT)
    if u >= U_BRANCH:
        return full("branch", u - U_BRANCH, 3)
    if u >= U_GATES:
        return full("gates", u - U_GATES, 1)
    if u >= U_GDN:
        return full("raw", u - U_GDN, 1) if u < U_Z else full("z", 1)
    if u >= U_MOBA:
        return full("moba", u - U_MOBA, 1)
    return full("mla", 1) if u == U_MLA else full("kv", 1, 1)


def layer_body(k, dram, layer):
    nc = k.nc
    k.begin(layer_uses())
    rows = k.s(MLA_ROWS, NT, MLA_COLS)
    cn, cT = k.s(COMB, NT, 384), k.s(COMB + 768, 3, S)
    gatesT, comb, btmp = k.s(WORK, 24, S), k.s(COMB, KC, S), k.s(12148, 4, 2, S)
    branchT = k.s(BRANCH_T, 3, 4, S)
    mla, moba = layer_attn(k, 0), layer_attn(k, 1)
    causal = k.c("causal")

    def unit(pe, u):
        pe.wait_ge(k.later_arrived[u % SLOTS], 16 * (u // SLOTS + 1))
        return k.ring[u % SLOTS][:, :]

    with nc.Block() as block:
        @block.sync
        def _(sp):
            sp.dma_start(k.lvec[:, :], dram["lvec"][bass.ds(layer, 1)].rearrange("o p n -> (o p) n")).then_inc(k.sem("lvec_loaded"), 16)
            for u in range(LAYER_UNITS):
                if u >= SLOTS:
                    sp.wait_ge(*layer_unit_read(k, u - SLOTS))
                w = LAYER_WORDS[u]
                sp.dma_start(k.ring[u % SLOTS][:, 0:w],
                             dram["layer_units"][bass.ds(layer * LAYER_UNITS + u, 1), :, 0:w].rearrange("o p n -> (o p) n"))\
                    .then_inc(k.later_arrived[u % SLOTS], 16)

        @block.tensor
        def _(pe):
            norm_pe(k, pe, 0)
            ffn_pe(k, pe, 0, U_FFA_IN, U_FFA_OUT, unit)
            norm_pe(k, pe, 1)
            hT_written(k, pe, 1)
            w = unit(pe, U_MLA)[:, 0:KC * MLA_COLS].rearrange("p (c n) -> p c n", c=KC)
            rows_pe(k, pe, ("mla",), w, k.hT, MLA_COLS)
            pe.wait_ge(k.sem("c_ready"), 1)
            for t in range(NT):
                b, full = k.claim(pe, ("cT", t))
                for c in range(3):
                    last = nc.tensor.transpose(b[:, c * P:(c + 1) * P], cn[:, t, c * P:(c + 1) * P], k.c("ident"))
                last.then_inc(full, 1)
            w = unit(pe, U_MLA_UP)
            k.evacuated(pe, ("cT", 0), ("cT", 1))
            for t in range(NT):
                for i in range(2):
                    b, full = k.claim(pe, ("q", t, i))
                    for c in range(2):
                        last = nc.tensor.matmul(b[:, 0:384], cT[:, c, t * P:(t + 1) * P],
                                                w[:, c * 768 + i * 384:c * 768 + (i + 1) * 384], start=(c == 0), stop=(c == 1))
                    last.then_inc(full, 1)
                for i in range(2):
                    b, full = k.claim(pe, ("kv", t, i))
                    nc.tensor.matmul(b[:, :], cT[:, 2, t * P:(t + 1) * P], w[:, 1536 + 512 * i:2048 + 512 * i],
                                     start=True, stop=True).then_inc(full, 1)
            attn_pe(k, pe, mla)
            for i in range(3):
                rows_pe(k, pe, ("moba", i), unit(pe, U_MOBA + i).rearrange("p (c n) -> p c n", c=KC), k.hT, 512)
            attn_pe(k, pe, moba)
            gdn_pe(k, pe, unit)
            for i in range(6):
                w = unit(pe, U_GATES + i).rearrange("p (c n) -> p c n", c=KC)
                for pair in range(2):
                    b, full = k.claim(pe, ("gates", i, pair))
                    for j in range(2):
                        for c in range(KC):
                            col = (2 * pair + j) * P
                            last = nc.tensor.matmul(b[:, j * S:(j + 1) * S], w[:, c, col:col + P], k.hT[:, c, :],
                                                    start=(c == 0), stop=(c == KC - 1))
                    last.then_inc(full, 1)
            k.evacuated(pe, ("goT", 0), ("goT", 1), *[("oT", n, t) for n in range(2) for t in range(NT)])
            for n in range(3):
                w = unit(pe, U_BRANCH + n).rearrange("p (c n) -> p c n", c=4)
                for dp in range(4):
                    b, full = k.claim(pe, ("branch", n, dp))
                    for j in range(2):
                        for c in range(4):
                            col = (2 * dp + j) * P
                            last = nc.tensor.matmul(b[:, j * S:(j + 1) * S], w[:, c, col:col + P], branchT[:, n, c, :],
                                                    start=(c == 0), stop=(c == 3))
                    last.then_inc(full, 1)
            pe.wait_ge(k.sem("comb_ready"), 4)
            for v in range(2):
                w = unit(pe, U_WOUT + v).rearrange("p (c n) -> p c n", c=KC)
                for t in range(NT):
                    b, full = k.claim(pe, ("wout", t, v))
                    for c in range(KC):
                        last = nc.tensor.matmul(b[:, :], comb[:, c, t * P:(t + 1) * P], w[:, c, :],
                                                start=(c == 0), stop=(c == KC - 1))
                    last.then_inc(full, 1)
            norm_pe(k, pe, 2)
            ffn_pe(k, pe, 1, U_FFB_IN, U_FFB_OUT, unit)

        @block.scalar
        def _(act):
            act.wait_ge(k.sem("lvec_loaded"), 16)
            norm_act(k, act, 0)
            ffn_act(k, act, 0)
            k.evacuated(act, *[("ffn_out", 0, t, v) for t in range(NT) for v in range(2)])
            norm_act(k, act, 1, power=1)
            for t in range(NT):
                b, free = k.filled(act, ("mla", t))
                nc.scalar.copy(rows[:, t, :], b[:, 0:MLA_COLS]).then_inc(free, 1)
            rstd_act(k, act, k.s(STATS + 192, 2, NT), 2)
            for t in range(NT):
                for i in range(2):
                    b, free = k.filled(act, ("q", t, i))
                    nc.scalar.copy(mla.qk[:, t * H + 4 * i:t * H + 4 * i + 4, :], part(b, 4, MLA_D)).then_inc(free, 1)
                for i in range(2):
                    b, free = k.filled(act, ("kv", t, i))
                    r = (NT + t) * H + 4 * i
                    nc.scalar.copy(mla.qk[:, r:r + 4, 0:64], part(b, 4, P)[:, :, 0:64])
                    nc.scalar.copy(mla.v[:, t, 4 * i:4 * i + 4, :], part(b, 4, P)[:, :, 64:P]).then_inc(free, 1)
            rstd_act(k, act, k.s(STATS + 128, 2 * NT * H), 3)
            attn_act(k, act, mla)
            for i in range(3):
                for t in range(NT):
                    b, free = k.filled(act, ("moba", i, t))
                    to = moba.v[:, t] if i == 2 else moba.qk[:, (i * NT + t) * H:(i * NT + t + 1) * H, :]
                    nc.scalar.copy(to, part(b, H, 64)).then_inc(free, 1)
            rstd_act(k, act, k.s(STATS + 128, 2 * NT * H), 4)
            attn_act(k, act, moba)
            gdn_act(k, act)
            for i in range(6):
                for pair in range(2):
                    b, free = k.filled(act, ("gates", i, pair))
                    c = 4 * i + 2 * pair
                    nc.scalar.activation(gatesT[:, c:c + 2, :], part(b, 2, S), ACT.Sigmoid).then_inc(free, 1)
            k.evacuated(act, *[("wout", t, v) for t in range(NT) for v in range(2)])
            norm_act(k, act, 2, power=6)
            ffn_act(k, act, 1)

        @block.vector
        def _(dve):
            V_ = nc.vector
            link = chain_of(dve, k.dve_step)
            dve.wait_ge(k.sem("lvec_loaded"), 16)
            norm_dve(k, dve, link, 0, k.lv("g_ffa"))
            ffn_dve(k, dve, 0, None)
            norm_dve(k, dve, link, 1, k.lv("g_mix"), 1)
            k.evacuated(dve, ("mla", 0), ("mla", 1))
            sq, st = k.s(9040, NT, 384), k.s(STATS + 192, 2, NT)
            lat = rows[:, :, 0:384]
            link(V_.tensor_tensor(sq, lat, lat, ALU.mult))
            V_.tensor_reduce(st[:, 0, :], sq[:, :, 0:256], AX.X, ALU.add)
            link(V_.tensor_reduce(st[:, 1, :], sq[:, :, 256:384], AX.X, ALU.add))
            link(V_.tensor_scalar(st[:, 1, :], st[:, 1, :], 2.0, None, ALU.mult))
            rstd_dve(k, dve, link, st, 1.0 / 256, 2)
            for t in range(NT):
                for i, (c0, c1) in enumerate(((0, 256), (256, 384))):
                    ins = V_.tensor_scalar(cn[:, t, c0:c1], rows[:, t, c0:c1], st[:, i, t:t + 1], None, ALU.mult)
            ins.then_inc(k.sem("c_ready"), 1)
            for t in range(NT):
                b, free = k.filled(dve, ("cT", t))
                V_.tensor_tensor(cT[:, :, t * P:(t + 1) * P], part(b, 3, P), bc(k.lv("c_norm").unsqueeze(2), [P, 3, P]),
                                 ALU.mult).then_inc(free, 1)
            for t in range(NT):
                r = (NT + t) * H
                V_.tensor_copy(mla.qk[:, r:r + H, 64:96], bc(rows[:, t, 384:416].unsqueeze(1), [P, H, 32]))\
                    .then_inc(k.sem("k_rope"), 1)
            dve.wait_ge(k.sem("k_rope"), 2)
            k.evacuated(dve, *[(x, t, i) for t in range(NT) for x in ("q", "kv") for i in range(2)])
            head_norm_dve(k, dve, link, mla.qk, k.s(9040, 32, MLA_D), MLA_D, (k.lv("q_norm"), k.lv("k_norm")), 3)
            rope_dve(k, dve, link, mla.qk, 9040, 64, 16, k.c("cos16"), k.c("sin16"), k.sem("qk_ready"))
            mask = lambda t, pair: bc(causal[:, (1 - t) * P:2 * P].unsqueeze(1), [P, 2, (t + 1) * P])
            attn_dve(k, dve, link, mla, MLA_D ** -0.5, mask)
            k.evacuated(dve, *[("moba", i, t) for i in range(3) for t in range(NT)])
            head_norm_dve(k, dve, link, moba.qk, k.s(9040, 32, MOBA_D), MOBA_D, (k.lv("moba_q"), k.lv("moba_k")), 4)
            rope_dve(k, dve, link, moba.qk, 9040, 0, 32, k.c("cos32"), k.c("sin32"), k.sem("qk_ready"))
            attn_dve(k, dve, link, moba, MOBA_D ** -0.5, mask)
            gdn_dve(k, dve, link)
            for n in range(3):
                for dp in range(4):
                    b, free = k.filled(dve, ("branch", n, dp))
                    if n == 0 and dp == 0:
                        k.evacuated(dve, *[("gates", i, pair) for i in range(6) for pair in range(2)])
                    g = gatesT[:, 8 * n + 2 * dp:8 * n + 2 * dp + 2, :]
                    c = comb[:, 2 * dp:2 * dp + 2, :]
                    if n == 0:
                        V_.tensor_tensor(c, part(b, 2, S), g, ALU.mult).then_inc(free, 1)
                        continue
                    V_.tensor_tensor(btmp[:, dp], part(b, 2, S), g, ALU.mult).then_inc(free, 1)
                    k.evacuated(dve, ("branch", n, dp))
                    ins = V_.tensor_tensor(c, c, btmp[:, dp], ALU.add)
                    if n == 1:
                        link(ins)
                    else:
                        ins.then_inc(k.sem("comb_ready"), 1)
            for v in range(2):
                for t in range(NT):
                    b, free = k.filled(dve, ("wout", t, v))
                    x = k.x[:, t, v * 512:(v + 1) * 512]
                    V_.tensor_tensor(x, b[:, :], x, ALU.add).then_inc(free, 1)
            norm_dve(k, dve, link, 2, k.lv("g_ffb"), 6)
            ffn_dve(k, dve, 1, None)
    k.end_phase()


def build(nc, dram, last="all"):
    with ExitStack() as ctx:
        k = Core(nc, ctx)
        phase_first(k, dram)
        if last != "first":
            phase_moe(k, dram)
        if last not in ("first", "moe"):
            phase_ple(k, dram)
        if last not in ("first", "moe", "ple"):
            with nc.Fori(0, LAYERS if last == "all" else 1) as layer:
                layer_body(k, dram, layer)
        with nc.Block() as block:
            @block.sync
            def _(sp):
                sp.dma_start(dram["out"].rearrange("o (t p) d -> p (o t) d", p=P), k.x[:, :, :]).then_inc(k.stored, 16)
                sp.wait_ge(k.stored, 16)



def bucket(dist):
    n = np.maximum(dist, 1).astype(np.float32)
    large = 16 + (np.log(n / np.float32(16)) / np.float32(np.log(2048 / 16)) * np.float32(16)).astype(np.int32)
    return np.where(dist < 16, dist, np.minimum(large, 31))


def constants():
    p, n = np.arange(P)[:, None], np.arange(P)[None, :]
    c = {"ident": p == n, "flip": p + n == P - 1, "ones": np.ones((P, P)), "tri": n >= p, "tri_strict": n > p,
         "after_mask": np.where(n >= p, 0.0, NEG), "iota": n + 0 * p,
         "causal": np.where(np.arange(2 * P)[None, :] <= p + P, 0.0, NEG)}
    levels = []
    for lev in range(LEVELS):
        b = 1 << lev
        levels.append((n // (2 * b) == p // (2 * b)) & (n % (2 * b) >= b) & (p % (2 * b) < b))
    c["levels"] = np.concatenate(levels, axis=1)
    for half in (16, 32):
        freq = np.float32(10000.0) ** (-np.arange(half, dtype=np.float32) * np.float32(2.0) / np.float32(2 * half))
        ang = np.arange(S, dtype=np.float32)[:, None] * freq[None, :].astype(np.float32)
        for name, f in (("cos", np.cos), ("sin", np.sin)):
            c[f"{name}{half}"] = f(ang.astype(np.float64)).reshape(NT, P, half).transpose(1, 0, 2).reshape(P, NT * half)
    const = np.zeros((P, CONST["all"][1]), np.float32)
    for name, a in c.items():
        const[:, CONST[name][0]:CONST[name][1]] = a
    t = np.arange(S)
    pool = np.zeros((4, S, S), np.float32)
    for g, w in enumerate((2, 4, 8, 16)):
        d = t[None, :] - t[:, None]
        pool[g] = ((d >= 0) & (d < w)) / np.minimum(t + 1, w)[None, :] - (d == 0)
    poolmat = pool.reshape(4, NT, P, S).transpose(2, 0, 1, 3).reshape(P, POOL_WORDS)
    d = 2 * P - 1 - np.arange(DIST)
    dd = np.maximum(d, 0)
    onehot = (np.arange(32)[:, None] == bucket(dd)[None, :]).astype(np.float32)
    n_in = (dd <= 128).astype(int) + (dd % 4 == 0) + (dd % 16 == 0)
    lnc = np.where((d >= 0) & (n_in > 0), np.log(np.maximum(n_in, 1)), NEG).astype(np.float32)
    return const, np.ascontiguousarray(poolmat), onehot, np.ascontiguousarray(np.broadcast_to(lnc, (H, DIST)))



def chunked(w):
    kk, n = w.shape
    return np.ascontiguousarray(w.reshape(kk // P, P, n).transpose(1, 0, 2)).reshape(P, -1)


def stack_units(parts):
    out = np.zeros((len(parts), P, UNIT), np.float32)
    for i, a in enumerate(parts):
        out[i, :, :a.shape[1]] = a
    return out


def ffn_parts(w_in, w_out):
    a = w_in.reshape(KC, P, 2, FFN_IN_UNITS, 2 * P).transpose(3, 1, 0, 2, 4).reshape(FFN_IN_UNITS, P, UNIT)
    return list(a), [chunked(w_out[512 * u:512 * (u + 1)]) for u in range(FFN_OUT_UNITS)]


def layer_parts(i, l):
    ffa_in, ffa_out = ffn_parts(i["ffa_w_in_2"][l], i["ffa_w_out_2"][l])
    ffb_in, ffb_out = ffn_parts(i["ffb_w_in_2"][l], i["ffb_w_out_2"][l])
    w = i["w_in_2"][l]
    mla = [chunked(np.concatenate([w[:, 0:416], w[:, 1952:1960]], axis=1)),
           np.concatenate([chunked(i["mla_w_uq_2"][l]), i["mla_w_ukv_2"][l]], axis=1)]
    cols = [2472, 2984, 3496, 416, 928, 1440, 1960] + [4008 + 512 * g for g in range(6)]
    return (ffa_in + ffa_out + mla + [chunked(w[:, c:c + 512]) for c in cols]
            + [chunked(i["w_branch_2"][l, n]) for n in range(3)]
            + [chunked(i["w_out_2"][l][:, 512 * v:512 * (v + 1)]) for v in range(2)] + ffb_in + ffb_out)


def by_partition(v):
    return v.reshape(-1, P).T


def rows_of(v):
    return np.broadcast_to(v.reshape(1, -1), (P, v.size))


def vector_table(table, parts):
    out = np.zeros((P, table["all"][1]), np.float32)
    for name, a in parts.items():
        out[:, table[name][0]:table[name][1]] = a
    return out


def layout(i):
    const, poolmat, onehot, lnc = constants()
    w = i["w_in"][0]
    first = [chunked(w[:, c:c + 512]) for c in (512, 1024, 1536, 0)]
    first += [chunked(i["w_out"][0][:, 512 * v:512 * (v + 1)]) for v in range(2)]
    gate_up = i["w_gate_up"][0].reshape(E, KC, P, 2, 4, 2 * P).transpose(0, 4, 2, 1, 3, 5).reshape(E, 4, P, UNIT)
    down = i["w_down"][0].reshape(E, KC, P, 2, 512).transpose(0, 3, 2, 1, 4).reshape(E, 2, P, UNIT)
    ple = [chunked(i["w_ple_gate"][0][:, 512 * v:512 * (v + 1)]) for v in range(2)] + [chunked(i["w_ple_proj"][0])]
    fvec = vector_table(FVEC, {
        "g_mix": by_partition(i["g_mix"][0]), "g_ffn": by_partition(i["g_ffn"][0]), "g_ple": by_partition(i["g_ple"][0]),
        "pool_scale": by_partition(i["pool_scale"][0]), "b_router": rows_of(i["b_router"][0]),
        "w_router": chunked(i["w_router"][0])})
    lvec = np.stack([vector_table(LVEC, {
        "g_ffa": by_partition(i["ffa_norm_2"][l]), "g_mix": by_partition(i["mix_norm_2"][l]),
        "g_ffb": by_partition(i["ffb_norm_2"][l]),
        "conv": i["gdn_conv_2"][l].reshape(4, 12, P).transpose(2, 1, 0).reshape(P, 48),
        "c_norm": by_partition(np.concatenate([i["mla_cq_norm_2"][l], i["mla_ckv_norm_2"][l]])),
        "q_norm": rows_of(i["mla_q_norm_2"][l]), "k_norm": rows_of(i["mla_k_norm_2"][l]),
        "out_norm": rows_of(i["gdn_out_norm_2"][l]), "moba_q": rows_of(i["moba_q_norm_2"][l]),
        "moba_k": rows_of(i["moba_k_norm_2"][l]), "a_log": rows_of(i["gdn_a_log_2"][l]),
        "dt": rows_of(i["gdn_dt_bias_2"][l])}) for l in range(LAYERS)])
    return {
        "x": i["x"], "const": const, "fvec": fvec, "lvec": lvec, "onehot": onehot, "lnc": lnc, "poolmat": poolmat,
        "rel_bias": i["rel_bias"], "w_pool": i["w_pool"], "first_units": stack_units(first),
        "expert_units": np.concatenate([gate_up, down], axis=1).reshape(E * EXPERT_UNITS, P, UNIT),
        "b_gu": np.ascontiguousarray(i["b_gate_up"][0].reshape(E, 16, P).transpose(2, 0, 1)), "b_down": i["b_down"],
        "ple_units": stack_units(ple), "pT": np.ascontiguousarray(i["p"][0, 0].T), "g_final": np.ascontiguousarray(rows_of(i["g_final"])),
        "layer_units": stack_units([a for l in range(LAYERS) for a in layer_parts(i, l)]),
    }


def declare(nc, arrays):
    dram = {name: nc.dram_tensor(f"in_{name}", a.shape, mybir.dt.from_np(a.dtype), kind="ExternalInput").ap()
            for name, a in arrays.items()}
    dram["rev"] = nc.dram_tensor("bias_by_distance", (H, DIST), F32, kind="Internal").ap()
    dram["out"] = nc.dram_tensor("out", (1, S, D), F32, kind="ExternalOutput").ap()
    return dram


def kernel(**inputs):
    import concourse.bacc as bacc
    from concourse.bass_utils import run_bass_kernel_spmd
    arrays = layout({name: np.asarray(a) for name, a in inputs.items()})
    nc = bacc.Bacc("TRN2", target_bir_lowering=False, num_devices=1)
    build(nc, declare(nc, arrays))
    r = run_bass_kernel_spmd(nc, [{f"in_{name}": a for name, a in arrays.items()}], core_ids=[0])
    return r.results[0]["out"]
```

```python
import concourse.bass as bass
from concourse import mybir
from concourse.alu_op_type import AluOpType as ALU
from contextlib import ExitStack
import numpy as np

F32 = mybir.dt.float32
I32 = mybir.dt.int32
F32R = mybir.dt.float32r
ACT = mybir.ActivationFunctionType
AX = mybir.AxisListType

P = 128
S, D = 256, 1024
NT, KC = S // P, D // P
EPS = 1e-6
NEG = -1e30
H, V = 8, 64
E, TOPK, FE = 32, 4, 1024
DFF = 2816
FC = DFF // P
UNIT = 4096
SLOTS = 6
FIRST_UNITS, PLE_UNITS, EXPERT_UNITS = 6, 3, 6
FFN_IN_UNITS, FFN_OUT_UNITS = FC // 2, 6
PLE_WORDS = [UNIT, UNIT, UNIT // 2]
FFN_STEPS = [("in", 0), ("in", 1), ("in", 2)]
for _i in range(4):
    FFN_STEPS += [("in", 2 * _i + 3), ("out", _i), ("in", 2 * _i + 4)]
FFN_STEPS += [("out", 4), ("out", 5)]
MIX_STEPS = [("mla", 0), ("gates", 0), ("up_proj", 0), ("gates", 1), ("gates", 2), ("moba", 0), ("moba", 1), ("moba", 2),
             ("gates", 3), ("gates", 4), ("branch", 0), ("gdn", 0), ("gdn", 1), ("gdn", 2), ("z", 0), ("gates", 5),
             ("branch", 2), ("branch", 1), ("wout", 0), ("wout", 1)]
STEPS = [("ffn0",) + x for x in FFN_STEPS] + [x for x in MIX_STEPS] + [("ffn1",) + x for x in FFN_STEPS]
LAYER_UNITS = len(STEPS)
STEP = {x: i for i, x in enumerate(STEPS)}
HALF = UNIT // 2


def halves_of(step):
    if step[-2:] == ("out", 5):
        return [(0, HALF)]
    if step[0] == "mla":
        return [(0, 4 * MLA_COLS), (4 * MLA_COLS, 4 * MLA_COLS)]
    if step[0] == "up_proj":
        return [(0, 1536), (1536, 1024)]
    return [(0, HALF), (HALF, HALF)]


LAYERS = 2
MLA_D, MOBA_D, FIRST_D = 96, 64, 64
MLA_COLS = 424
GH = 4


def columns(widths):
    at, out = 0, {}
    for name, w in widths:
        out[name] = (at, at + w)
        at += w
    out["all"] = (0, at)
    return out


CONST = columns([("ident", P), ("flip", P), ("ones", P), ("tri", P), ("tri_strict", P), ("after_mask", P), ("causal", 2 * P),
                 ("iota", P), ("slot", P), ("levels", 7 * P), ("cos16", 32), ("sin16", 32), ("cos32", 64), ("sin32", 64)])
FVEC = columns([("g_mix", KC), ("g_ffn", KC), ("g_ple", KC), ("pool_scale", 4), ("b_router", E), ("w_router", KC * E)])
LVEC = columns([("g_ffa", KC), ("g_mix", KC), ("g_ffb", KC), ("conv", 48), ("c_norm", 3), ("q_norm", 96),
                ("k_norm", 96), ("out_norm", P), ("moba_q", 64), ("moba_k", 64), ("a_log", GH), ("dt", GH)])
POOL_WORDS = 4 * NT * S
COMB, SILU_TMP, MLA_ROWS, WORK, QKT, V_ROWS = 0, 2048, 2048, 2896, 5968, 10064
GATES_T, STATS, SCRATCH = 12660, 18804, 19172
RAW_SLOTS, SPLIT_SLOTS = 4, 3


class BankUses:

    def __init__(self):
        self.count, self.at = [0] * 8, {}

    def add(self, key, bank):
        self.at[key] = (bank, self.count[bank])
        self.count[bank] += 1


class Core:

    def __init__(self, nc, ctx):
        self.nc, self.ctx, self.names = nc, ctx, {}
        sb = lambda name, shape, dt=F32: ctx.enter_context(nc.sbuf_tensor(name, shape, dt))
        self.x = sb("x_res", [P, NT, D])
        self.h = sb("h_rows", [P, NT, D])
        self.const = sb("const", [P, CONST["all"][1]])
        self.fvec = sb("fvec", [P, FVEC["all"][1]])
        self.lvec = sb("lvec", [P, LVEC["all"][1]])
        self.scratch = sb("scratch", [P, SCRATCH])
        self.bank = [ctx.enter_context(nc.psum_tensor(f"bank{b}", [P, 512], F32)) for b in range(8)]
        sem = lambda name: ctx.enter_context(nc.semaphore(name))
        self.arrived = [sem(f"weights_arrived{i}") for i in range(SLOTS)]
        self.stored = sem("output_stored")
        self.later_arrived = [sem(f"later_weights_arrived{i}") for i in range(SLOTS)]
        self.bank_full = [sem(f"bank_full{b}") for b in range(8)]
        self.bank_free = [sem(f"bank_free{b}") for b in range(8)]
        self.dve_step = sem("dve_step")
        self.act_step = sem("act_step")
        self.pool = [sem(f"stage{i}") for i in range(70)]
        self.clear = range(self.later_arrived[0].num, self.pool[-1].num + 1)

    def first_memory(self, ctx):
        sb = lambda name, shape, dt=F32: ctx.enter_context(self.nc.sbuf_tensor(name, shape, dt))
        self.ring = [sb(f"ring{i}", [P, UNIT]) for i in range(SLOTS)]
        self.hT = sb("hT", [P, KC, S])

    def layer_memory(self, ctx):
        sb = lambda name, shape, dt=F32: ctx.enter_context(self.nc.sbuf_tensor(name, shape, dt))
        self.raw = [sb(f"raw{i}", [P, HALF // 2]) for i in range(RAW_SLOTS)]
        self.w = [[sb(f"w_{part}{i}", [P, HALF], F32R) for i in range(SPLIT_SLOTS)] for part in ("hi", "lo")]
        self.hT2 = [sb(f"hT_{part}", [P, KC, S], F32R) for part in ("hi", "lo")]
        self.act2 = [sb(f"act_{part}", [P, 12, S], F32R) for part in ("hi", "lo")]

    def c(self, name, w=None):
        a, b = CONST[name]
        return self.const[:, a:b]

    def f(self, name):
        a, b = FVEC[name]
        return self.fvec[:, a:b]

    def lv(self, name):
        a, b = LVEC[name]
        return self.lvec[:, a:b]

    def s(self, at, *shape):
        n = int(np.prod(shape))
        v = self.scratch[:, at:at + n]
        if len(shape) == 1:
            return v
        names = "abcd"[:len(shape)]
        return v.rearrange(f"p ({' '.join(names)}) -> p {' '.join(names)}", **dict(zip(names, shape)))

    def begin(self, uses):
        self.names, self.uses = {}, uses

    def sem(self, name):
        if name not in self.names:
            self.names[name] = self.pool[len(self.names)]
        return self.names[name]

    def end_phase(self):
        self.nc.all_engine_barrier(sems_to_clear=self.clear)

    def claim(self, pe, key):
        b, k = self.uses.at[key]
        if k:
            pe.wait_ge(self.bank_free[b], k)
        return self.bank[b], self.bank_full[b]

    def filled(self, eng, key):
        b, k = self.uses.at[key]
        eng.wait_ge(self.bank_full[b], k + 1)
        return self.bank[b], self.bank_free[b]

    def evacuated(self, eng, *keys):
        for key in keys:
            b, k = self.uses.at[key]
            eng.wait_ge(self.bank_free[b], k + 1)


def part(bank, *shape):
    n = int(np.prod(shape))
    names = "abc"[:len(shape)]
    return bank[:, 0:n].rearrange(f"p ({' '.join(names)}) -> p {' '.join(names)}", **dict(zip(names, shape)))


def chain_of(eng, sem):
    count = [0]

    def link(ins):
        count[0] += 1
        ins.then_inc(sem, 1)
        eng.wait_ge(sem, count[0])
    return link



def rstd_dve(k, dve, link, v, mean, n):
    link(k.nc.vector.tensor_scalar(v, v, mean, EPS, ALU.mult, ALU.add))
    k.nc.vector.reciprocal(v, v).then_inc(k.sem("inverse_variance"), 1)
    dve.wait_ge(k.sem("rstd_ready"), n + 1)


def rstd_act(k, act, v, n):
    act.wait_ge(k.sem("inverse_variance"), n + 1)
    k.nc.scalar.activation(v, v, ACT.Sqrt).then_inc(k.sem("rstd_ready"), 1)


def bc(ap, shape):
    return ap.to_broadcast(shape)



def norm_uses(uses, n, banks=(0, 1, 2, 3)):
    for t in range(NT):
        for half in range(2):
            uses.add(("norm", n, t, half), banks[2 * t + half])


def norm_act(k, act, n, x_ready=None, power=0):
    nc, st = k.nc, k.s(STATS, SCRATCH - STATS)
    if x_ready is not None:
        act.wait_ge(*x_ready)
    for t in range(NT):
        nc.scalar.activation(k.h[:, t, :], k.x[:, t, :], ACT.Square, accum_out=st[:, t:t + 1]).then_inc(k.sem("ss_ready"), 1)
    rstd_act(k, act, st[:, 0:2], power)


def norm_dve(k, dve, link, n, gain, power=0):
    nc, st = k.nc, k.s(STATS, SCRATCH - STATS)
    dve.wait_ge(k.sem("ss_ready"), 2 * (n + 1))
    rstd_dve(k, dve, link, st[:, 0:2], 1.0 / D, power)
    for t in range(NT):
        nc.vector.tensor_scalar(k.h[:, t, :], k.x[:, t, :], st[:, t:t + 1], None, ALU.mult).then_inc(k.sem("h_ready"), 1)
    for half in range(2):
        for t in range(NT):
            b, free = k.filled(dve, ("norm", n, t, half))
            nc.vector.tensor_tensor(k.hT[:, 4 * half:4 * half + 4, t * P:(t + 1) * P], part(b, 4, P),
                                    bc(gain[:, 4 * half:4 * half + 4].unsqueeze(2), [P, 4, P]), ALU.mult).then_inc(free, 1)


def norm_pe(k, pe, n):
    nc = k.nc
    for half in range(2):
        for t in range(NT):
            if half == 0:
                pe.wait_ge(k.sem("h_ready"), 2 * n + t + 1)
            b, full = k.claim(pe, ("norm", n, t, half))
            for j in range(4):
                c = 4 * half + j
                last = nc.tensor.transpose(b[:, j * P:(j + 1) * P], k.h[:, t, c * P:(c + 1) * P], k.c("ident"))
            last.then_inc(full, 1)


def hT_written(k, eng, n, halves=(0, 1)):
    k.evacuated(eng, *[("norm", n, t, half) for t in range(NT) for half in halves])



def attn_uses(uses, n):
    for q in range(2):
        for t in range(NT):
            for half in range(2):
                uses.add(("qkT", n, q, t, half), 4 * q + 2 * t + half)
    for t in range(NT):
        for pair in range(4):
            uses.add(("score", n, t, pair), 4 * t + pair)
    for half in range(2):
        uses.add(("pT", n, 0, half), half)
    for pair in range(4):
        uses.add(("pT", n, 1, pair), 2 + pair)
    for t in range(NT):
        uses.add(("oT", n, t), 6 + t)


class Attn:

    def __init__(self, k, n, d, qk, v, qkT, prob, pT, outT):
        self.n, self.d = n, d
        self.qk = k.s(qk, 2 * NT * H, d)
        self.v = k.s(v, NT, H, V)
        self.qkT = k.s(qkT, 2, H, S)
        self.prob = [k.s(prob, H, P), k.s(prob + H * P, H, 2 * P)]
        self.pT = [k.s(pT, H, 1, P), k.s(pT + H * P, H, 2, P)]
        self.outT = outT
        self.st = k.s(STATS + 64 + 0, 64)


def attn_pe(k, pe, a):
    nc, n, d = k.nc, a.n, a.d
    pe.wait_ge(k.sem("qk_ready"), a.n + 1)
    for q in range(2):
        for t in range(NT):
            for half in range(2):
                b, full = k.claim(pe, ("qkT", n, q, t, half))
                for j in range(4):
                    row = (q * NT + t) * H + 4 * half + j
                    last = nc.tensor.transpose(b[0:d, j * P:(j + 1) * P], a.qk[:, row, :], k.c("ident"))
                last.then_inc(full, 1)
    k.evacuated(pe, *[("qkT", n, q, t, half) for q in range(2) for t in range(NT) for half in range(2)])
    for t in range(NT):
        w = (t + 1) * P
        for pair in range(4):
            b, full = k.claim(pe, ("score", n, t, pair))
            for j in range(2):
                h = 2 * pair + j
                last = nc.tensor.matmul(b[:, j * 2 * P:j * 2 * P + w], a.qkT[0:d, 0, h, t * P:(t + 1) * P],
                                        a.qkT[0:d, 1, h, 0:w], start=True, stop=True)
            last.then_inc(full, 1)


def attn_values_pe(k, pe, a):
    nc, n = k.nc, a.n
    for t in range(NT):
        per = 4 if t == 0 else 2
        for g in range(H // per):
            b, full = k.claim(pe, ("pT", n, t, g))
            for j in range(per):
                h = per * g + j
                if h % 2 == 0:
                    pe.wait_ge(k.sem("probs_normalised"), H * n + 4 * t + h // 2 + 1)
                for c in range(t + 1):
                    at = (j * (t + 1) + c) * P
                    last = nc.tensor.transpose(b[:, at:at + P], a.prob[t][:, h, c * P:(c + 1) * P], k.c("ident"))
            last.then_inc(full, 1)
    for t in range(NT):
        b, full = k.claim(pe, ("oT", n, t))
        k.evacuated(pe, *[("pT", n, t, g) for g in range(2 if t == 0 else 4)])
        for pair in range(H // 2):
            for c in range(t + 1):
                for g in range(2):
                    last = nc.tensor.matmul(b[g * V:(g + 1) * V, pair * P:(pair + 1) * P], a.v[:, c, 2 * pair + g, :],
                                            a.pT[t][:, 2 * pair + g, c, :], start=(c == 0), stop=(c == t))
        last.then_inc(full, 1)


def attn_act(k, act, a):
    nc, n, d = k.nc, a.n, a.d
    for q in range(2):
        for t in range(NT):
            for half in range(2):
                b, free = k.filled(act, ("qkT", n, q, t, half))
                nc.scalar.copy(a.qkT[0:d, q, 4 * half:4 * half + 4, t * P:(t + 1) * P], part(b, 4, P)[0:d])\
                    .then_inc(free, 1)
    for t in range(NT):
        for h in range(H):
            act.wait_ge(k.sem("max_ready"), 8 * n + 4 * t + h // 2 + 1)
            nc.scalar.activation(a.prob[t][:, h, :], a.prob[t][:, h, :], ACT.Exp, bias=a.st[:, 8 * t + h:8 * t + h + 1],
                                 accum_out=a.st[:, 16 + 8 * t + h:17 + 8 * t + h]).then_inc(k.sem("prob_ready"), 1)
    for t in range(NT):
        per = 4 if t == 0 else 2
        for g in range(H // per):
            b, free = k.filled(act, ("pT", n, t, g))
            nc.scalar.copy(a.pT[t][:, per * g:per * g + per, :, :].rearrange("p a b c -> p (a b c)"),
                           b[:, 0:per * (t + 1) * P]).then_inc(free, 1)


def attn_dve(k, dve, link, a, scale, mask):
    nc, n = k.nc, a.n

    def scores(t, pair):
        b, free = k.filled(dve, ("score", n, t, pair))
        s = a.prob[t][:, 2 * pair:2 * pair + 2, :]
        nc.vector.scalar_tensor_tensor(out=s, in0=part(b, 2, 2 * P)[:, :, 0:(t + 1) * P], scalar=scale, in1=mask(t, pair),
                                       op0=ALU.mult, op1=ALU.add).then_inc(free, 1)
        k.evacuated(dve, ("score", n, t, pair))
        m = 8 * t + 2 * pair
        nc.vector.tensor_reduce(a.st[:, m:m + 2], s, AX.X, ALU.max, negate=True).then_inc(k.sem("max_ready"), 1)

    def normalise(t, pair):
        dve.wait_ge(k.sem("prob_ready"), 2 * H * n + H * t + 2 * pair + 2)
        m = 8 * t + 2 * pair
        link(nc.vector.reciprocal(a.st[:, 32 + m:34 + m], a.st[:, 16 + m:18 + m]))
        s = a.prob[t][:, 2 * pair:2 * pair + 2, :]
        nc.vector.tensor_tensor(s, s, bc(a.st[:, 32 + m:34 + m].unsqueeze(2), [P, 2, (t + 1) * P]), ALU.mult)\
            .then_inc(k.sem("probs_normalised"), 1)

    for pair in range(H // 2):
        scores(0, pair)
    for pair in range(H // 2):
        scores(1, pair)
        normalise(0, pair)
    for pair in range(H // 2):
        normalise(1, pair)
    for t in range(NT):
        b, free = k.filled(dve, ("oT", n, t))
        if len(a.outT) == 1:
            nc.vector.tensor_copy(a.outT[0][:, :, t * P:(t + 1) * P], part(b, 4, P)).then_inc(free, 1)
            continue
        hi, lo = (v[:, :, t * P:(t + 1) * P] for v in a.outT)
        link(nc.vector.tensor_copy(hi, part(b, 4, P)))
        nc.vector.tensor_tensor(lo, part(b, 4, P), hi, ALU.subtract).then_inc(free, 1)


def rows_pe(k, pe, key, w, lhsT, cols, chunks=KC):
    for t in range(NT):
        b, full = k.claim(pe, key + (t,))
        for c in range(chunks):
            last = k.nc.tensor.matmul(b[:, 0:cols], lhsT[:, c, t * P:(t + 1) * P], w[:, c, 0:cols],
                                      start=(c == 0), stop=(c == chunks - 1))
        last.then_inc(full, 1)
    return last



class Splits:

    def __init__(self, k, eng, emit):
        self.k, self.eng, self.emit, self.done = k, eng, emit, 0

    def ahead(self, step):
        upto = min(last_half_of(step) + SPLIT_SLOTS + 1, len(HALVES))
        for i in range(self.done, upto):
            self.emit(self.k, self.eng, i)
        self.done = max(self.done, upto)


HALVES = [(i, at, words) for i, x in enumerate(STEPS) for at, words in halves_of(x)]


def last_half_of(step):
    return max(i for i, h in enumerate(HALVES) if h[0] == step)


def half_read(k, i):
    step = STEPS[HALVES[i][0]]
    if ends_a_bank(i):
        b, n = k.uses.at[("q", 1, 1) if (step[0], HALVES[i][1]) == ("up_proj", 0) else last_use(step)]
        return k.bank_full[b], n + 1
    return k.sem("half_used"), sum(1 for j in range(i + 1) if not ends_a_bank(j))


def ends_a_bank(i):
    step = STEPS[HALVES[i][0]]
    if step[0] == "up_proj":
        return True
    return (HALVES[i][1] > 0 or step[-2:] == ("out", 5)) and not (step[-2] == "out" and step[-1] < 5)


def last_use(step):
    if step[0] in ("ffn0", "ffn1"):
        n = int(step[0] == "ffn1")
        return ("up", n, step[2]) if step[1] == "in" else ("ffn_out", n, 1, 1)
    name, i = step
    return {"mla": ("mla", 1), "up_proj": ("kv", 1, 1), "moba": ("moba", i, 1), "gdn": ("raw", i, 1), "z": ("z", 1),
            "gates": ("gates", i, 1), "branch": ("branch", i, 3), "wout": ("wout", 1, i)}[name]


def pieces(i):
    words = HALVES[i][2] // 2
    return [(2 * i + j, slice(j * words, (j + 1) * words)) for j in range(2)]


def hi_act(k, act, i):
    if i >= SPLIT_SLOTS:
        act.wait_ge(*half_read(k, i - SPLIT_SLOTS))
    for n, at in pieces(i):
        act.wait_ge(k.later_arrived[n % RAW_SLOTS], 16 * (n // RAW_SLOTS + 1))
        k.nc.scalar.copy(k.w[0][i % SPLIT_SLOTS][:, at], k.raw[n % RAW_SLOTS][:, 0:at.stop - at.start]).then_inc(k.sem("weights_hi"), 1)


def lo_pool(k, pool, i):
    for n, at in pieces(i):
        pool.wait_ge(k.sem("weights_hi"), n + 1)
        k.nc.gpsimd.tensor_tensor(k.w[1][i % SPLIT_SLOTS][:, at], k.raw[n % RAW_SLOTS][:, 0:at.stop - at.start],
                                  k.w[0][i % SPLIT_SLOTS][:, at], ALU.subtract).then_inc(k.sem("weights_split"), 1)


def weights(k, pe, step, shape):
    own = [i for i, h in enumerate(HALVES) if h[0] == STEP[step]]
    for h, i in enumerate(own):
        pe.wait_ge(k.sem("weights_split"), 2 * i + 2)
        words = HALVES[i][2]
        yield h, h == len(own) - 1, [k.w[j][i % SPLIT_SLOTS][:, 0:words].rearrange("p (c n) -> p c n", n=shape) for j in range(2)]


def mm3(nc, out, lhsT, rhs, start, stop):
    nc.tensor.matmul(out, lhsT[0], rhs[0], start=start, stop=False)
    nc.tensor.matmul(out, lhsT[0], rhs[1], start=False, stop=False)
    return nc.tensor.matmul(out, lhsT[1], rhs[0], start=False, stop=stop)


def columns_pe(k, pe, step, keys, operand_ready=lambda h: None):
    nc = k.nc
    banks = [k.claim(pe, key) for key in keys]
    for h, last_half, w in weights(k, pe, step, 512):
        operand_ready(h)
        for g, (b, full) in enumerate(banks):
            for j in range(2):
                col = (2 * g + j) * P
                for c in range(4):
                    last = mm3(nc, b[:, j * S:(j + 1) * S], [v[:, c, col:col + P] for v in w],
                               [v[:, 4 * h + c, :] for v in k.hT2], start=(h == 0 and j == 0 and c == 0),
                               stop=(last_half and j == 1 and c == 3))
            if last_half:
                last.then_inc(full, 1)
        if not last_half:
            last.then_inc(k.sem("half_used"), 1)


def rows3_pe(k, pe, step, keys, operand, cols, operand_ready=lambda h: None):
    nc = k.nc
    banks = [k.claim(pe, key) for key in keys]
    for h, last_half, w in weights(k, pe, step, cols):
        operand_ready(h)
        for t, (b, full) in enumerate(banks):
            for c in range(4):
                last = mm3(nc, b[:, 0:cols], [v[:, 4 * h + c, t * P:(t + 1) * P] for v in operand],
                           [v[:, c, :] for v in w], start=(h == 0 and c == 0), stop=(last_half and c == 3))
            if last_half:
                last.then_inc(full, 1)
        if not last_half:
            last.then_inc(k.sem("half_used"), 1)



def norm2_dve(k, dve, link, n, gain, power):
    nc, st = k.nc, k.s(STATS, SCRATCH - STATS)
    V_ = nc.vector
    dve.wait_ge(k.sem("ss_ready"), 2 * (n + 1))
    rstd_dve(k, dve, link, st[:, 0:2], 1.0 / D, power)
    for t in range(NT):
        V_.tensor_scalar(k.h[:, t, :], k.x[:, t, :], st[:, t:t + 1], None, ALU.mult).then_inc(k.sem("h_ready"), 1)
    for half in range(2):
        for t in range(NT):
            cols = slice(t * P, (t + 1) * P)
            b, free = k.filled(dve, ("norm", n, t, half))
            c4 = slice(4 * half, 4 * half + 4)
            link(V_.tensor_tensor(k.hT2[0][:, c4, cols], part(b, 4, P), bc(gain[:, c4].unsqueeze(2), [P, 4, P]), ALU.mult))
            for j in range(4):
                c = 4 * half + j
                ins = V_.scalar_tensor_tensor(out=k.hT2[1][:, c, cols], in0=b[:, j * P:(j + 1) * P], scalar=gain[:, c:c + 1],
                                              in1=k.hT2[0][:, c, cols], op0=ALU.mult, op1=ALU.subtract)
            ins.then_inc(free, 1)



def ffn_uses(uses, n):
    for u in range(FFN_IN_UNITS):
        uses.add(("gate", n, u), 2 * (u % 2))
        uses.add(("up", n, u), 2 * (u % 2) + 1)
    for t in range(NT):
        for v in range(2):
            uses.add(("ffn_out", n, t, v), 4 + 2 * t + v)


def ffn_pe(k, pe, n):
    nc = k.nc
    hT_ready = lambda h: hT_written(k, pe, 2 * n, (h,))
    out = None
    for kind, u in FFN_STEPS:
        step = (f"ffn{n}", kind, u)
        if kind == "in":
            keys = [("gate", n, u), ("up", n, u)]
            columns_pe(k, pe, step, keys, hT_ready) if u == 0 else columns_pe(k, pe, step, keys)
            continue
        if out is None:
            out = {(t, v): k.claim(pe, ("ffn_out", n, t, v)) for t in range(NT) for v in range(2)}
        pe.wait_ge(k.sem("act_lo"), FFN_IN_UNITS * n + min(2 * u + 2, FFN_IN_UNITS))
        for h, _last, w in weights(k, pe, step, D):
            for i in range(2):
                c = 4 * u + 2 * h + i
                for t in range(NT):
                    for v in range(2):
                        last = mm3(nc, out[t, v][0][:, :], [a[:, c % 12, t * P:(t + 1) * P] for a in k.act2],
                                   [a[:, i, v * 512:(v + 1) * 512] for a in w], start=(c == 0), stop=(c == FC - 1))
                        if c == FC - 1:
                            last.then_inc(out[t, v][1], 1)
            if u < FFN_OUT_UNITS - 1:
                last.then_inc(k.sem("half_used"), 1)


def ffn_act(k, act, n, splits):
    silu, prod = k.s(SILU_TMP, 2, 512), k.s(SILU_TMP + 1024, 2, 512)
    for kind, u in FFN_STEPS:
        splits.ahead(STEP[f"ffn{n}", kind, u])
        if kind == "out":
            continue
        b, free = k.filled(act, ("gate", n, u))
        k.nc.scalar.activation(silu[:, u % 2, :], b[:, :], ACT.Silu).then_inc(free, 1)
        k.evacuated(act, ("up", n, u))
        at = 2 * u % 12
        k.nc.scalar.copy(k.act2[0][:, at:at + 2, :].rearrange("p c n -> p (c n)"), prod[:, u % 2, :]).then_inc(k.sem("act_hi"), 1)


def ffn_dve(k, dve, n):
    nc = k.nc
    silu, prod = k.s(SILU_TMP, 2, 512), k.s(SILU_TMP + 1024, 2, 512)
    for kind, u in FFN_STEPS:
        if kind == "out":
            continue
        b, free = k.filled(dve, ("up", n, u))
        k.evacuated(dve, ("gate", n, u))
        nc.vector.tensor_tensor(prod[:, u % 2, :], silu[:, u % 2, :], b[:, :], ALU.mult).then_inc(free, 1)
        dve.wait_ge(k.sem("act_hi"), FFN_IN_UNITS * n + u + 1)
        hi, lo = (a[:, 2 * u % 12:2 * u % 12 + 2, :].rearrange("p c n -> p (c n)") for a in k.act2)
        nc.vector.tensor_tensor(lo, prod[:, u % 2, :], hi, ALU.subtract).then_inc(k.sem("act_lo"), 1)
        dve.wait_ge(k.sem("act_lo"), FFN_IN_UNITS * n + u + 1)
    for t in range(NT):
        for v in range(2):
            b, free = k.filled(dve, ("ffn_out", n, t, v))
            x = k.x[:, t, v * 512:(v + 1) * 512]
            nc.vector.scalar_tensor_tensor(out=x, in0=b[:, :], scalar=0.5, in1=x, op0=ALU.mult, op1=ALU.add)\
                .then_inc(free, 1)



def head_norm_dve(k, dve, link, qk, sq, d, gains, power):
    nc, n = k.nc, 2 * NT * H
    st = k.s(STATS + 128, n)
    link(nc.vector.tensor_tensor(sq, qk, qk, ALU.mult))
    link(nc.vector.tensor_reduce(st, sq, AX.X, ALU.add))
    rstd_dve(k, dve, link, st, 1.0 / d, power)
    link(nc.vector.tensor_tensor(qk, qk, bc(st.unsqueeze(2), [P, n, d]), ALU.mult))
    for i, g in enumerate(gains):
        half = qk[:, i * n // 2:(i + 1) * n // 2, :]
        link(nc.vector.tensor_tensor(half, half, bc(g.unsqueeze(1), [P, n // 2, d]), ALU.mult))


def rope_dve(k, dve, link, qk, tmp, at, half, cos, sin, last_sem):
    nc = k.nc
    n = NT * H * half
    for i in range(2):
        rows = qk[:, i * NT * H:(i + 1) * NT * H, :].rearrange("p (t h) d -> p t h d", t=NT)
        x1, x2 = rows[:, :, :, at:at + half], rows[:, :, :, at + half:at + 2 * half]
        a, b, c, d = (k.s(tmp + j * n, NT, H, half) for j in range(4))
        cb, sb = (bc(v.rearrange("p (t f) -> p t f", t=NT).unsqueeze(2), [P, NT, H, half]) for v in (cos, sin))
        nc.vector.tensor_tensor(a, x1, cb, ALU.mult)
        nc.vector.tensor_tensor(b, x2, sb, ALU.mult)
        nc.vector.tensor_tensor(c, x2, cb, ALU.mult)
        link(nc.vector.tensor_tensor(d, x1, sb, ALU.mult))
        nc.vector.tensor_tensor(x1, a, b, ALU.subtract)
        ins = nc.vector.tensor_tensor(x2, c, d, ALU.add)
        if i == 0:
            link(ins)
        else:
            ins.then_inc(last_sem, 1)



GDN_RAW, GDN_CONV, GDN_SQ, GDN_V, GDN_KDEC, GDN_DIAG = 2896, 6004, 9076, 11124, 12148, 0
GDN_DECAY, GDN_M, GDN_QK = 2896, 3920, 4944
GDN_X, GDN_XT, GDN_P, GDN_OT = 9076, 10100, 0, 1024
LEVELS = 7


def gdn_uses(uses):
    for i in range(3):
        for pair in range(2):
            uses.add(("raw", i, pair), 2 * i + pair)
    for t in range(NT):
        uses.add(("z", t), 6 + t)
    for pair in range(2):
        uses.add(("gates", 5, pair), 2 + pair)
    for b in range(4):
        uses.add(("l2", b), b)
    uses.add(("gc",), 4)
    for t in range(NT):
        uses.add(("gcB", t), 5 + t)
    branch_uses(uses, 2, 0)
    for t in range(NT):
        uses.add(("KK", t), (7, 4)[t])
    for t in range(NT):
        uses.add(("vT", t), t)
    for t in range(NT):
        uses.add(("betaB", t), 2 + t)
    for t in range(NT):
        uses.add(("QK", t), 5 + t)
    uses.add(("kdec",), 0)
    for lev in range(LEVELS):
        for t in range(NT):
            uses.add(("P", lev, t), 4 * t + 3)
        for t in range(NT):
            if lev < LEVELS - 1:
                uses.add(("XP", lev, t), 4 * t + 1)
            uses.add(("PX", lev, t), 4 * t + 2)
    for key, b in ((("vn", 0), 0), (("go", 0), 1), (("S1",), 2), (("KS",), 3), (("QS",), 4), (("vn", 1), 5),
                   (("go", 1), 6), (("goT", 0), 0), (("goT", 1), 1)):
        uses.add(key, b)


class Gdn:
    def __init__(self, k):
        self.raw = k.s(GDN_RAW, 12, S + 3)
        self.cv = k.s(GDN_CONV, 12, S)
        self.sq = k.s(GDN_SQ, 8, S)
        self.v = k.s(GDN_V, NT, GH, P)
        self.kdec = k.s(GDN_KDEC, GH, P)
        self.gdiag = k.s(GDN_DIAG, NT, GH, P)
        self.bdiag = k.h[:, 1, :].rearrange("p (t h n) -> p t h n", t=NT, h=GH)
        self.z = k.h[:, 0, :].rearrange("p (t n) -> p t n", t=NT)
        self.o = self.bdiag
        self.decay, self.m, self.qk = (k.s(a, NT, GH, P) for a in (GDN_DECAY, GDN_M, GDN_QK))
        self.X, self.XT, self.P, self.OT = (k.s(a, NT, GH, P) for a in (GDN_X, GDN_XT, GDN_P, GDN_OT))
        self.R, self.vn, self.S1, self.tmp = self.OT, self.X, k.s(GDN_P, GH, P), k.s(GDN_P + GH * P, GH, P)
        small = lambda at, *shape: k.s(STATS + 256 + at, *shape)
        self.beta, self.xa, self.nax, self.ex, self.ln = (small(8 * i, NT, GH) for i in range(5))
        self.eal, self.g, self.gsum, self.glast = small(40, GH), small(44, NT, GH), small(52, NT, GH), small(60, GH)
        self.gsum_all, self.eg, self.dk, self.ostat = small(52, 12), small(64, NT, GH), small(72, GH), small(76, 8)
        self.b_in = k.s(MLA_ROWS, NT, MLA_COLS)[:, :, 416:420]
        self.a_in = k.s(MLA_ROWS, NT, MLA_COLS)[:, :, 420:424]


def heads_mm(nc, b, lhsT, rhs):
    for h in range(GH):
        last = nc.tensor.matmul(b[:, h * P:(h + 1) * P], lhsT[:, h, :], rhs[:, h, :], start=True, stop=True)
    return last


def gdn_pe(k, pe):
    nc, G = k.nc, Gdn(k)
    for b4 in range(4):
        b, full = k.claim(pe, ("l2", b4))
        pe.wait_ge(k.sem("sq_ready"), b4 // 2 + 1)
        nc.tensor.matmul(b[:, :], k.c("ones"), G.sq[:, 2 * b4:2 * b4 + 2, :], start=True, stop=True).then_inc(full, 1)
    b, full = k.claim(pe, ("gc",))
    pe.wait_ge(k.sem("g_ready"), 1)
    nc.tensor.matmul(b[:, 0:4], k.c("tri"), G.g[:, 0, :], start=True, stop=True)
    nc.tensor.matmul(b[:, 4:8], k.c("tri"), G.g[:, 1, :], start=True, stop=True)
    nc.tensor.matmul(b[:, 8:12], k.c("ones"), G.g[:, 0, :], start=True, stop=True).then_inc(full, 1)
    pe.wait_ge(k.sem("gdiag_ready"), 1)
    for t in range(NT):
        b, full = k.claim(pe, ("gcB", t))
        nc.tensor.matmul(b[:, :], k.c("ones"), G.gdiag[:, t, :, :], start=True, stop=True).then_inc(full, 1)
    k.evacuated(pe, ("oT", 1, 0), ("oT", 1, 1))
    branch_pe(k, pe, 2)
    pe.wait_ge(k.sem("l2_done"), 1)
    for t in range(NT):
        b, full = k.claim(pe, ("KK", t))
        keys = G.cv[:, GH:2 * GH, t * P:(t + 1) * P]
        heads_mm(nc, b, keys, keys).then_inc(full, 1)
    pe.wait_ge(k.sem("conv_silu"), 3)
    for t in range(NT):
        b, full = k.claim(pe, ("vT", t))
        for h in range(GH):
            last = nc.tensor.transpose(b[:, h * P:(h + 1) * P], G.cv[:, 8 + h, t * P:(t + 1) * P], k.c("ident"))
        last.then_inc(full, 1)
    pe.wait_ge(k.sem("bdiag_ready"), 1)
    for t in range(NT):
        b, full = k.claim(pe, ("betaB", t))
        nc.tensor.matmul(b[:, :], k.c("ones"), G.bdiag[:, t, :, :], start=True, stop=True).then_inc(full, 1)
    for t in range(NT):
        b, full = k.claim(pe, ("QK", t))
        cols = slice(t * P, (t + 1) * P)
        heads_mm(nc, b, G.cv[:, GH:2 * GH, cols], G.cv[:, 0:GH, cols]).then_inc(full, 1)
    b, full = k.claim(pe, ("kdec",))
    for h in range(GH):
        last = nc.tensor.transpose(b[:, h * P:(h + 1) * P], G.cv[:, GH + h, 0:P], k.c("ident"))
    last.then_inc(full, 1)
    for lev in range(LEVELS):
        for t in range(NT):
            b, full = k.claim(pe, ("P", lev, t))
            pe.wait_ge(k.sem("ot_ready"), 2 * lev + t + 1)
            if lev:
                k.evacuated(pe, ("XP", lev - 1, t))
            heads_mm(nc, b, G.OT[:, t], G.X[:, t]).then_inc(full, 1)
        for t in range(NT):
            k.evacuated(pe, ("P", lev, t))
            if lev:
                k.evacuated(pe, ("PX", lev - 1, t))
            if lev < LEVELS - 1:
                b, full = k.claim(pe, ("XP", lev, t))
                heads_mm(nc, b, G.XT[:, t], G.P[:, t]).then_inc(full, 1)
            b, full = k.claim(pe, ("PX", lev, t))
            heads_mm(nc, b, G.P[:, t], G.XT[:, t]).then_inc(full, 1)
    k.evacuated(pe, ("PX", LEVELS - 1, 0), ("PX", LEVELS - 1, 1))
    b, full = k.claim(pe, ("vn", 0))
    pe.wait_ge(k.sem("r_ready"), 1)
    heads_mm(nc, b, G.XT[:, 0], G.R[:, 0]).then_inc(full, 1)
    k.evacuated(pe, ("vn", 0))
    b, full = k.claim(pe, ("go", 0))
    heads_mm(nc, b, G.qk[:, 0], G.vn[:, 0]).then_inc(full, 1)
    b, full = k.claim(pe, ("S1",))
    k.evacuated(pe, ("kdec",))
    heads_mm(nc, b, G.kdec, G.vn[:, 0]).then_inc(full, 1)
    k.evacuated(pe, ("S1",))
    b, full = k.claim(pe, ("KS",))
    heads_mm(nc, b, G.cv[:, GH:2 * GH, P:2 * P], G.S1).then_inc(full, 1)
    b, full = k.claim(pe, ("QS",))
    heads_mm(nc, b, G.cv[:, 0:GH, P:2 * P], G.S1).then_inc(full, 1)
    b, full = k.claim(pe, ("vn", 1))
    pe.wait_ge(k.sem("r_ready"), 2)
    heads_mm(nc, b, G.XT[:, 1], G.R[:, 1]).then_inc(full, 1)
    k.evacuated(pe, ("vn", 1))
    b, full = k.claim(pe, ("go", 1))
    heads_mm(nc, b, G.qk[:, 1], G.vn[:, 1]).then_inc(full, 1)
    pe.wait_ge(k.sem("go_ready"), 1)
    for t in range(NT):
        b, full = k.claim(pe, ("goT", t))
        for h in range(GH):
            last = nc.tensor.transpose(b[:, h * P:(h + 1) * P], G.o[:, t, h, :], k.c("ident"))
        last.then_inc(full, 1)


def gdn_act(k, act, splits):
    nc, G = k.nc, Gdn(k)
    act.wait_ge(k.sem("xa_ready"), 1)
    nc.scalar.activation(G.ex, G.nax, ACT.Exp).then_inc(k.act_step, 1)
    nc.scalar.activation(G.eal, k.lv("a_log"), ACT.Exp)
    act.wait_ge(k.act_step, 1)
    nc.scalar.activation(G.ln, G.ex, ACT.Ln, bias=1.0).then_inc(k.sem("softplus"), 1)
    nc.scalar.activation(G.beta, G.b_in, ACT.Sigmoid).then_inc(k.sem("beta_ready"), 1)
    for i in range(3):
        splits.ahead(STEP["gdn", i])
        for pair in range(2):
            b, free = k.filled(act, ("raw", i, pair))
            nc.scalar.copy(G.raw[:, 4 * i + 2 * pair:4 * i + 2 * pair + 2, 3:3 + S], part(b, 2, S)).then_inc(free, 1)
    splits.ahead(STEP["z", 0])
    for t in range(NT):
        b, free = k.filled(act, ("z", t))
        nc.scalar.activation(G.z[:, t, :], b[:, :], ACT.Silu).then_inc(free, 1)
    for i in range(3):
        act.wait_ge(k.sem("conv_ready"), i + 1)
        cv = G.cv[:, 4 * i:4 * i + 4, :]
        nc.scalar.activation(cv, cv, ACT.Silu).then_inc(k.sem("conv_silu"), 1)
    gates_act(k, act, splits, 5)
    for i in range(2):
        act.wait_ge(k.sem("l2_inverse"), 2 * i + 2)
        sq = G.sq[:, 4 * i:4 * i + 4, :]
        nc.scalar.activation(sq, sq, ACT.Sqrt).then_inc(k.sem("l2_rstd"), 1)
    act.wait_ge(k.sem("dk_in"), 1)
    nc.scalar.activation(G.dk, G.dk, ACT.Exp).then_inc(k.sem("eg_ready"), 1)
    nc.scalar.activation(G.eg, G.gsum, ACT.Exp).then_inc(k.sem("eg_ready"), 1)
    for t in range(NT):
        act.wait_ge(k.sem("decay_in"), t + 1)
        nc.scalar.activation(G.decay[:, t], G.decay[:, t], ACT.Exp).then_inc(k.sem("decay_ready"), 1)
    splits.ahead(STEP["branch", 2])
    for t in range(NT):
        b, free = k.filled(act, ("vT", t))
        nc.scalar.copy(G.v[:, t], part(b, GH, P)).then_inc(free, 1)
    for lev in range(LEVELS):
        for t in range(NT):
            b, free = k.filled(act, ("P", lev, t))
            nc.scalar.copy(G.P[:, t], part(b, GH, P)).then_inc(free, 1)
    rstd_act(k, act, G.ostat, 5)
    for t in range(NT):
        b, _free = k.filled(act, ("goT", t))
        nc.scalar.copy(k.act2[0][:, 4:8, t * P:(t + 1) * P], part(b, 4, P)).then_inc(k.sem("go_hi"), 1)


def gdn_dve(k, dve, link):
    nc, G = k.nc, Gdn(k)
    V_ = nc.vector
    heads = lambda ap: bc(ap.unsqueeze(2), [P, GH, P])
    same = lambda name: bc(k.c(name).unsqueeze(1), [P, GH, P])
    link(V_.tensor_tensor(G.xa, G.a_in, bc(k.lv("dt").unsqueeze(1), [P, NT, GH]), ALU.add))
    V_.scalar_tensor_tensor(out=G.nax, in0=G.xa, scalar=-1.0, in1=G.xa, op0=ALU.mult, op1=ALU.min).then_inc(k.sem("xa_ready"), 1)
    V_.memset(G.raw[:, :, 0:3], 0.0)
    dve.wait_ge(k.sem("softplus"), 1)
    V_.tensor_scalar(G.eal, G.eal, -1.0, None, ALU.mult)
    link(V_.scalar_tensor_tensor(out=G.xa, in0=G.xa, scalar=0.0, in1=G.ln, op0=ALU.max, op1=ALU.add))
    V_.tensor_tensor(G.g, G.xa, bc(G.eal.unsqueeze(1), [P, NT, GH]), ALU.mult).then_inc(k.sem("g_ready"), 1)
    dve.wait_ge(k.sem("g_ready"), 1)
    for t in range(NT):
        ins = V_.tensor_tensor(G.gdiag[:, t], same("tri"), heads(G.g[:, t, :]), ALU.mult)
    ins.then_inc(k.sem("gdiag_ready"), 1)
    dve.wait_ge(k.sem("beta_ready"), 1)
    for t in range(NT):
        ins = V_.tensor_tensor(G.bdiag[:, t], same("ident"), heads(G.beta[:, t, :]), ALU.mult)
    ins.then_inc(k.sem("bdiag_ready"), 1)
    conv = k.lv("conv").rearrange("p (c j) -> p c j", j=4)
    for i in range(3):
        k.evacuated(dve, ("raw", i, 0), ("raw", i, 1))
        for j in range(4):
            for c in range(4 * i, 4 * i + 4):
                x, y, w = G.raw[:, c, j:j + S], G.cv[:, c, :], conv[:, c, j:j + 1]
                if j == 0:
                    ins = V_.tensor_scalar(y, x, w, None, ALU.mult)
                else:
                    ins = V_.scalar_tensor_tensor(out=y, in0=x, scalar=w, in1=y, op0=ALU.mult, op1=ALU.add)
            if j < 3:
                link(ins)
            else:
                ins.then_inc(k.sem("conv_ready"), 1)
    for i in range(2):
        dve.wait_ge(k.sem("conv_silu"), i + 1)
        cv = G.cv[:, 4 * i:4 * i + 4, :]
        V_.tensor_tensor(G.sq[:, 4 * i:4 * i + 4, :], cv, cv, ALU.mult).then_inc(k.sem("sq_ready"), 1)
    for b4 in range(4):
        b, free = k.filled(dve, ("l2", b4))
        V_.tensor_scalar(G.sq[:, 2 * b4:2 * b4 + 2, :], part(b, 2, S), EPS, None, ALU.add).then_inc(free, 1)
    for b4 in range(4):
        k.evacuated(dve, ("l2", b4))
        part_sq = G.sq[:, 2 * b4:2 * b4 + 2, :]
        V_.reciprocal(part_sq, part_sq).then_inc(k.sem("l2_inverse"), 1)
    dve.wait_ge(k.sem("l2_rstd"), 2)
    q, kk = G.cv[:, 0:GH, :], G.cv[:, GH:2 * GH, :]
    V_.scalar_tensor_tensor(out=q, in0=q, scalar=float(P) ** -0.5, in1=G.sq[:, 0:GH, :], op0=ALU.mult, op1=ALU.mult)
    V_.tensor_tensor(kk, kk, G.sq[:, GH:2 * GH, :], ALU.mult).then_inc(k.sem("l2_done"), 1)
    b, free = k.filled(dve, ("gc",))
    V_.tensor_copy(G.gsum_all, b[:, 0:12]).then_inc(free, 1)
    k.evacuated(dve, ("gc",))
    V_.tensor_tensor(G.dk, G.glast, G.gsum[:, 0, :], ALU.subtract).then_inc(k.sem("dk_in"), 1)
    for t in range(NT):
        b, free = k.filled(dve, ("gcB", t))
        V_.tensor_tensor(G.decay[:, t], part(b, GH, P), same("after_mask"), ALU.add).then_inc(free, 1)
        k.evacuated(dve, ("gcB", t))
        V_.tensor_tensor(G.decay[:, t], G.decay[:, t], heads(G.gsum[:, t, :]), ALU.subtract).then_inc(k.sem("decay_in"), 1)
    link(V_.tensor_copy(G.X[:, :].rearrange("p t h n -> p (t h) n"), bc(k.c("ident").unsqueeze(1), [P, 8, P])))
    link(V_.tensor_copy(G.XT[:, :].rearrange("p t h n -> p (t h) n"), bc(k.c("ident").unsqueeze(1), [P, 8, P])))
    branch_dve(k, dve, 2)
    for t in range(NT):
        dve.wait_ge(k.sem("decay_ready"), t + 1)
        b, free = k.filled(dve, ("KK", t))
        V_.tensor_tensor(G.m[:, t], part(b, GH, P), G.decay[:, t], ALU.mult).then_inc(free, 1)
        b, free = k.filled(dve, ("betaB", t))
        k.evacuated(dve, ("KK", t))
        V_.tensor_tensor(G.m[:, t], part(b, GH, P), G.m[:, t], ALU.mult).then_inc(free, 1)
        b, free = k.filled(dve, ("QK", t))
        V_.tensor_tensor(G.qk[:, t], part(b, GH, P), G.decay[:, t], ALU.mult).then_inc(free, 1)
    levels = k.c("levels").rearrange("p (l n) -> p l n", l=LEVELS)
    k.evacuated(dve, ("betaB", 0), ("betaB", 1))

    def level_part(lev, t):
        V_.tensor_tensor(G.OT[:, t], G.m[:, t], bc(levels[:, lev, :].unsqueeze(1), [P, GH, P]), ALU.mult)\
            .then_inc(k.sem("ot_ready"), 1)

    for t in range(NT):
        level_part(0, t)
    for lev in range(LEVELS):
        for t in range(NT):
            if lev < LEVELS - 1:
                b, free = k.filled(dve, ("XP", lev, t))
                V_.tensor_tensor(G.X[:, t], G.X[:, t], part(b, GH, P), ALU.subtract).then_inc(free, 1)
                k.filled(dve, ("P", lev, t))
                level_part(lev + 1, t)
            b, free = k.filled(dve, ("PX", lev, t))
            V_.tensor_tensor(G.XT[:, t], G.XT[:, t], part(b, GH, P), ALU.subtract).then_inc(free, 1)
            if lev < LEVELS - 1:
                k.evacuated(dve, ("XP", lev, t))
            k.evacuated(dve, ("PX", lev, t))
    k.evacuated(dve, ("vT", 0), ("vT", 1))
    V_.tensor_tensor(G.R[:, 0], G.v[:, 0], heads(G.beta[:, 0, :]), ALU.mult).then_inc(k.sem("r_ready"), 1)
    k.evacuated(dve, ("z", 0), ("z", 1))
    z8 = k.h[:, 0, :].rearrange("p (a n) -> p a n", n=P)
    link(V_.tensor_tensor(z8, z8, bc(k.lv("out_norm").unsqueeze(1), [P, 8, P]), ALU.mult))
    dve.wait_ge(k.sem("eg_ready"), 2)
    b, free = k.filled(dve, ("kdec",))
    V_.tensor_tensor(G.kdec, part(b, GH, P), heads(G.dk), ALU.mult).then_inc(free, 1)
    b, free = k.filled(dve, ("vn", 0))
    V_.tensor_copy(G.vn[:, 0], part(b, GH, P)).then_inc(free, 1)
    b, free = k.filled(dve, ("go", 0))
    V_.tensor_copy(G.o[:, 0], part(b, GH, P)).then_inc(free, 1)
    b, free = k.filled(dve, ("S1",))
    V_.tensor_copy(G.S1, part(b, GH, P)).then_inc(free, 1)
    b, free = k.filled(dve, ("KS",))
    V_.tensor_tensor(G.tmp, part(b, GH, P), heads(G.eg[:, 1, :]), ALU.mult).then_inc(free, 1)
    k.evacuated(dve, ("KS",))
    link(V_.tensor_tensor(G.tmp, G.v[:, 1], G.tmp, ALU.subtract))
    V_.tensor_tensor(G.R[:, 1], G.tmp, heads(G.beta[:, 1, :]), ALU.mult).then_inc(k.sem("r_ready"), 1)
    b, free = k.filled(dve, ("QS",))
    dve.wait_ge(k.sem("r_ready"), 2)
    V_.tensor_tensor(G.tmp, part(b, GH, P), heads(G.eg[:, 1, :]), ALU.mult).then_inc(free, 1)
    b, free = k.filled(dve, ("vn", 1))
    V_.tensor_copy(G.vn[:, 1], part(b, GH, P)).then_inc(free, 1)
    k.evacuated(dve, ("QS",))
    b, free = k.filled(dve, ("go", 1))
    V_.tensor_tensor(G.o[:, 1], part(b, GH, P), G.tmp, ALU.add).then_inc(free, 1)
    k.evacuated(dve, ("go", 0), ("go", 1))
    o8, sq8 = (v.rearrange("p t h n -> p (t h) n") for v in (G.o, G.gdiag))
    link(V_.tensor_tensor(sq8, o8, o8, ALU.mult))
    link(V_.tensor_reduce(G.ostat, sq8, AX.X, ALU.add))
    rstd_dve(k, dve, link, G.ostat, 1.0 / P, 5)
    link(V_.tensor_tensor(o8, o8, bc(G.ostat.unsqueeze(2), [P, 8, P]), ALU.mult))
    flat = k.h[:, 1, :]
    V_.tensor_tensor(flat, flat, k.h[:, 0, :], ALU.mult).then_inc(k.sem("go_ready"), 1)
    for t in range(NT):
        b, free = k.filled(dve, ("goT", t))
        dve.wait_ge(k.sem("go_hi"), t + 1)
        hi, lo = (v[:, 4:8, t * P:(t + 1) * P] for v in k.act2)
        V_.tensor_tensor(lo, part(b, 4, P), hi, ALU.subtract).then_inc(free, 1)


def gates_act(k, act, splits, i):
    splits.ahead(STEP["gates", i])
    for pair in range(2):
        b, free = k.filled(act, ("gates", i, pair))
        c = 4 * i + 2 * pair
        k.nc.scalar.activation(k.s(GATES_T, 24, S)[:, c:c + 2, :], part(b, 2, S), ACT.Sigmoid).then_inc(free, 1)



F_MIX, F_POOLED, F_U, F_WPOOL = 0, 2048, 4096, 5120
F_POOLMAT, F_ONEHOT, F_LNC, F_REV, F_RELB = 13136, 15200, 15584, 15968, 16352
DIST = 384


def first_attn(k):
    return Attn(k, 0, FIRST_D, 5968, 12112, 13136, 5968, 9040, [k.s(F_MIX + 4 * S, 4, S)])


def phase_first(k, dram):
    nc = k.nc
    uses = BankUses()
    norm_uses(uses, 0)
    uses.add(("dist",), 4)
    for i in range(4):
        for t in range(NT):
            uses.add(("rows", i, t), (4 + 2 * i + t) % 8)
    for g in range(4):
        uses.add(("pooled", g), g)
    for g in range(4):
        uses.add(("mixed", g), 4 + g)
    for i in range(4):
        uses.add(("flip", i), i)
    attn_uses(uses, 0)
    for v in range(2):
        for t in range(NT):
            uses.add(("wout", t, v), 2 + 2 * v + t)
    k.begin(uses)
    bias = k.h[:, :, :].rearrange("p t (a n) -> p (t a) n", n=2 * P)
    pooled, mixT = k.s(F_POOLED, 4, S), k.s(F_MIX, KC, S)
    poolmat, u_rows, w_pool = k.s(F_POOLMAT, 4, NT, S), k.s(F_U, NT, 4, P), k.s(F_WPOOL, 4, P)
    onehot, lnc, rev = (k.s(a, DIST) for a in (F_ONEHOT, F_LNC, F_REV))
    relb = k.s(F_RELB, H)
    a = first_attn(k)

    with nc.Block() as block:
        @block.sync
        def _(sp):
            sp.dma_start(k.x[:, :, :], dram["x"].rearrange("o (t p) d -> p (o t) d", p=P)).then_inc(k.sem("x_loaded"), 16)
            sp.dma_start(k.const[:, :], dram["const"]).then_inc(k.sem("const_loaded"), 16)
            sp.dma_start(k.fvec[:, :], dram["fvec"]).then_inc(k.sem("fvec_loaded"), 16)
            sp.dma_start(k.s(F_ONEHOT, 1, DIST)[0:32], dram["onehot"].unsqueeze(1))\
                .then_inc(k.sem("dist_in"), 16)
            sp.dma_start(lnc[0:H, :], dram["lnc"]).then_inc(k.sem("dist_in"), 16)
            sp.dma_start(relb[0:32, :], dram["rel_bias"]).then_inc(k.sem("dist_in"), 16)
            for u in range(2):
                sp.dma_start(k.ring[u][:, :], dram["first_units"][u]).then_inc(k.arrived[u], 16)
            sp.dma_start(k.scratch[:, F_POOLMAT:F_POOLMAT + POOL_WORDS], dram["poolmat"]).then_inc(k.sem("pool_in"), 16)
            sp.dma_start(w_pool, dram["w_pool"].rearrange("o g c d -> c (o g) d")).then_inc(k.sem("pool_in"), 16)
            for u in range(2, FIRST_UNITS):
                sp.dma_start(k.ring[u][:, :], dram["first_units"][u]).then_inc(k.arrived[u], 16)
            sp.wait_ge(k.sem("rev_ready"), 1)
            sp.dma_start(dram["rev"], rev[0:H, :]).then_inc(k.sem("rev_stored"), 16)
            sp.wait_ge(k.sem("rev_stored"), 16)
            hT_written(k, sp, 0)
            base = dram["rev"]
            for h in range(H):
                src = bass.AP(base.tensor, base.offset + h * DIST, [[1, P], [1, 2 * P]])
                sp.dma_start(bias[:, h, :], src).then_inc(k.sem("bias_loaded"), 16)
            for u in range(EXPERT_UNITS):
                b, n = uses.at[("rows", u, 1) if u < 4 else ("wout", 1, u - 4)]
                sp.wait_ge(k.bank_full[b], n + 1)
                sp.dma_start(k.ring[u][:, :], dram["expert_units"][u]).then_inc(k.arrived[u], 16)

        @block.tensor
        def _(pe):
            pe.wait_ge(k.sem("const_loaded"), 16)
            norm_pe(k, pe, 0)
            b, full = k.claim(pe, ("dist",))
            pe.wait_ge(k.sem("dist_in"), 48)
            nc.tensor.matmul(b[0:H, 0:DIST], relb[0:32, :], onehot[0:32, :], start=True, stop=True).then_inc(full, 1)
            hT_written(k, pe, 0)
            for i in range(4):
                pe.wait_ge(k.arrived[i], 16)
                rows_pe(k, pe, ("rows", i), k.ring[i][:, :].rearrange("p (c n) -> p c n", c=KC), k.hT, 512)
            pe.wait_ge(k.sem("pool_in"), 32)
            k.evacuated(pe, ("rows", 3, 0), ("rows", 3, 1))
            for g in range(4):
                b, full = k.claim(pe, ("pooled", g))
                for t in range(NT):
                    last = nc.tensor.matmul(b[:, 0:S], u_rows[:, t, g, :], poolmat[:, g, t, :], start=(t == 0), stop=(t == 1))
                last.then_inc(full, 1)
            for g in range(4):
                b, full = k.claim(pe, ("mixed", g))
                k.evacuated(pe, ("pooled", g))
                nc.tensor.matmul(b[:, 0:S], w_pool[:, g, :], pooled[:, g, :], start=True, stop=True).then_inc(full, 1)
            pe.wait_ge(k.sem("bias_loaded"), 16 * H)
            for i in range(4):
                b, full = k.claim(pe, ("flip", i))
                nc.tensor.matmul(b[:, :], k.c("flip"), bias[:, 2 * i:2 * i + 2, :], start=True, stop=True).then_inc(full, 1)
            attn_pe(k, pe, a)
            attn_values_pe(k, pe, a)
            k.evacuated(pe, ("oT", 0, 0), ("oT", 0, 1), *[("mixed", g) for g in range(4)])
            for v in range(2):
                pe.wait_ge(k.arrived[4 + v], 16)
                w = k.ring[4 + v][:, :].rearrange("p (c n) -> p c n", c=KC)
                for t in range(NT):
                    b, full = k.claim(pe, ("wout", t, v))
                    for c in range(KC):
                        last = nc.tensor.matmul(b[:, :], mixT[:, c, t * P:(t + 1) * P], w[:, c, :],
                                                start=(c == 0), stop=(c == KC - 1))
                    last.then_inc(full, 1)

        @block.scalar
        def _(act):
            norm_act(k, act, 0, (k.sem("x_loaded"), 16))
            for i in range(4):
                for t in range(NT):
                    b, free = k.filled(act, ("rows", i, t))
                    to = (a.qk[:, t * H:(t + 1) * H, :], a.qk[:, (NT + t) * H:(NT + t + 1) * H, :], a.v[:, t, :, :],
                          u_rows[:, t])[i]
                    nc.scalar.copy(to, part(b, *((4, P) if i == 3 else (H, 64)))).then_inc(free, 1)
            act.wait_ge(k.sem("rev_stored"), 16)
            attn_act(k, act, a)

        @block.vector
        def _(dve):
            link = chain_of(dve, k.dve_step)
            dve.wait_ge(k.sem("fvec_loaded"), 16)
            norm_dve(k, dve, link, 0, k.f("g_mix"))
            b, free = k.filled(dve, ("dist",))
            nc.vector.tensor_tensor(rev[0:H, :], b[0:H, 0:DIST], lnc[0:H, :], ALU.add).then_inc(free, 1)
            k.evacuated(dve, ("dist",))
            nc.vector.tensor_copy(k.s(STATS, 1), k.s(STATS, 1)).then_inc(k.sem("rev_ready"), 1)
            for g in range(4):
                b, free = k.filled(dve, ("pooled", g))
                nc.vector.tensor_copy(pooled[:, g, :], b[:, 0:S]).then_inc(free, 1)
            for g in range(4):
                b, free = k.filled(dve, ("mixed", g))
                nc.vector.tensor_scalar(mixT[:, g, :], b[:, 0:S], k.f("pool_scale")[:, g:g + 1], None, ALU.mult).then_inc(free, 1)
            k.evacuated(dve, *[("rows", i, t) for i in range(2) for t in range(NT)])
            nc.vector.memset(k.s(STATS + 4, 1), 0.0).then_inc(k.sem("qk_ready"), 1)
            for i in range(4):
                b, free = k.filled(dve, ("flip", i))
                nc.vector.tensor_copy(bias[:, 2 * i:2 * i + 2, :], part(b, 2, 2 * P)).then_inc(free, 1)
            k.evacuated(dve, *[("flip", i) for i in range(4)])
            attn_dve(k, dve, link, a, FIRST_D ** -0.5,
                     lambda t, pair: bias[:, 2 * pair:2 * pair + 2, (1 - t) * P:2 * P])
            for v in range(2):
                for t in range(NT):
                    b, free = k.filled(dve, ("wout", t, v))
                    x = k.x[:, t, v * 512:(v + 1) * 512]
                    nc.vector.tensor_tensor(x, b[:, :], x, ALU.add).then_inc(free, 1)
    k.end_phase()



SL = 64
ROUNDS = S // SL
M_XSEL, M_ACT, M_ROWS, M_GU, M_SIG, M_Y = 0, 512, 1024, 2048, 3072, 3584
M_SEL, M_GSEL, M_GSELT, M_ZERO, M_RANK, M_GATE = 4096, 4352, 4608, 4864, 4992, 5250
M_BGU, M_BDOWN, M_ROUTE = 5508, 7556, 8580
LIMIT, ALPHA = 7.0, 1.702
TURNS = ROUNDS * E + 1
BIG = 1e30


def phase_moe(k, dram):
    nc = k.nc
    uses = BankUses()
    norm_uses(uses, 0)
    for t in range(NT):
        uses.add(("logits", t), t)
    for t in range(NT):
        uses.add(("rank", t), 2 + t)
    uses.add(("count",), 0)
    uses.add(("gateT",), 1)
    for t in range(NT):
        for v in range(2):
            uses.add(("acc", t, v), 4 + 2 * t + v)
    for half in range(2):
        uses.add(("gather", half), half)
    base = list(uses.count)
    turn = BankUses()
    for key, b in ((("rows", 0), 0), (("gu", 0), 2), (("rows", 1), 1), (("gather", 0), 0), (("gu", 1), 3),
                   (("gather", 1), 1), (("selT",), 2), (("y",), 3)):
        turn.add(key, b)
    k.begin(uses)

    def turn_claim(pe, key, it):
        b, n = turn.at[key]
        pe.wait_ge(k.bank_free[b], it * turn.count[b] + (base[b] + n))
        return k.bank[b], k.bank_full[b]

    def turn_filled(eng, key, it):
        b, n = turn.at[key]
        eng.wait_ge(k.bank_full[b], it * turn.count[b] + (base[b] + n + 1))
        return k.bank[b], k.bank_free[b]

    def turn_evacuated(eng, key, it):
        b, n = turn.at[key]
        eng.wait_ge(k.bank_free[b], it * turn.count[b] + (base[b] + n + 1))

    xsel, acts, rows, gu = k.s(M_XSEL, KC, SL), k.s(M_ACT, KC, SL), k.s(M_ROWS, 2, 512), k.s(M_GU, 2, 4, P)
    sig, y, sel, gsel, gselT = k.s(M_SIG, 2, 4, SL), k.s(M_Y, 512), k.s(M_SEL, NT, P), k.s(M_GSEL, NT, P), k.s(M_GSELT, NT, P)
    rank, gate, bgu = k.s(M_RANK, NT, TURNS), k.s(M_GATE, NT, TURNS), k.s(M_BGU, ROUNDS * E, 16)
    b_down, zero = k.s(M_BDOWN, D), k.s(M_ZERO, P)
    small = lambda at, *shape: k.s(M_ROUTE + at, *shape)
    logits, left, eq, score, onehot, chosen, ex, raw = (small(64 * i, NT, E) for i in range(8))
    order, m, first, top, den = small(512, E), small(544, NT), small(546, NT), small(548, NT), small(550, NT)
    count, gateT, more = small(552, 1), small(560, NT, P), small(556, ROUNDS)
    turns_i = small(553, 1).bitcast(I32)
    wide = lambda ap: bc(ap.unsqueeze(2), [P, NT, E])

    def turns_of(eng):
        eng.wait_ge(k.sem("turns_ready"), 1)
        return eng.value_load(turns_i[0:1, 0:1], min_val=E, max_val=ROUNDS * E)

    with nc.Block() as block:
        @block.sync
        def _(sp):
            for r in range(ROUNDS):
                sp.dma_start(bgu[:, r * E:(r + 1) * E, :], dram["b_gu"]).then_inc(k.sem("b_loaded"), 16)
            sp.dma_start(b_down[0:E, :], dram["b_down"].rearrange("o e d -> (o e) d")).then_inc(k.sem("b_loaded"), 16)
            turns = turns_of(sp)
            with sp.Fori(0, turns - 1) as it:
                for u in range(EXPERT_UNITS):
                    turn_filled(sp, (("rows", 0), ("rows", 1), ("y",))[u // 2], it)
                    sp.sem_inc(k.sem("unit_released"), 1)
                    nxt = ((it + 1) & (E - 1)) * EXPERT_UNITS + u
                    sp.dma_start(k.ring[u][:, :], dram["expert_units"][bass.ds(nxt, 1)].rearrange("o p n -> (o p) n"))\
                        .then_inc(k.arrived[u], 16)

        @block.tensor
        def _(pe):
            norm_pe(k, pe, 0)
            hT_written(k, pe, 0)
            w_router = k.f("w_router").rearrange("p (c e) -> p c e", c=KC)
            rows_pe(k, pe, ("logits",), w_router, k.hT, E)
            pe.wait_ge(k.sem("chosen_ready"), 1)
            for t in range(NT):
                b, full = k.claim(pe, ("rank", t))
                last = nc.tensor.matmul(b[:, 0:E], k.c("tri_strict"), chosen[:, t, :], start=True, stop=(t == 0))
                if t == 1:
                    last = nc.tensor.matmul(b[:, 0:E], k.c("ones"), chosen[:, 0, :], start=False, stop=True)
                last.then_inc(full, 1)
            b, full = k.claim(pe, ("count",))
            for t in range(NT):
                last = nc.tensor.matmul(b[:, 0:E], k.c("ones"), chosen[:, t, :], start=(t == 0), stop=(t == 1))
            last.then_inc(full, 1)
            b, full = k.claim(pe, ("gateT",))
            pe.wait_ge(k.sem("gate_ready"), 1)
            for t in range(NT):
                last = nc.tensor.transpose(b[0:E, t * P:(t + 1) * P], gate[:, t, 0:E], k.c("ident"))
            last.then_inc(full, 1)
            pe.wait_ge(k.sem("b_loaded"), 16 * (ROUNDS + 1))
            k.evacuated(pe, ("gateT",))
            for t in range(NT):
                for v in range(2):
                    b, full = k.claim(pe, ("acc", t, v))
                    nc.tensor.matmul(b[:, :], gateT[0:E, t, :], b_down[0:E, v * 512:(v + 1) * 512], start=True, stop=False)

            def gather(banks, first=0):
                for half, (b, full) in enumerate(banks, first):
                    for j in range(4):
                        c = 4 * half + j
                        for t in range(NT):
                            last = nc.tensor.matmul(b[:, j * P:(j + 1) * P], k.h[:, t, c * P:(c + 1) * P], sel[:, t, :],
                                                    start=(t == 0), stop=(t == 1))
                    last.then_inc(full, 1)

            pe.wait_ge(k.sem("sel_ready"), 1)
            gather([k.claim(pe, ("gather", half)) for half in range(2)])
            turns = turns_of(pe)

            def product(u, it, b, lhsT, start, stop):
                pe.wait_ge(k.arrived[u], (it + 2) * 16)
                w = k.ring[u][:, :].rearrange("p (c g n) -> p c g n", c=4, g=2)
                for c in range(4):
                    for g in range(2):
                        last = nc.tensor.matmul(b[g * SL:(g + 1) * SL, :], lhsT[:, c, :], w[:, c, g, :],
                                                start=start and c == 0, stop=stop and c == 3)
                return last

            def scatter():
                for t in range(NT):
                    for v in range(2):
                        half = slice(v * SL, (v + 1) * SL)
                        nc.tensor.matmul(k.bank[4 + 2 * t + v][:, :], gselT[half, t, :], y[half, :], start=False, stop=False)

            def transposed(half, it):
                b, full = turn_claim(pe, ("gu", half), it)
                turn_evacuated(pe, ("rows", half), it)
                for j in range(4):
                    last = nc.tensor.transpose(b[:, j * P:(j + 1) * P], rows[:, half, j * P:(j + 1) * P], k.c("ident"))
                last.then_inc(full, 1)

            pe.wait_ge(k.sem("nothing_ready"), 2)
            with pe.Fori(0, turns) as it:
                for half in range(2):
                    pe.wait_ge(k.bank_free[half], it * turn.count[half] + base[half])
                b, full = turn_claim(pe, ("rows", 0), it)
                product(0, it, b, xsel[:, 0:4, :], True, False)
                product(1, it, b, xsel[:, 4:8, :], False, True).then_inc(full, 1)
                for bk in (2, 3):
                    pe.wait_ge(k.bank_free[bk], it * turn.count[bk] + base[bk])
                scatter()
                b, full = turn_claim(pe, ("rows", 1), it)
                product(2, it, b, xsel[:, 0:4, :], True, False)
                transposed(0, it)
                product(3, it, b, xsel[:, 4:8, :], False, True).then_inc(full, 1)
                pe.wait_ge(k.sem("sel_ready"), it + 2)
                gather([turn_claim(pe, ("gather", 0), it)], 0)
                transposed(1, it)
                gather([turn_claim(pe, ("gather", 1), it)], 1)
                pe.wait_ge(k.sem("gsel_ready"), it + 1)
                b, full = turn_claim(pe, ("selT",), it)
                for t in range(NT):
                    last = nc.tensor.transpose(b[:, t * P:(t + 1) * P], gsel[:, t, :], k.c("ident"))
                last.then_inc(full, 1)
                b, full = turn_claim(pe, ("y",), it)
                pe.wait_ge(k.sem("act_ready"), it * 2 + 1)
                product(4, it, b, acts[:, 0:4, :], True, False)
                pe.wait_ge(k.sem("act_ready"), it * 2 + 2)
                product(5, it, b, acts[:, 4:8, :], False, True).then_inc(full, 1)
            for bk in (2, 3):
                pe.wait_ge(k.bank_free[bk], turns * turn.count[bk] + base[bk])
            scatter()
            pe.wait_ge(k.sem("zero_ready"), 1)
            for t in range(NT):
                for v in range(2):
                    nc.tensor.matmul(k.bank[4 + 2 * t + v][:, :], zero[0:E, :], b_down[0:E, v * 512:(v + 1) * 512], start=False, stop=True)\
                        .then_inc(k.bank_full[4 + 2 * t + v], 1)

        @block.scalar
        def _(act):
            norm_act(k, act, 0)
            act.wait_ge(k.sem("centred"), 1)
            nc.scalar.activation(ex, ex, ACT.Exp).then_inc(k.sem("exp_ready"), 1)
            b, free = k.filled(act, ("gateT",))
            nc.scalar.copy(gateT[0:E], part(b, NT, P)[0:E]).then_inc(free, 1)
            turns = turns_of(act)
            with act.Fori(0, turns) as it:
                for half in range(2):
                    b, free = turn_filled(act, ("rows", half), it)
                    nc.scalar.copy(rows[:, half, :], b[:, :]).then_inc(free, 1)
                    act.wait_ge(k.sem("clamped"), it * 2 + (half + 1))
                    nc.scalar.activation(sig[:, half], gu[:, half, :, 0:SL], ACT.Sigmoid, scale=ALPHA)\
                        .then_inc(k.sem("sig_ready"), 1)
                b, free = turn_filled(act, ("selT",), it)
                nc.scalar.copy(gselT, part(b, NT, P)).then_inc(free, 1)
                b, free = turn_filled(act, ("y",), it)
                nc.scalar.copy(y, b[:, :]).then_inc(free, 1)

        @block.vector
        def _(dve):
            V_ = nc.vector
            link = chain_of(dve, k.dve_step)
            gain = k.f("g_ffn")
            norm_dve(k, dve, link, 0, gain)
            V_.memset(zero, 0.0).then_inc(k.sem("zero_ready"), 1)
            V_.memset(y, 0.0).then_inc(k.sem("nothing_ready"), 1)
            V_.memset(gselT, 0.0).then_inc(k.sem("nothing_ready"), 1)
            V_.memset(rank[:, :, ROUNDS * E:], -1000.0)
            V_.memset(gate[:, :, ROUNDS * E:], 0.0)
            V_.memset(chosen, 0.0)
            V_.tensor_scalar(order, k.c("iota")[:, 0:E], -1.0, float(E), ALU.mult, ALU.add)
            for t in range(NT):
                b, free = k.filled(dve, ("logits", t))
                V_.tensor_tensor(logits[:, t, :], b[:, 0:E], k.f("b_router"), ALU.add).then_inc(free, 1)
            k.evacuated(dve, ("logits", 0), ("logits", 1))
            link(V_.tensor_copy(left, logits))
            for r in range(TOPK):
                m_r = top if r == 0 else m
                link(V_.tensor_reduce(m_r, left, AX.X, ALU.max))
                link(V_.tensor_tensor(eq, left, wide(m_r), ALU.is_equal))
                link(V_.tensor_tensor(score, eq, bc(order.unsqueeze(1), [P, NT, E]), ALU.mult))
                link(V_.tensor_reduce(first, score, AX.X, ALU.max))
                link(V_.tensor_tensor(onehot, score, wide(first), ALU.is_equal))
                link(V_.scalar_tensor_tensor(out=left, in0=onehot, scalar=-BIG, in1=left, op0=ALU.mult, op1=ALU.add))
                ins = V_.tensor_tensor(chosen, chosen, onehot, ALU.add)
                if r < TOPK - 1:
                    link(ins)
                else:
                    ins.then_inc(k.sem("chosen_ready"), 1)
            V_.tensor_tensor(ex, logits, wide(top), ALU.subtract).then_inc(k.sem("centred"), 1)
            dve.wait_ge(k.sem("exp_ready"), 1)
            link(V_.tensor_tensor(ex, ex, chosen, ALU.mult))
            link(V_.tensor_reduce(den, ex, AX.X, ALU.add))
            link(V_.reciprocal(den, den))
            for r in range(ROUNDS):
                ins = V_.tensor_tensor(gate[:, :, r * E:(r + 1) * E], ex, wide(den), ALU.mult)
            ins.then_inc(k.sem("gate_ready"), 1)
            for t in range(NT):
                b, free = k.filled(dve, ("rank", t))
                V_.scalar_tensor_tensor(out=raw[:, t, :], in0=b[:, 0:E], scalar=1000.0, in1=chosen[:, t, :],
                                        op0=ALU.add, op1=ALU.mult).then_inc(free, 1)
            k.evacuated(dve, ("rank", 0), ("rank", 1))
            for r in range(ROUNDS):
                ins = V_.tensor_scalar(rank[:, :, r * E:(r + 1) * E], raw, -1000.0 - SL * r, None, ALU.add)
            link(ins)
            b, free = k.filled(dve, ("count",))
            V_.tensor_reduce(count, b[:, 0:E], AX.X, ALU.max).then_inc(free, 1)
            k.evacuated(dve, ("count",))
            for r in range(1, ROUNDS):
                V_.tensor_scalar(more[:, r - 1:r], count, float(SL * r), float(E), ALU.is_gt, ALU.mult)
            link(V_.memset(more[:, ROUNDS - 1:], float(E)))
            link(V_.tensor_reduce(count, more, AX.X, ALU.add))
            V_.tensor_copy(turns_i, count).then_inc(k.sem("turns_ready"), 1)
            dve.wait_ge(k.sem("gate_ready"), 1)

            def select(out, col, gated, done):
                for t in range(NT):
                    g = gate[:, t, col] if gated else None
                    ins = V_.tensor_scalar(out[:, t, :], k.c("slot"), rank[:, t, col], g, ALU.is_equal,
                                           *((ALU.mult,) if gated else ()))
                ins.then_inc(k.sem(done), 1)

            def take(half, b, free):
                V_.tensor_tensor(xsel[:, 4 * half:4 * half + 4, :], part(b, 4, P)[:, :, 0:SL],
                                 bc(gain[:, 4 * half:4 * half + 4].unsqueeze(2), [P, 4, SL]), ALU.mult).then_inc(free, 1)

            select(sel, slice(0, 1), False, "sel_ready")
            for half in range(2):
                take(half, *k.filled(dve, ("gather", half)))
            dve.wait_ge(k.sem("b_loaded"), 16 * (ROUNDS + 1))
            turns = turns_of(dve)
            with dve.Fori(0, turns) as it:
                b, _n = turn.at[("selT",)]
                dve.wait_ge(k.bank_full[b], it * turn.count[b] + base[b])
                select(gsel, bass.ds(it, 1), True, "gsel_ready")
                select(sel, bass.ds(it + 1, 1), False, "sel_ready")

                bias = bgu[:, bass.ds(it, 1), :].rearrange("p o (h j g) -> p (o h) j g", h=2, g=2)
                step = k.sem("swiglu_step")
                for half in range(2):
                    b, free = turn_filled(dve, ("gu", half), it)
                    both = gu[:, half].rearrange("p j (g n) -> p (j g) n", g=2)
                    wide_bias = bias[:, half].rearrange("p j g -> p (j g)").unsqueeze(2)
                    V_.tensor_tensor(both, b[:, :].rearrange("p (a n) -> p a n", n=SL), bc(wide_bias, [P, 8, SL]), ALU.add)\
                        .then_inc(free, 1)
                    turn_evacuated(dve, ("gu", half), it)
                    V_.tensor_scalar(both, both, LIMIT, None, ALU.min).then_inc(k.sem("clamped"), 1)
                    dve.wait_ge(k.sem("clamped"), it * 2 + (half + 1))
                    g, up = gu[:, half, :, 0:SL], gu[:, half, :, SL:P]
                    V_.tensor_scalar(up, up, -LIMIT, 1.0, ALU.max, ALU.add).then_inc(step, 1)
                    dve.wait_ge(step, it * 4 + (2 * half + 1))
                    V_.tensor_tensor(up, up, g, ALU.mult).then_inc(step, 1)
                    dve.wait_ge(step, it * 4 + (2 * half + 2))
                    dve.wait_ge(k.sem("sig_ready"), it * 2 + (half + 1))
                    V_.tensor_tensor(acts[:, 4 * half:4 * half + 4, :], up, sig[:, half], ALU.mult).then_inc(k.sem("act_ready"), 1)
                    take(half, *turn_filled(dve, ("gather", half), it))
                dve.wait_ge(k.sem("act_ready"), it * 2 + 2)
            for t in range(NT):
                for v in range(2):
                    b, free = k.filled(dve, ("acc", t, v))
                    x = k.x[:, t, v * 512:(v + 1) * 512]
                    V_.tensor_tensor(x, b[:, :], x, ALU.add).then_inc(free, 1)
    k.end_phase()



def phase_ple(k, dram):
    nc = k.nc
    uses = BankUses()
    norm_uses(uses, 0)
    for v in range(2):
        for t in range(NT):
            uses.add(("pgate", v, t), 2 * v + t)
    for v in range(2):
        for t in range(NT):
            uses.add(("proj", v, t), 4 + 2 * v + t)
    k.begin(uses)
    sg, tmp, pT, g_final = k.s(0, NT, D), k.s(2048, 4, 512), k.s(4096, 2, S), k.s(4608, D)

    with nc.Block() as block:
        @block.sync
        def _(sp):
            for u in range(PLE_UNITS):
                w = PLE_WORDS[u]
                sp.dma_start(k.ring[u][:, 0:w], dram["ple_units"][u, :, 0:w]).then_inc(k.later_arrived[u], 16)
            sp.dma_start(pT, dram["pT"].rearrange("(c p) n -> p c n", p=P)).then_inc(k.sem("p_loaded"), 16)
            sp.dma_start(g_final, dram["g_final"]).then_inc(k.sem("p_loaded"), 16)

        @block.tensor
        def _(pe):
            norm_pe(k, pe, 0)
            hT_written(k, pe, 0)
            for v in range(2):
                pe.wait_ge(k.later_arrived[v], 16)
                rows_pe(k, pe, ("pgate", v), k.ring[v][:, :].rearrange("p (c n) -> p c n", c=KC), k.hT, 512)
            pe.wait_ge(k.later_arrived[2], 16)
            pe.wait_ge(k.sem("p_loaded"), 32)
            w = k.ring[2][:, 0:PLE_WORDS[2]].rearrange("p (c n) -> p c n", c=2)
            for v in range(2):
                rows_pe(k, pe, ("proj", v), w[:, :, v * 512:(v + 1) * 512], pT, 512, chunks=2)

        @block.scalar
        def _(act):
            norm_act(k, act, 0)
            for v in range(2):
                for t in range(NT):
                    b, free = k.filled(act, ("pgate", v, t))
                    nc.scalar.activation(sg[:, t, v * 512:(v + 1) * 512], b[:, :], ACT.Sigmoid).then_inc(free, 1)
            for t in range(NT):
                act.wait_ge(k.sem("x_updated"), NT * 2)
                nc.scalar.activation(k.h[:, t, :], k.x[:, t, :], ACT.Square, accum_out=k.s(STATS + 8 + t, 1))\
                    .then_inc(k.sem("last_ss"), 1)
            rstd_act(k, act, k.s(STATS + 8, NT), 1)

        @block.vector
        def _(dve):
            link = chain_of(dve, k.dve_step)
            norm_dve(k, dve, link, 0, k.f("g_ple"))
            for v in range(2):
                for t in range(NT):
                    b, free = k.filled(dve, ("proj", v, t))
                    k.evacuated(dve, ("pgate", v, t))
                    s = tmp[:, 2 * v + t, :]
                    nc.vector.tensor_tensor(s, b[:, :], sg[:, t, v * 512:(v + 1) * 512], ALU.mult).then_inc(free, 1)
                    k.evacuated(dve, ("proj", v, t))
                    x = k.x[:, t, v * 512:(v + 1) * 512]
                    nc.vector.tensor_tensor(x, x, s, ALU.add).then_inc(k.sem("x_updated"), 1)
            dve.wait_ge(k.sem("last_ss"), 2)
            st = k.s(STATS + 8, NT)
            rstd_dve(k, dve, link, st, 1.0 / D, 1)
            for t in range(NT):
                nc.vector.scalar_tensor_tensor(out=k.x[:, t, :], in0=k.x[:, t, :], scalar=st[:, t:t + 1], in1=g_final,
                                               op0=ALU.mult, op1=ALU.mult)
    k.end_phase()




def branch_uses(uses, n, bank):
    for dp in range(4):
        uses.add(("branch", n, dp), bank + dp)


def branch_pe(k, pe, n):
    banks = [k.claim(pe, ("branch", n, dp)) for dp in range(4)]
    for h, last_half, w in weights(k, pe, ("branch", n), D):
        for dp, (b, full) in enumerate(banks):
            for j in range(2):
                col = (2 * dp + j) * P
                for c in range(2):
                    last = mm3(k.nc, b[:, j * S:(j + 1) * S], [v[:, c, col:col + P] for v in w],
                               [v[:, 4 * n + 2 * h + c, :] for v in k.act2],
                               start=(h == 0 and j == 0 and c == 0), stop=(last_half and j == 1 and c == 1))
            if last_half:
                last.then_inc(full, 1)
        if not last_half:
            last.then_inc(k.sem("half_used"), 1)


def branch_dve(k, dve, n):
    gatesT = k.s(GATES_T, 24, S)
    k.evacuated(dve, *[("gates", i, pair) for i in (2 * n, 2 * n + 1) for pair in range(2)])
    for dp in range(4):
        b, free = k.filled(dve, ("branch", n, dp))
        g = gatesT[:, 8 * n + 2 * dp:8 * n + 2 * dp + 2, :]
        k.nc.vector.tensor_tensor(g, part(b, 2, S), g, ALU.mult).then_inc(free, 1)


def layer_uses():
    uses = BankUses()
    gates = lambda i: [uses.add(("gates", i, pair), (2 * i + pair) % 4) for pair in range(2)]
    norm_uses(uses, 0)
    ffn_uses(uses, 0)
    norm_uses(uses, 1)
    for t in range(NT):
        uses.add(("mla", t), 4 + t)
    gates(0)
    for t in range(NT):
        uses.add(("cT", t), 6 + t)
    for t in range(NT):
        for i in range(2):
            uses.add(("q", t, i), 4 * t + i)
    for t in range(NT):
        for i in range(2):
            uses.add(("kv", t, i), 4 * t + 2 + i)
    gates(1)
    gates(2)
    attn_uses(uses, 0)
    for i in range(3):
        for t in range(NT):
            uses.add(("moba", i, t), 2 + 2 * i + t)
    gates(3)
    gates(4)
    branch_uses(uses, 0, 4)
    attn_uses(uses, 1)
    gdn_uses(uses)
    branch_uses(uses, 1, 4)
    for v in range(2):
        for t in range(NT):
            uses.add(("wout", t, v), 2 * v + t)
    norm_uses(uses, 2, (4, 5, 6, 7))
    ffn_uses(uses, 1)
    return uses


def layer_attn(k, n):
    out = [v[:, 8 * n:8 * n + 4, :] for v in k.act2]
    return Attn(k, n, (MLA_D, MOBA_D)[n], WORK, V_ROWS, QKT, WORK, QKT, out)


def layer_body(k, dram, layer):
    nc = k.nc
    k.begin(layer_uses())
    rows = k.s(MLA_ROWS, NT, MLA_COLS)
    cn = k.h[:, 0, 0:NT * 384].rearrange("p (t n) -> p t n", t=NT)
    cT = [v[:, 4:7, :] for v in k.act2]
    gatesT, comb = k.s(GATES_T, 24, S), k.s(COMB, KC, S)
    mla, moba = layer_attn(k, 0), layer_attn(k, 1)
    causal = k.c("causal")

    with nc.Block() as block:
        @block.sync
        def _(sp):
            sp.dma_start(k.lvec[:, :], dram["lvec"][bass.ds(layer, 1)].rearrange("o p n -> (o p) n")).then_inc(k.sem("lvec_loaded"), 16)
            for i, (step, at, _words) in enumerate(HALVES):
                for n, part_at in pieces(i):
                    if n >= RAW_SLOTS:
                        sp.wait_ge(k.sem("weights_split"), n - RAW_SLOTS + 1)
                    a, b = at + part_at.start, at + part_at.stop
                    sp.dma_start(k.raw[n % RAW_SLOTS][:, 0:b - a],
                                 dram["layer_units"][bass.ds(layer * LAYER_UNITS + step, 1), :, a:b].rearrange("o p n -> (o p) n"))\
                        .then_inc(k.later_arrived[n % RAW_SLOTS], 16)

        @block.tensor
        def _(pe):
            gates = lambda i: columns_pe(k, pe, ("gates", i), [("gates", i, pair) for pair in range(2)])
            norm_pe(k, pe, 0)
            ffn_pe(k, pe, 0)
            norm_pe(k, pe, 1)
            rows3_pe(k, pe, ("mla", 0), [("mla", t) for t in range(NT)], k.hT2, MLA_COLS,
                     lambda h: hT_written(k, pe, 1, (h,)))
            gates(0)
            pe.wait_ge(k.sem("c_ready"), 1)
            for t in range(NT):
                b, full = k.claim(pe, ("cT", t))
                for c in range(3):
                    last = nc.tensor.transpose(b[:, c * P:(c + 1) * P], cn[:, t, c * P:(c + 1) * P], k.c("ident"))
                last.then_inc(full, 1)
            k.evacuated(pe, ("cT", 0), ("cT", 1))
            for h, _last, w in weights(k, pe, ("up_proj", 0), 256):
                for t in range(NT):
                    for i in range(2):
                        b, full = k.claim(pe, (("q", "kv")[h], t, i))
                        n = (384, 512)[h]
                        chunks = (0, 1) if h == 0 else (2,)
                        for c in chunks:
                            at = (c * 768 if h == 0 else 0) + i * n
                            flat = [v.rearrange("p a b -> p (a b)")[:, at:at + n] for v in w]
                            last = mm3(nc, b[:, 0:n], [v[:, c, t * P:(t + 1) * P] for v in cT], flat,
                                       start=(c == chunks[0]), stop=(c == chunks[-1]))
                        last.then_inc(full, 1)
            gates(1)
            gates(2)
            attn_pe(k, pe, mla)
            attn_values_pe(k, pe, mla)
            for i in range(3):
                rows3_pe(k, pe, ("moba", i), [("moba", i, t) for t in range(NT)], k.hT2, 512)
            gates(3)
            gates(4)
            k.evacuated(pe, ("oT", 0, 0), ("oT", 0, 1))
            branch_pe(k, pe, 0)
            attn_pe(k, pe, moba)
            attn_values_pe(k, pe, moba)
            for i in range(3):
                columns_pe(k, pe, ("gdn", i), [("raw", i, pair) for pair in range(2)])
            rows3_pe(k, pe, ("z", 0), [("z", t) for t in range(NT)], k.hT2, 512)
            gates(5)
            gdn_pe(k, pe)
            k.evacuated(pe, ("goT", 0), ("goT", 1))
            branch_pe(k, pe, 1)
            for v in range(2):
                rows3_pe(k, pe, ("wout", v), [("wout", t, v) for t in range(NT)], k.hT2, 512,
                         lambda h: pe.wait_ge(k.sem("comb_ready"), 2 * h + 2))
            norm_pe(k, pe, 2)
            ffn_pe(k, pe, 1)

        @block.scalar
        def _(act):
            splits = Splits(k, act, hi_act)
            act.wait_ge(k.sem("lvec_loaded"), 16)
            norm_act(k, act, 0)
            for i in range(SPLIT_SLOTS):
                hi_act(k, act, i)
            splits.done = SPLIT_SLOTS
            ffn_act(k, act, 0, splits)
            k.evacuated(act, *[("ffn_out", 0, t, v) for t in range(NT) for v in range(2)])
            norm_act(k, act, 1, power=1)
            splits.ahead(STEP["mla", 0])
            for t in range(NT):
                b, free = k.filled(act, ("mla", t))
                nc.scalar.copy(rows[:, t, :], b[:, 0:MLA_COLS]).then_inc(free, 1)
            rstd_act(k, act, k.s(STATS + 192, 2, NT), 2)
            gates_act(k, act, splits, 0)
            splits.ahead(STEP["up_proj", 0])
            for t in range(NT):
                for i in range(2):
                    b, free = k.filled(act, ("q", t, i))
                    nc.scalar.copy(mla.qk[:, t * H + 4 * i:t * H + 4 * i + 4, :], part(b, 4, MLA_D)).then_inc(free, 1)
            for t in range(NT):
                for i in range(2):
                    b, free = k.filled(act, ("kv", t, i))
                    r = (NT + t) * H + 4 * i
                    nc.scalar.copy(mla.qk[:, r:r + 4, 0:64], part(b, 4, P)[:, :, 0:64])
                    nc.scalar.copy(mla.v[:, t, 4 * i:4 * i + 4, :], part(b, 4, P)[:, :, 64:P]).then_inc(free, 1)
            splits.ahead(STEP["gates", 1])
            rstd_act(k, act, k.s(STATS + 128, 2 * NT * H), 3)
            gates_act(k, act, splits, 1)
            gates_act(k, act, splits, 2)
            attn_act(k, act, mla)
            for i in range(3):
                splits.ahead(STEP["moba", i])
                for t in range(NT):
                    b, free = k.filled(act, ("moba", i, t))
                    to = moba.v[:, t] if i == 2 else moba.qk[:, (i * NT + t) * H:(i * NT + t + 1) * H, :]
                    nc.scalar.copy(to, part(b, H, 64)).then_inc(free, 1)
            splits.ahead(STEP["gates", 3])
            rstd_act(k, act, k.s(STATS + 128, 2 * NT * H), 4)
            gates_act(k, act, splits, 3)
            gates_act(k, act, splits, 4)
            splits.ahead(STEP["branch", 0])
            attn_act(k, act, moba)
            gdn_act(k, act, splits)
            splits.ahead(STEP["branch", 1])
            for dp in range(4):
                act.wait_ge(k.sem("comb_sum"), dp + 1)
                nc.scalar.copy(k.hT2[0][:, 2 * dp:2 * dp + 2, :], comb[:, 2 * dp:2 * dp + 2, :]).then_inc(k.sem("comb_hi"), 1)
            for v in range(2):
                splits.ahead(STEP["wout", v])
            k.evacuated(act, *[("wout", t, v) for t in range(NT) for v in range(2)])
            norm_act(k, act, 2, power=6)
            ffn_act(k, act, 1, splits)

        @block.vector
        def _(dve):
            V_ = nc.vector
            link = chain_of(dve, k.dve_step)
            dve.wait_ge(k.sem("lvec_loaded"), 16)
            norm2_dve(k, dve, link, 0, k.lv("g_ffa"), 0)
            ffn_dve(k, dve, 0)
            norm2_dve(k, dve, link, 1, k.lv("g_mix"), 1)
            k.evacuated(dve, ("mla", 0), ("mla", 1))
            sq, st = k.s(QKT, NT, 384), k.s(STATS + 192, 2, NT)
            lat = rows[:, :, 0:384]
            link(V_.tensor_tensor(sq, lat, lat, ALU.mult))
            V_.tensor_reduce(st[:, 0, :], sq[:, :, 0:256], AX.X, ALU.add)
            link(V_.tensor_reduce(st[:, 1, :], sq[:, :, 256:384], AX.X, ALU.add))
            link(V_.tensor_scalar(st[:, 1, :], st[:, 1, :], 2.0, None, ALU.mult))
            rstd_dve(k, dve, link, st, 1.0 / 256, 2)
            for t in range(NT):
                for i, (c0, c1) in enumerate(((0, 256), (256, 384))):
                    ins = V_.tensor_scalar(cn[:, t, c0:c1], rows[:, t, c0:c1], st[:, i, t:t + 1], None, ALU.mult)
            ins.then_inc(k.sem("c_ready"), 1)
            gain = k.lv("c_norm")
            for t in range(NT):
                b, free = k.filled(dve, ("cT", t))
                cols = slice(t * P, (t + 1) * P)
                link(V_.tensor_tensor(cT[0][:, :, cols], part(b, 3, P), bc(gain.unsqueeze(2), [P, 3, P]), ALU.mult))
                for c in range(3):
                    ins = V_.scalar_tensor_tensor(out=cT[1][:, c, cols], in0=b[:, c * P:(c + 1) * P], scalar=gain[:, c:c + 1],
                                                  in1=cT[0][:, c, cols], op0=ALU.mult, op1=ALU.subtract)
                ins.then_inc(free, 1)
            for t in range(NT):
                r = (NT + t) * H
                V_.tensor_copy(mla.qk[:, r:r + H, 64:96], bc(rows[:, t, 384:416].unsqueeze(1), [P, H, 32]))\
                    .then_inc(k.sem("k_rope"), 1)
            dve.wait_ge(k.sem("k_rope"), 2)
            k.evacuated(dve, *[(x, t, i) for t in range(NT) for x in ("q", "kv") for i in range(2)])
            head_norm_dve(k, dve, link, mla.qk, k.s(QKT, 32, MLA_D), MLA_D, (k.lv("q_norm"), k.lv("k_norm")), 3)
            rope_dve(k, dve, link, mla.qk, QKT, 64, 16, k.c("cos16"), k.c("sin16"), k.sem("qk_ready"))
            mask = lambda t, pair: bc(causal[:, (1 - t) * P:2 * P].unsqueeze(1), [P, 2, (t + 1) * P])
            attn_dve(k, dve, link, mla, MLA_D ** -0.5, mask)
            k.evacuated(dve, *[("moba", i, t) for i in range(3) for t in range(NT)])
            head_norm_dve(k, dve, link, moba.qk, k.s(QKT, 32, MOBA_D), MOBA_D, (k.lv("moba_q"), k.lv("moba_k")), 4)
            rope_dve(k, dve, link, moba.qk, QKT, 0, 32, k.c("cos32"), k.c("sin32"), k.sem("qk_ready"))
            branch_dve(k, dve, 0)
            attn_dve(k, dve, link, moba, MOBA_D ** -0.5, mask)
            gdn_dve(k, dve, link)
            branches = gatesT.rearrange("p (n c) s -> p n c s", n=3)
            link(V_.tensor_tensor(comb, branches[:, 0], branches[:, 2], ALU.add))
            branch_dve(k, dve, 1)
            for dp in range(4):
                k.evacuated(dve, ("branch", 1, dp))
                c2 = slice(2 * dp, 2 * dp + 2)
                V_.tensor_tensor(comb[:, c2, :], comb[:, c2, :], branches[:, 1, c2, :], ALU.add).then_inc(k.sem("comb_sum"), 1)
            for dp in range(4):
                dve.wait_ge(k.sem("comb_hi"), dp + 1)
                hi, lo = (v[:, 2 * dp:2 * dp + 2, :] for v in k.hT2)
                V_.tensor_tensor(lo, comb[:, 2 * dp:2 * dp + 2, :], hi, ALU.subtract).then_inc(k.sem("comb_ready"), 1)
            for v in range(2):
                for t in range(NT):
                    b, free = k.filled(dve, ("wout", t, v))
                    x = k.x[:, t, v * 512:(v + 1) * 512]
                    V_.tensor_tensor(x, b[:, :], x, ALU.add).then_inc(free, 1)
            norm2_dve(k, dve, link, 2, k.lv("g_ffb"), 6)
            ffn_dve(k, dve, 1)

        @block.gpsimd
        def _(pool):
            for i in range(len(HALVES)):
                lo_pool(k, pool, i)
    k.end_phase()


def build(nc, dram, last="all"):
    with ExitStack() as ctx:
        k = Core(nc, ctx)
        with ExitStack() as memory:
            k.first_memory(memory)
            phase_first(k, dram)
            if last != "first":
                phase_moe(k, dram)
            if last not in ("first", "moe"):
                phase_ple(k, dram)
        if last not in ("first", "moe", "ple"):
            with ExitStack() as memory:
                k.layer_memory(memory)
                with nc.Fori(0, LAYERS if last == "all" else 1) as layer:
                    layer_body(k, dram, layer)
        with nc.Block() as block:
            @block.sync
            def _(sp):
                sp.dma_start(dram["out"].rearrange("o (t p) d -> p (o t) d", p=P), k.x[:, :, :]).then_inc(k.stored, 16)
                sp.wait_ge(k.stored, 16)



def bucket(dist):
    n = np.maximum(dist, 1).astype(np.float32)
    large = 16 + (np.log(n / np.float32(16)) / np.float32(np.log(2048 / 16)) * np.float32(16)).astype(np.int32)
    return np.where(dist < 16, dist, np.minimum(large, 31))


def constants():
    p, n = np.arange(P)[:, None], np.arange(P)[None, :]
    c = {"ident": p == n, "flip": p + n == P - 1, "ones": np.ones((P, P)), "tri": n >= p, "tri_strict": n > p,
         "after_mask": np.where(n >= p, 0.0, NEG), "iota": n + 0 * p, "slot": n % SL + 0 * p,
         "causal": np.where(np.arange(2 * P)[None, :] <= p + P, 0.0, NEG)}
    levels = []
    for lev in range(LEVELS):
        b = 1 << lev
        levels.append((n // (2 * b) == p // (2 * b)) & (n % (2 * b) >= b) & (p % (2 * b) < b))
    c["levels"] = np.concatenate(levels, axis=1)
    for half in (16, 32):
        freq = np.float32(10000.0) ** (-np.arange(half, dtype=np.float32) * np.float32(2.0) / np.float32(2 * half))
        ang = np.arange(S, dtype=np.float32)[:, None] * freq[None, :].astype(np.float32)
        for name, f in (("cos", np.cos), ("sin", np.sin)):
            c[f"{name}{half}"] = f(ang.astype(np.float64)).reshape(NT, P, half).transpose(1, 0, 2).reshape(P, NT * half)
    const = np.zeros((P, CONST["all"][1]), np.float32)
    for name, a in c.items():
        const[:, CONST[name][0]:CONST[name][1]] = a
    t = np.arange(S)
    pool = np.zeros((4, S, S), np.float32)
    for g, w in enumerate((2, 4, 8, 16)):
        d = t[None, :] - t[:, None]
        pool[g] = ((d >= 0) & (d < w)) / np.minimum(t + 1, w)[None, :] - (d == 0)
    poolmat = pool.reshape(4, NT, P, S).transpose(2, 0, 1, 3).reshape(P, POOL_WORDS)
    d = 2 * P - 1 - np.arange(DIST)
    dd = np.maximum(d, 0)
    onehot = (np.arange(32)[:, None] == bucket(dd)[None, :]).astype(np.float32)
    n_in = (dd <= 128).astype(int) + (dd % 4 == 0) + (dd % 16 == 0)
    lnc = np.where((d >= 0) & (n_in > 0), np.log(np.maximum(n_in, 1)), NEG).astype(np.float32)
    return const, np.ascontiguousarray(poolmat), onehot, np.ascontiguousarray(np.broadcast_to(lnc, (H, DIST)))



def chunked(w):
    kk, n = w.shape
    return np.ascontiguousarray(w.reshape(kk // P, P, n).transpose(1, 0, 2)).reshape(P, -1)


def stack_units(parts):
    out = np.zeros((len(parts), P, UNIT), np.float32)
    for i, a in enumerate(parts):
        out[i, :, :a.shape[1]] = a
    return out


def ffn_parts(w_in, w_out):
    a = w_in.reshape(KC, P, 2, FFN_IN_UNITS, 2 * P).transpose(3, 1, 0, 2, 4).reshape(FFN_IN_UNITS, P, UNIT)
    return list(a), [chunked(w_out[512 * u:512 * (u + 1)]) for u in range(FFN_OUT_UNITS)]


def layer_parts(i, l):
    w = i["w_in_2"][l]
    parts = {("mla", 0): chunked(np.concatenate([w[:, 0:416], w[:, 1952:1960]], axis=1)),
             ("up_proj", 0): np.concatenate([chunked(i["mla_w_uq_2"][l]), i["mla_w_ukv_2"][l]], axis=1),
             ("z", 0): chunked(w[:, 1960:2472])}
    for n in range(3):
        parts["moba", n] = chunked(w[:, 2472 + 512 * n:2984 + 512 * n])
        parts["gdn", n] = chunked(w[:, 416 + 512 * n:928 + 512 * n])
        parts["branch", n] = chunked(i["w_branch_2"][l, n])
    for g in range(6):
        parts["gates", g] = chunked(w[:, 4008 + 512 * g:4520 + 512 * g])
    for v in range(2):
        parts["wout", v] = chunked(i["w_out_2"][l][:, 512 * v:512 * (v + 1)])
    for n, name in enumerate(("ffa", "ffb")):
        both = ffn_parts(i[f"{name}_w_in_2"][l], i[f"{name}_w_out_2"][l])
        for kind, units in zip(("in", "out"), both):
            for u, a in enumerate(units):
                parts[f"ffn{n}", kind, u] = a
    return [parts[x] for x in STEPS]


def by_partition(v):
    return v.reshape(-1, P).T


def rows_of(v):
    return np.broadcast_to(v.reshape(1, -1), (P, v.size))


def vector_table(table, parts):
    out = np.zeros((P, table["all"][1]), np.float32)
    for name, a in parts.items():
        out[:, table[name][0]:table[name][1]] = a
    return out


def layout(i):
    const, poolmat, onehot, lnc = constants()
    w = i["w_in"][0]
    first = [chunked(w[:, c:c + 512]) for c in (512, 1024, 1536, 0)]
    first += [chunked(i["w_out"][0][:, 512 * v:512 * (v + 1)]) for v in range(2)]
    gate_up = i["w_gate_up"][0].reshape(E, 2, 4, P, 2, 2, 512).transpose(0, 5, 1, 3, 2, 4, 6).reshape(E, 4, P, UNIT)
    down = i["w_down"][0].reshape(E, 2, 4, P, D).transpose(0, 1, 3, 2, 4).reshape(E, 2, P, UNIT)
    ple = [chunked(i["w_ple_gate"][0][:, 512 * v:512 * (v + 1)]) for v in range(2)] + [chunked(i["w_ple_proj"][0])]
    fvec = vector_table(FVEC, {
        "g_mix": by_partition(i["g_mix"][0]), "g_ffn": by_partition(i["g_ffn"][0]), "g_ple": by_partition(i["g_ple"][0]),
        "pool_scale": by_partition(i["pool_scale"][0]), "b_router": rows_of(i["b_router"][0]),
        "w_router": chunked(i["w_router"][0])})
    lvec = np.stack([vector_table(LVEC, {
        "g_ffa": by_partition(i["ffa_norm_2"][l]), "g_mix": by_partition(i["mix_norm_2"][l]),
        "g_ffb": by_partition(i["ffb_norm_2"][l]),
        "conv": i["gdn_conv_2"][l].reshape(4, 12, P).transpose(2, 1, 0).reshape(P, 48),
        "c_norm": by_partition(np.concatenate([i["mla_cq_norm_2"][l], i["mla_ckv_norm_2"][l]])),
        "q_norm": rows_of(i["mla_q_norm_2"][l]), "k_norm": rows_of(i["mla_k_norm_2"][l]),
        "out_norm": rows_of(i["gdn_out_norm_2"][l]), "moba_q": rows_of(i["moba_q_norm_2"][l]),
        "moba_k": rows_of(i["moba_k_norm_2"][l]), "a_log": rows_of(i["gdn_a_log_2"][l]),
        "dt": rows_of(i["gdn_dt_bias_2"][l])}) for l in range(LAYERS)])
    return {
        "x": i["x"], "const": const, "fvec": fvec, "lvec": lvec, "onehot": onehot, "lnc": lnc, "poolmat": poolmat,
        "rel_bias": i["rel_bias"], "w_pool": i["w_pool"], "first_units": stack_units(first),
        "expert_units": np.concatenate([gate_up, down], axis=1).reshape(E * EXPERT_UNITS, P, UNIT),
        "b_gu": np.ascontiguousarray(i["b_gate_up"][0].reshape(E, 2, 2, 4, P).transpose(4, 0, 2, 3, 1)).reshape(P, E, 16), "b_down": i["b_down"],
        "ple_units": stack_units(ple), "pT": np.ascontiguousarray(i["p"][0, 0].T), "g_final": np.ascontiguousarray(rows_of(i["g_final"])),
        "layer_units": stack_units([a for l in range(LAYERS) for a in layer_parts(i, l)]),
    }


def declare(nc, arrays):
    dram = {name: nc.dram_tensor(f"in_{name}", a.shape, mybir.dt.from_np(a.dtype), kind="ExternalInput").ap()
            for name, a in arrays.items()}
    dram["rev"] = nc.dram_tensor("bias_by_distance", (H, DIST), F32, kind="Internal").ap()
    dram["out"] = nc.dram_tensor("out", (1, S, D), F32, kind="ExternalOutput").ap()
    return dram


def kernel(**inputs):
    import concourse.bacc as bacc
    from concourse.bass_utils import run_bass_kernel_spmd
    arrays = layout({name: np.asarray(a) for name, a in inputs.items()})
    nc = bacc.Bacc("TRN2", target_bir_lowering=False, num_devices=1)
    build(nc, declare(nc, arrays))
    r = run_bass_kernel_spmd(nc, [{f"in_{name}": a for name, a in arrays.items()}], core_ids=[0])
    return r.results[0]["out"]
```
